# Optimizing a Trainium2 kernel written in Bass

```python
import math
import jax
import jax.numpy as jnp
from jax import lax
import numpy as np

D_MODEL = 1024
BATCH = 1
SEQ = 256
DEPTH = 2

HEAD_DIM = 64
EPS = 1e-6
A_HEADS = 4
A_PATTERNS = ((128, 1), (512, 4), (2048, 16))
A_BLOCK = 128
ROPE_THETA = 500000.0
ROPE_DIM = HEAD_DIM // 4
R_HEADS = 4
R_QK_DIM = 64
R_V_DIM = 128
R_CHUNK = 128
R_ROPE_THETA = 10000.0
S_CHANNELS = 256
S_GROUP = 16
S_GROUPS = S_CHANNELS // S_GROUP
S_STATE = 64
A_WIDTH = A_HEADS * HEAD_DIM
R_WIDTH = R_HEADS * R_V_DIM
MIX_WIDTH = A_WIDTH + R_WIDTH + S_CHANNELS
IN_SPLITS = (A_WIDTH, A_WIDTH, A_WIDTH, R_HEADS * R_QK_DIM, R_HEADS * R_QK_DIM, R_WIDTH, R_WIDTH, S_CHANNELS)
IN_COLS = sum(IN_SPLITS)
D_FF = 2816
N_EXPERTS = 8
TOP_K = 2
D_FF_EXPERT = 3584

kernel_name = "hybrid_dilated_retention_s5_moe_block"

def rms_norm(x, g):
    xf = x.astype(jnp.float32)
    y = xf * lax.rsqrt(jnp.mean(xf * xf, axis=-1, keepdims=True) + EPS)
    return (y * g.astype(jnp.float32)).astype(x.dtype)

def rotary(x, pos, rot_dim, theta):
    half = rot_dim // 2
    inv = jnp.power(theta, -jnp.arange(half, dtype=jnp.float32) * 2.0 / rot_dim)
    ang = pos.astype(jnp.float32)[:, None] * inv[None, :]
    cos = jnp.cos(ang)[:, None, :]
    sin = jnp.sin(ang)[:, None, :]
    xr = x[..., :rot_dim].astype(jnp.float32)
    x1, x2 = xr[..., :half], xr[..., half:]
    rot = jnp.concatenate([x1 * cos - x2 * sin, x2 * cos + x1 * sin], axis=-1).astype(x.dtype)
    return jnp.concatenate([rot, x[..., rot_dim:]], axis=-1)

def dilated_window_attention(q, k, v, dilation):
    b, h, s, hd = q.shape
    span = A_BLOCK * dilation
    s_pad = -(-s // span) * span
    lr = s_pad // dilation
    nb = lr // A_BLOCK

    def to_blocks(t):
        t = jnp.pad(t, ((0, 0), (0, 0), (0, s_pad - s), (0, 0)))
        t = t.reshape(b, h, lr, dilation, hd).transpose(0, 1, 3, 2, 4)
        return t.reshape(b, h, dilation, nb, A_BLOCK, hd)

    def with_prev(t):
        prev = jnp.pad(t, ((0, 0), (0, 0), (0, 0), (1, 0), (0, 0), (0, 0)))[:, :, :, :-1]
        return jnp.concatenate([prev, t], axis=4)

    qb = to_blocks(q)
    kk = with_prev(to_blocks(k))
    vv = with_prev(to_blocks(v))
    scores = jnp.einsum('bhrnid,bhrnjd->bhrnij', qb, kk) * (hd ** -0.5)
    i = jnp.arange(A_BLOCK)[:, None]
    j = jnp.arange(2 * A_BLOCK)[None, :]
    steps = A_BLOCK + i - j
    band = (steps >= 0) & (steps <= A_BLOCK)
    blk = jnp.arange(nb)[:, None, None]
    mask = band[None] & ((blk > 0) | (j >= A_BLOCK)[None])
    scores = jnp.where(mask, scores, -jnp.inf)
    m = jnp.max(scores, axis=-1, keepdims=True)
    p = jnp.exp(scores - m)
    l = jnp.sum(p, axis=-1, keepdims=True)
    o = jnp.einsum('bhrnij,bhrnjd->bhrnid', p / l, vv)
    lse = (m + jnp.log(l))[..., 0]

    def from_blocks(t):
        t = t.reshape(b, h, dilation, lr, *t.shape[5:])
        t = jnp.moveaxis(t, 2, 3)
        return t.reshape(b, h, s_pad, *t.shape[4:])[:, :, :s]

    return from_blocks(o), from_blocks(lse)

def mixer_dilated(q, k, v, q_g, k_g, pos):
    b, s, _ = q.shape
    shp = (b, s, A_HEADS, HEAD_DIM)
    q = rotary(rms_norm(q.reshape(shp), q_g), pos, ROPE_DIM, ROPE_THETA)
    k = rotary(rms_norm(k.reshape(shp), k_g), pos, ROPE_DIM, ROPE_THETA)
    v = v.reshape(shp)
    qh, kh, vh = [t.astype(jnp.float32).transpose(0, 2, 1, 3) for t in (q, k, v)]
    outs, lses = [], []
    for _, dil in A_PATTERNS:
        o_p, lse_p = dilated_window_attention(qh, kh, vh, dil)
        outs.append(o_p)
        lses.append(lse_p)
    w = jax.nn.softmax(jnp.stack(lses, axis=0), axis=0)
    o = jnp.einsum('pbhs,pbhsd->bhsd', w, jnp.stack(outs, axis=0))
    return o.transpose(0, 2, 1, 3).reshape(b, s, A_WIDTH).astype(q.dtype)

def mixer_retention(q, k, v, g, gn_g, pos):
    f32 = jnp.float32
    b, s, _ = q.shape
    dtype = q.dtype
    q = rotary(q.reshape(b, s, R_HEADS, R_QK_DIM), pos, R_QK_DIM, R_ROPE_THETA).astype(f32)
    k = (rotary(k.reshape(b, s, R_HEADS, R_QK_DIM), pos, R_QK_DIM, R_ROPE_THETA).astype(f32) * (R_QK_DIM ** -0.5))
    v = v.astype(f32).reshape(b, s, R_HEADS, R_V_DIM)
    log_gamma = jnp.log1p(-jnp.exp2(-5.0 - jnp.arange(R_HEADS, dtype=f32)))
    n = s // R_CHUNK
    qc = q.reshape(b, n, R_CHUNK, R_HEADS, R_QK_DIM)
    kc = k.reshape(b, n, R_CHUNK, R_HEADS, R_QK_DIM)
    vc = v.reshape(b, n, R_CHUNK, R_HEADS, R_V_DIM)
    idx = jnp.arange(R_CHUNK, dtype=f32)
    diff = idx[:, None] - idx[None, :]
    decay = jnp.where(diff >= 0, jnp.exp(log_gamma[:, None, None] * jnp.maximum(diff, 0.0)), 0.0)
    inner = jnp.einsum('bnihd,bnjhd->bnhij', qc, kc) * decay
    inner = jnp.einsum('bnhij,bnjhe->bnihe', inner, vc)
    zeta = jnp.exp(log_gamma[:, None] * (R_CHUNK - 1.0 - idx))
    xi = jnp.exp(log_gamma[:, None] * (idx + 1.0))
    kv = jnp.einsum('bnjhd,bnjhe,hj->nbhde', kc, vc, zeta)
    chunk_decay = jnp.exp(log_gamma * R_CHUNK)[None, :, None, None]

    def step(state, kv_n):
        return chunk_decay * state + kv_n, state

    _, prev = lax.scan(step, jnp.zeros((b, R_HEADS, R_QK_DIM, R_V_DIM), f32), kv)
    cross = jnp.einsum('bnihd,nbhde,hi->bnihe', qc, prev, xi)
    y = (inner + cross).reshape(b, s, R_HEADS, R_V_DIM)
    mu = jnp.mean(y, axis=-1, keepdims=True)
    var = jnp.mean(jnp.square(y - mu), axis=-1, keepdims=True)
    y = ((y - mu) * lax.rsqrt(var + 1e-5)).reshape(b, s, R_WIDTH) * gn_g.astype(f32)
    return (jax.nn.silu(g.astype(f32)) * y).astype(dtype)

def mixer_ssm(u, a_re, a_im, b_re, b_im, c_re, c_im, d_skip, log_dt, glu_w, glu_b):
    f32 = jnp.float32
    bsz, s, _ = u.shape
    uf = u.astype(f32).reshape(bsz, s, S_GROUPS, S_GROUP)
    dt = jnp.exp(log_dt.astype(f32))[:, None]
    lam_re = a_re.astype(f32)
    lam_im = a_im.astype(f32)
    mag = jnp.exp(lam_re * dt)
    abar_re = mag * jnp.cos(lam_im * dt)
    abar_im = mag * jnp.sin(lam_im * dt)
    den = lam_re * lam_re + lam_im * lam_im
    nr = abar_re - 1.0
    ni = abar_im
    f_re = ((nr * lam_re + ni * lam_im) / den)[..., None]
    f_im = ((ni * lam_re - nr * lam_im) / den)[..., None]
    br = b_re.astype(f32)
    bi = b_im.astype(f32)
    bb_re = f_re * br - f_im * bi
    bb_im = f_re * bi + f_im * br
    x_re = jnp.einsum('bsgc,gpc->bsgp', uf, bb_re)
    x_im = jnp.einsum('bsgc,gpc->bsgp', uf, bb_im)
    shp = (bsz, s, S_GROUPS, S_STATE)
    at_re = jnp.broadcast_to(abar_re, shp)
    at_im = jnp.broadcast_to(abar_im, shp)

    def combine(e1, e2):
        a1r, a1i, b1r, b1i = e1
        a2r, a2i, b2r, b2i = e2
        return (a2r * a1r - a2i * a1i,
                a2r * a1i + a2i * a1r,
                a2r * b1r - a2i * b1i + b2r,
                a2r * b1i + a2i * b1r + b2i)

    _, _, h_re, h_im = lax.associative_scan(combine, (at_re, at_im, x_re, x_im), axis=1)
    y = (jnp.einsum('gcp,bsgp->bsgc', c_re.astype(f32), h_re)
         - jnp.einsum('gcp,bsgp->bsgc', c_im.astype(f32), h_im)
         + d_skip.astype(f32).reshape(S_GROUPS, S_GROUP) * uf)
    z = jax.nn.gelu(y.reshape(bsz, s, S_CHANNELS))
    out = z * jax.nn.sigmoid(z @ glu_w.astype(f32) + glu_b.astype(f32))
    return out.astype(u.dtype)

def swiglu(x, w_gate, w_up, w_down):
    return (jax.nn.silu(x @ w_gate) * (x @ w_up)) @ w_down

def moe_swiglu(x, router, w_gate, w_up, w_down):
    b, s, d = x.shape
    t = x.reshape(b * s, d)
    probs = jax.nn.softmax((t @ router).astype(jnp.float32), axis=-1)
    top_p, top_i = lax.top_k(probs, TOP_K)
    top_p = top_p / jnp.sum(top_p, axis=-1, keepdims=True)
    gates = jnp.sum(jax.nn.one_hot(top_i, N_EXPERTS, dtype=jnp.float32) * top_p[..., None], axis=1)
    out = jnp.zeros((b * s, d), jnp.float32)
    for e in range(N_EXPERTS):
        out = out + gates[:, e:e + 1] * swiglu(t, w_gate[e], w_up[e], w_down[e]).astype(jnp.float32)
    return out.astype(x.dtype).reshape(b, s, d)

def setup_inputs(seed: int = 0) -> dict:
    key = jax.random.key(seed)
    ks = iter(jax.random.split(key, 32))
    f32 = jnp.float32
    L = DEPTH
    NE = (DEPTH + 1) // 2
    NO = DEPTH // 2
    G, P = S_GROUPS, S_STATE

    def nrm(shape, scale):
        return jax.random.normal(next(ks), shape, f32) * scale

    return {
        "x": nrm((BATCH, SEQ, D_MODEL), 1.0),
        "norm1_g": 1.0 + nrm((L, D_MODEL), 0.02),
        "w_in": nrm((L, D_MODEL, IN_COLS), D_MODEL ** -0.5),
        "q_norm_g": 1.0 + nrm((L, HEAD_DIM), 0.02),
        "k_norm_g": 1.0 + nrm((L, HEAD_DIM), 0.02),
        "ret_gn_g": 1.0 + nrm((L, R_WIDTH), 0.02),
        "ssm_a_re": -0.5 + nrm((L, G, P), 0.01),
        "ssm_a_im": jnp.pi * jnp.arange(P, dtype=f32)[None, None, :] + nrm((L, G, P), 0.01),
        "ssm_b_re": nrm((L, G, P, S_GROUP), (2 * S_GROUP) ** -0.5),
        "ssm_b_im": nrm((L, G, P, S_GROUP), (2 * S_GROUP) ** -0.5),
        "ssm_c_re": nrm((L, G, S_GROUP, P), 0.5),
        "ssm_c_im": nrm((L, G, S_GROUP, P), 0.5),
        "ssm_d": nrm((L, S_CHANNELS), 0.5),
        "ssm_log_dt": jax.random.uniform(next(ks), (L, G), f32, math.log(1e-3), math.log(1e-1)),
        "ssm_glu_w": nrm((L, S_CHANNELS, S_CHANNELS), S_CHANNELS ** -0.5),
        "ssm_glu_b": nrm((L, S_CHANNELS), 0.01),
        "w_out": nrm((L, MIX_WIDTH, D_MODEL), MIX_WIDTH ** -0.5),
        "norm2_g": 1.0 + nrm((L, D_MODEL), 0.02),
        "ffn_w_gate": nrm((NE, D_MODEL, D_FF), D_MODEL ** -0.5),
        "ffn_w_up": nrm((NE, D_MODEL, D_FF), D_MODEL ** -0.5),
        "ffn_w_down": nrm((NE, D_FF, D_MODEL), D_FF ** -0.5),
        "moe_router": nrm((NO, D_MODEL, N_EXPERTS), D_MODEL ** -0.5),
        "moe_w_gate": nrm((NO, N_EXPERTS, D_MODEL, D_FF_EXPERT), D_MODEL ** -0.5),
        "moe_w_up": nrm((NO, N_EXPERTS, D_MODEL, D_FF_EXPERT), D_MODEL ** -0.5),
        "moe_w_down": nrm((NO, N_EXPERTS, D_FF_EXPERT, D_MODEL), D_FF_EXPERT ** -0.5),
    }

def reference(x, norm1_g, w_in, q_norm_g, k_norm_g, ret_gn_g, ssm_a_re, ssm_a_im, ssm_b_re, ssm_b_im,
              ssm_c_re, ssm_c_im, ssm_d, ssm_log_dt, ssm_glu_w, ssm_glu_b, w_out, norm2_g,
              ffn_w_gate, ffn_w_up, ffn_w_down, moe_router, moe_w_gate, moe_w_up, moe_w_down):
    s = x.shape[1]
    pos = jnp.arange(s, dtype=jnp.int32)
    cuts = list(np.cumsum(IN_SPLITS)[:-1])
    h = x
    for layer in range(DEPTH):
        xn = rms_norm(h, norm1_g[layer])
        proj = xn @ w_in[layer]
        qa, ka, va, qr, kr, vr, gr, us = jnp.split(proj, cuts, axis=-1)
        ya = mixer_dilated(qa, ka, va, q_norm_g[layer], k_norm_g[layer], pos)
        yr = mixer_retention(qr, kr, vr, gr, ret_gn_g[layer], pos)
        yc = mixer_ssm(us, ssm_a_re[layer], ssm_a_im[layer], ssm_b_re[layer], ssm_b_im[layer],
                       ssm_c_re[layer], ssm_c_im[layer], ssm_d[layer], ssm_log_dt[layer],
                       ssm_glu_w[layer], ssm_glu_b[layer])
        mixed = jnp.concatenate([ya, yr, yc], axis=-1)
        h = h + mixed @ w_out[layer]
        xn2 = rms_norm(h, norm2_g[layer])
        if layer % 2 == 0:
            i = layer // 2
            h = h + swiglu(xn2, ffn_w_gate[i], ffn_w_up[i], ffn_w_down[i])
        else:
            i = layer // 2
            h = h + moe_swiglu(xn2, moe_router[i], moe_w_gate[i], moe_w_up[i], moe_w_down[i])
    return h


_drawn_inputs = setup_inputs


def setup_inputs(seed=0):
    import zlib

    import numpy as np

    out = dict(_drawn_inputs(seed))
    spreads = {}
    factors = {'q_norm_g': 8.0, 'k_norm_g': 8.0, 'ssm_a_re': 39.228, 'ssm_glu_b': 22.123}
    for name, (base, spread) in spreads.items():
        noise = np.random.default_rng([zlib.crc32(name.encode()), seed]).standard_normal(out[name].shape)
        drawn = base * np.exp(spread * noise) if base else spread * noise
        out[name] = jnp.asarray(drawn.astype(out[name].dtype))
    for name, factor in factors.items():
        out[name] = (out[name] * factor).astype(out[name].dtype)
    return out
```

```python
from contextlib import ExitStack

import numpy as np

import concourse.bass as bass
from concourse import mybir

F32 = mybir.dt.float32
I32 = mybir.dt.int32
ALU = mybir.AluOpType
ACT = mybir.ActivationFunctionType
AX_X = mybir.AxisListType.X

P = 128
SEQ, D = 256, 1024
NT = SEQ // P
KC = D // P
HD = 64
HEADS = 4
RV = 128
GROUPS, GC, STATES = 16, 16, 64
CH = 8
NCH = SEQ // CH
EPS = 1e-6
BLK = 512
PROJ = 2304
NE = 8
QC, VC, QR, KR, VR, GR = 0, 512, 768, 1024, 1280, 1792

CO = {}
_at = 0
for _name, _n in (("ident", 128), ("swap", 128), ("tri", 128), ("ones", 128), ("iota", 128),
                  ("cosA", 16), ("sinA", 16), ("cosR", 64), ("sinR", 64), ("count", 384), ("mask", 384),
                  ("decay", 4 * 384), ("sg", 2), ("rev", 8), ("mhalf", 16), ("mone", 16), ("euler", 16)):
    CO[_name] = (_at, _n)
    _at += _n
NCONST = _at
PO = {}
_at = 0
for _name, _n in (("g1", 8), ("g2", 8), ("gn", 4), ("glub", 2), ("qkg", 128), ("are", 16), ("aim", 16),
                  ("logdt", 16), ("b1", 256), ("b2", 256), ("c1", 256), ("c2", 256), ("gluw", 512),
                  ("dskip", 256)):
    PO[_name] = (_at, _n)
    _at += _n
NPAR = _at


def constants():
    f = np.float32
    c = np.zeros((P, NCONST), f)

    def put(name, a):
        o, n = CO[name]
        c[:, o:o + n] = np.asarray(a, f).reshape(P, n)

    p = np.arange(P)
    put("ident", np.eye(P))
    put("swap", np.eye(P)[(p + 64) % P])
    put("tri", p[:, None] < p[None, :])
    put("ones", np.ones((P, P)))
    put("iota", np.tile(p, (P, 1)))
    pos = np.arange(SEQ, dtype=f)
    for nm, theta, rot in (("A", 500000.0, 16), ("R", 10000.0, 64)):
        half = rot // 2
        inv = np.power(f(theta), -np.arange(half, dtype=f) * f(2.0) / f(rot)).astype(f)
        ang = (pos[:, None] * inv[None, :]).astype(f)
        put("cos" + nm, np.cos(ang).reshape(NT, P, half).transpose(1, 0, 2))
        put("sin" + nm, np.sin(ang).reshape(NT, P, half).transpose(1, 0, 2))
    i, j = np.arange(SEQ)[:, None], np.arange(SEQ)[None, :]
    d = i - j
    cnt = sum(((d >= 0) & (d <= 128 * r) & (d % r == 0)).astype(f) for r in (1, 4, 16))
    msk = np.where(cnt > 0, 0.0, -1e30).astype(f)
    for nm, a in (("count", cnt), ("mask", msk)):
        put(nm, np.concatenate([a[0:P, 0:P], a[P:, :]], 1))
    lg = np.log1p(-np.exp2(-5.0 - np.arange(HEADS)))
    dec = np.where(d >= 0, np.exp(lg[:, None, None] * np.maximum(d, 0)), 0.0) * HD ** -0.5
    dT = dec.transpose(0, 2, 1)
    put("decay", np.stack([np.concatenate([dT[h, 0:P, :], dT[h, P:, P:]], 1) for h in range(HEADS)], 1))
    put("sg", np.stack([np.where(p < 64, -1, 1), np.where(p < 64, 1, -1)], 1))
    put("rev", np.tile(np.arange(NE, 0, -1), (P, 1)))
    put("mhalf", np.full((P, 16), -0.5))
    put("mone", np.full((P, 16), -1.0))
    put("euler", np.full((P, 16), np.e))
    return c


def ring_order():
    def mixer(l):
        return ([("in", l, b, kh) for b in (4, 0, 1, 2, 3) for kh in range(2)]
                + [("out", l, n, kh) for kh in range(2) for n in range(2)])
    return mixer(0), mixer(1)


def trunk(nc, a, out):
    x, w_in, w_out = a["x"], a["w_in"], a["w_out"]
    w_gate, w_up, w_down = a["ffn_w_gate"], a["ffn_w_up"], a["ffn_w_down"]
    m_gate, m_up, m_down = a["moe_w_gate"], a["moe_w_up"], a["moe_w_down"]
    FU = w_gate.shape[2] // 256
    MU = m_gate.shape[3] // BLK
    assert FU % 2 == 1 and MU % 2 == 1 and FU >= 3 and MU >= 5
    PAIRS = (FU - 1) // 2
    ET = 6 * MU
    RA, RM = 6, 14
    assert ET % RM == 0
    ER = ET // RM
    MIX = 14
    FFN_TILES = 3 * FU
    BASE = [0, MIX + FFN_TILES]

    gu_at = lambda u: MIX + 2 if u == 0 else MIX + 3 * u + 1
    d_at = lambda u: MIX + 3 * u + (5 if u < FU - 1 else 3)
    mgu_at = lambda u: 4 if u == 0 else 6 * u + 2
    md_at = lambda u: 6 * u + (10 if u < MU - 1 else 6)

    with ExitStack() as ctx:
        def sem(name):
            return ctx.enter_context(nc.semaphore(name))

        psum = ctx.enter_context(nc.psum_tensor("psum", [P, 8, BLK], F32))
        PB = [psum[:, b, :] for b in range(8)]
        top = [0]
        ARENA = 52800
        arena = ctx.enter_context(nc.sbuf_tensor("arena", [P, ARENA], F32))
        flag = ctx.enter_context(nc.sbuf_tensor("flag", [P, 2], I32))
        scr_u = nc.dram_tensor("scratch_u", [256, 256], F32, kind="Internal").ap()
        scr_y = nc.dram_tensor("scratch_y", [256, 256], F32, kind="Internal").ap()

        def take(*shape, at=None):
            n = int(np.prod(shape))
            o = top[0] if at is None else at
            if at is None:
                top[0] += n
            assert o + n <= ARENA, (o + n, ARENA)
            v = arena[:, o:o + n]
            names = "abcd"[:len(shape)]
            if len(shape) > 1:
                v = v.rearrange(f"p ({' '.join(names)}) -> p {' '.join(names)}",
                                **{k: s for k, s in zip(names, shape)})
            return v

        h = take(NT, D)
        cst = take(NCONST)
        par = take(2, NPAR)
        router = take(KC, NE)
        xs = take(NT, D)
        xnT = take(KC, SEQ)
        st = take(256)
        ringA_at = top[0]
        ringA = [take(2048) for _ in range(RA)]
        mix_at = top[0]
        proj = take(NT, PROJ)
        qk_at = top[0]
        qkT = take(8, SEQ)
        take(256)
        vt = take(GROUPS, CH + 1, GC, at=qk_at)
        wt = take(GROUPS, CH, GC, at=qk_at)
        E_at = top[0]
        E = take(HEADS, 384)
        PT = take(HEADS, 384)
        AT = take(HEADS, 384)
        Wpre = take(GROUPS, CH, GC, at=E_at)
        Kall = take(GROUPS, CH, GC, at=E_at + 2048)
        uTr = take(2, CH, NCH)
        U = take(GROUPS, NCH)
        xsb = take(GROUPS, NCH)
        t1 = take(GROUPS, NCH)
        t2 = take(GROUPS, NCH)
        G = take(GROUPS, NCH)
        Hs = take(GROUPS, NCH + 1)
        zT = take(2, CH, NCH)
        sgm = take(2, CH, NCH)
        cosT = take(GROUPS, NCH)
        sinT = take(GROUPS, NCH)
        mg = take(GROUPS, NCH)
        Mt = take(GROUPS, CH, GC)
        Wl = take(GROUPS, P)
        V = take(GROUPS, CH + 1, GC)
        Tre = take(32, CH + 1)
        Tim = take(32, CH + 1)
        ptmp = take(4, 256)
        pv = take(24, GROUPS)
        prs = take(GROUPS, CH + 1)
        tims = take(GROUPS, CH)
        Bb1 = take(GROUPS, GC)
        Bb2 = take(GROUPS, GC)
        rtA = xs[:, 1, 512:1024].rearrange("p (a b) -> p a b", a=4)
        fsil = [take(BLK, at=mix_at + 512 * i) for i in range(2)]
        fhT = [take(2, SEQ, at=mix_at + 1024 + 512 * i) for i in range(2)]
        moe_at = mix_at + (RM - RA) * 2048
        ringM = ringA + [take(2048, at=mix_at + 2048 * i) for i in range(RM - RA)]
        top[0] = moe_at
        xgT = take(KC, P)
        PH = take(NT, NE + 1, P)
        PG_at = top[0]
        PG = take(NT, NE, P)
        PTg = take(NE, SEQ)
        PTcur = take(SEQ)
        msil = [take(BLK, at=PG_at + BLK * i) for i in range(2)]
        mh = take(2, BLK, at=PG_at + 2 * BLK)
        mhT = take(2, 4, P)
        yb = take(D)
        rt = take(320)
        assert top[0] <= ARENA, top[0]

        def C(name, *shape):
            o, n = CO[name]
            v = cst[:, o:o + n]
            if len(shape) > 1:
                names = "abcd"[:len(shape)]
                v = v.rearrange(f"p ({' '.join(names)}) -> p {' '.join(names)}",
                                **{k: s for k, s in zip(names, shape)})
            return v

        def R(l, name, *shape):
            o, n = PO[name]
            v = par[:, l, o:o + n]
            if len(shape) > 1:
                names = "abcd"[:len(shape)]
                v = v.rearrange(f"p ({' '.join(names)}) -> p {' '.join(names)}",
                                **{k: s for k, s in zip(names, shape)})
            return v

        ident = C("ident")

        x_in, cst_in, par_in, router_in = sem("x_in"), sem("cst_in"), sem("par_in"), sem("router_in")
        tile_in = [sem(f"tile_in{s}") for s in range(RA)]
        tile_used = sem("tile_used")
        mtile_in = [sem(f"mtile_in{s}") for s in range(RM)]
        mtile_used = sem("mtile_used")
        ss_ready, rstd_ready, xs_ready = sem("ss_ready"), sem("rstd_ready"), sem("xs_ready")
        nT_ps, xnT_ready = sem("nT_ps"), sem("xnT_ready")
        proj_ready, u_ready = sem("proj_ready"), sem("u_ready")
        u_out, u_in = sem("u_out"), sem("u_in")
        sincos_arg, trig_ready, poles_ready, prep_ready = (
            sem("sincos_arg"), sem("trig_ready"), sem("poles_ready"), sem("prep_ready"))
        prepT_ps, prepT_ev, K_raw, K_ready, toep_in = (
            sem("prepT_ps"), sem("prepT_ev"), sem("K_raw"), sem("K_ready"), sem("toep_in"))
        x_ps, x_sb, scan_ready, hs_ready, y_ps = (
            sem("x_ps"), sem("x_sb"), sem("scan_ready"), sem("hs_ready"), sem("y_ps"))
        perm_ps, gelu_ready, y_out, z_in = sem("perm_ps"), sem("gelu_ready"), sem("y_out"), sem("z_in")
        glu_ps, sgm_ready, mixS_ready = sem("glu_ps"), sem("sgm_ready"), sem("mixS_ready")
        sq_ready, ssq_ready, rq_ready = sem("sq_ready"), sem("ssq_ready"), sem("rq_ready")
        qk_ready, qr_ready, qkT_ps, qkT_ready = sem("qk_ready"), sem("qr_ready"), sem("qkT_ps"), sem("qkT_ready")
        s_ps, s_masked, negm_ready, exp_ready, p_ready = (
            sem("s_ps"), sem("s_masked"), sem("negm_ready"), sem("exp_ready"), sem("p_ready"))
        pT_ps, PT_ready, att_ps = sem("pT_ps"), sem("PT_ready"), sem("att_ps")
        rs_ps, AT_ready, ry_ps = sem("rs_ps"), sem("AT_ready"), sem("ry_ps")
        var_ready, rvar_ready, mixed_ready = sem("var_ready"), sem("rvar_ready"), sem("mixed_ready")
        mT_ps, mixT_ready, h1_ready = sem("mT_ps"), sem("mixT_ready"), sem("h1_ready")
        sil_ready, hT_ready, h2_ready = sem("sil_ready"), sem("hT_ready"), sem("h2_ready")
        lg_ps, lgm_ready, lge_ready, mask_ready, pos_ps, hot_ready, flag_ready = (
            sem("lg_ps"), sem("lgm_ready"), sem("lge_ready"), sem("mask_ready"), sem("pos_ps"),
            sem("hot_ready"), sem("flag_ready"))
        gT_ps, PTg_ready, first_y = sem("gT_ps"), sem("PTg_ready"), sem("first_y")
        xg_ps, xgA_ready, xgD_ready = sem("xg_ps"), sem("xgA_ready"), sem("xgD_ready")
        msil_ready, mh_ready, mhT_ps, mhT_ready = (
            sem("msil_ready"), sem("mh_ready"), sem("mhT_ps"), sem("mhT_ready"))
        yA_ready, yD_ready, sc_ps, sc_done, out_ready, out_done = (
            sem("yA_ready"), sem("yD_ready"), sem("sc_ps"), sem("sc_done"), sem("out_ready"), sem("out_done"))
        dve_step, act_step, pool_step, pool_z = sem("dve_step"), sem("act_step"), sem("pool_step"), sem("pool_z")

        block = ctx.enter_context(nc.Block())

        class Steps:

            def __init__(self, eng, s):
                self.eng, self.s, self.n = eng, s, 0

            def add(self, ins):
                ins.then_inc(self.s, 1)
                self.n += 1

            def wait(self):
                self.eng.wait_ge(self.s, self.n)

            def link(self, ins):
                self.add(ins)
                self.wait()

        @block.sync
        def _(sp):
            sp.dma_start(h[:, :, :], x[0].rearrange("(t p) d -> p t d", p=P)).then_inc(x_in, 16)
            sp.dma_start(cst, a["consts"]).then_inc(cst_in, 16)
            sp.dma_start(par[:, :, :], a["params"]).then_inc(par_in, 16)
            sp.dma_start(router, a["router"]).then_inc(router_in, 16)

            def tile(k, dst_shape, src):
                if k >= RA:
                    sp.wait_ge(tile_used, k - RA + 1)
                v = ringA[k % RA].rearrange("p (c n) -> p c n", c=dst_shape)
                sp.dma_start(v, src).then_inc(tile_in[k % RA], 16)

            def rows(w, r0, nchunk, c0, nc_):
                return w[r0 * P:(r0 + nchunk) * P, c0:c0 + nc_].rearrange("(c p) n -> p c n", p=P)

            def mixer_tiles(l):
                for k, (kind, _, b, kh) in enumerate(ring_order()[l]):
                    w = w_in if kind == "in" else w_out
                    tile(BASE[l] + k, 4, rows(w[l], 4 * kh, 4, b * BLK, BLK))

            def ffn_unit(k, u, ud):
                yield k, KC, w_gate, u
                yield k + 1, KC, w_up, u
                yield k + 2, 2, w_down, ud

            mixer_tiles(0)
            k0 = MIX
            tile(k0, KC, rows(w_gate[0], 0, KC, 0, 256))
            tile(k0 + 1, KC, rows(w_up[0], 0, KC, 0, 256))
            with sp.Fori(0, PAIRS) as i:
                for j in range(2):
                    for m, w in ((0, w_gate), (1, w_up), (2, w_down)):
                        kk = k0 + 2 + 3 * j + m
                        sp.wait_ge(tile_used, i * 6 + (kk - RA + 1))
                        v = ringA[kk % RA].rearrange("p (c n) -> p c n", c=2 if m == 2 else KC)
                        if m == 2:
                            src = w[0].rearrange("(u c p) n -> u p c n", c=2, p=P)[i * 2 + j]
                        else:
                            src = w[0].rearrange("(c p) (u n) -> u p c n", p=P, n=256)[i * 2 + j + 1]
                        sp.dma_start(v, src).then_inc(tile_in[kk % RA], 16)
            tile(k0 + FFN_TILES - 1, 2, w_down[0].rearrange("(u c p) n -> u p c n", c=2, p=P)[FU - 1])
            mixer_tiles(1)

            def mtile(m, e):
                if m < 4:
                    kind, u, half = "gu"[m // 2], 0, m % 2
                elif m >= ET - 2:
                    kind, u, half = "d", MU - 1, m % 2
                else:
                    r = (m - 4) % 6
                    u = (m - 4) // 6 + 1
                    kind, half = "gud"[r // 2], r % 2
                    if kind == "d":
                        u -= 1
                if kind == "d":
                    r0 = (4 * u + 2 * half) * P
                    return 2, m_down[0].rearrange("e r n -> e r n")[e, r0:r0 + 2 * P, :].rearrange(
                        "(c p) n -> p c n", p=P)
                w = m_gate if kind == "g" else m_up
                return 4, w[0][e, half * 4 * P:(half + 1) * 4 * P, u * BLK:(u + 1) * BLK].rearrange(
                    "(c p) n -> p c n", p=P)

            def mload(m, e):
                c, src = mtile(m, e)
                sp.dma_start(ringM[m % RM].rearrange("p (c n) -> p c n", c=c), src).then_inc(mtile_in[m % RM], 16)

            def expert_pass(ps):
                used0 = ps * NE * ET
                for m in range(RM):
                    if ps == 0 and m < RA:
                        last = max(k for k in range(BASE[1] + MIX) if k % RA == m)
                        sp.wait_ge(tile_used, last + 1)
                    elif ps == 0:
                        sp.wait_ge(h1_ready, 4 * 2)
                    else:
                        sp.wait_ge(mtile_used, used0 - RM + m + 1)
                    mload(m, 0)
                with sp.Fori(0, NE - 1) as e:
                    for m in range(ET):
                        sp.wait_ge(mtile_used, e * ET + (used0 + m + 1))
                        n = m + RM
                        mload(n % ET, e + n // ET)
                for m in range(ET - RM):
                    sp.wait_ge(mtile_used, (NE - 1) * ET + used0 + m + 1)
                    mload(m + RM, NE - 1)

            expert_pass(0)
            sp.wait_ge(flag_ready, 1)
            more = sp.value_load(flag[0:1, 0:1], min_val=0, max_val=1)
            with sp.If(more > 0):
                expert_pass(1)
            sp.wait_ge(out_ready, 1)
            sp.dma_start(out[0].rearrange("(t p) d -> p t d", p=P), h[:, :, :]).then_inc(out_done, 16)
            sp.wait_ge(out_done, 16)

        def s5_setup(l, eng, lk):
            def tt(o, x0, x1, op):
                lk.add(eng.tensor_tensor(o, x0, x1, op))

            def ts(o, x0, s1, s2=None, o0=ALU.mult, o1=None):
                lk.add(eng.tensor_scalar(o, x0, s1, s2, o0, o1) if o1 is not None
                       else eng.tensor_scalar(o, x0, s1, None, o0))

            sg, sg2 = C("sg")[:, 0:1], C("sg")[:, 1:2]
            S = lambda n: pv[:, n, :]
            mag, sn, cs, rden = S(0), S(1), S(2), S(3)
            nr, f1, f2, f3, f4, fre, fim, fs, fns = (S(n) for n in range(9, 18))
            are, aim = R(l, "are"), R(l, "aim")
            b1, b2 = R(l, "b1", GROUPS, GC), R(l, "b2", GROUPS, GC)
            c1, c2 = R(l, "c1", GROUPS, GC), R(l, "c2", GROUPS, GC)

            A = Tre[:, 0:16, 1]
            tt(A, mag, cs, ALU.mult)
            tt(Tim[:, 0:16, 1], mag, sn, ALU.mult)
            lk.add(eng.tensor_copy(Tre[:, 16:32, 1], cs))
            lk.add(eng.tensor_copy(Tim[:, 16:32, 1], sn))
            lk.wait()
            ts(nr, A, -1.0, o0=ALU.add)
            lk.wait()
            tt(f1, nr, are, ALU.mult)
            tt(f2, Tim[:, 0:16, 1], aim, ALU.mult)
            tt(f3, Tim[:, 0:16, 1], are, ALU.mult)
            tt(f4, nr, aim, ALU.mult)
            lk.wait()
            tt(f1, f1, f2, ALU.add)
            tt(f3, f3, f4, ALU.subtract)
            lk.wait()
            tt(fre, f1, rden, ALU.mult)
            tt(fim, f3, rden, ALU.mult)
            lk.wait()
            ts(fs, fim, sg)
            ts(fns, fim, sg2)
            lk.wait()
            wide = lambda v: v.unsqueeze(2).to_broadcast([P, GROUPS, GC])
            q1, q2 = ptmp[:, 0, :], ptmp[:, 1, :]
            q1, q2 = (q.rearrange("p (a b) -> p a b", a=GROUPS) for q in (q1, q2))
            tt(Bb1, wide(fre), b1, ALU.mult)
            tt(q1, wide(fs), b2, ALU.mult)
            tt(Bb2, wide(fre), b2, ALU.mult)
            tt(q2, wide(fns), b1, ALU.mult)
            lk.wait()
            tt(Bb1, Bb1, q1, ALU.add)
            tt(Bb2, Bb2, q2, ALU.add)
            lk.wait()

            def powers(re, im, rows, n, cnt):
                b = lambda v: v[:, :, n:n + 1].to_broadcast([P, rows, cnt])
                q = [ptmp[:, k, 0:rows * cnt].rearrange("p (a b) -> p a b", a=rows) for k in range(4)]
                r, i = re[:, :, 1:cnt + 1], im[:, :, 1:cnt + 1]
                tt(q[0], r, b(re), ALU.mult)
                tt(q[1], i, b(im), ALU.mult)
                tt(q[2], r, b(im), ALU.mult)
                tt(q[3], i, b(re), ALU.mult)
                lk.wait()
                tt(re[:, :, n + 1:n + cnt + 1], q[0], q[1], ALU.subtract)
                tt(im[:, :, n + 1:n + cnt + 1], q[2], q[3], ALU.add)
                lk.wait()

            for n in (1, 2, 4):
                powers(Tre, Tim, 32, n, n)
            lk.add(eng.tensor_copy(cosT[:, :, 1], Tre[:, 16:32, CH]))
            lk.add(eng.tensor_copy(sinT[:, :, 1], Tim[:, 16:32, CH]))
            lk.wait()
            for n, cnt in ((1, 1), (2, 2), (4, 4), (8, 8), (16, 15)):
                powers(cosT, sinT, GROUPS, n, cnt)
            ts(sinT, sinT, sg2)
            tt(f1, mag, mag, ALU.mult)
            lk.wait()
            tt(f2, f1, f1, ALU.mult)
            lk.wait()
            tt(f3, f2, f2, ALU.mult)
            lk.wait()
            lk.add(eng.tensor_copy(mg[:, :, 1:NCH], f3.unsqueeze(2).to_broadcast([P, GROUPS, NCH - 1])))
            ts(prs, Tre[:, 0:16, :], sg2)
            ts(tims, Tim[:, 0:16, 0:CH], sg)
            lk.wait()
            b4 = lambda v, n: v.unsqueeze(3).to_broadcast([P, GROUPS, n, GC])
            c4 = lambda v, n: v.unsqueeze(2).to_broadcast([P, GROUPS, n, GC])
            tt(V, b4(prs, CH + 1), c4(c1, CH + 1), ALU.mult)
            tt(vt, b4(Tim[:, 0:16, :], CH + 1), c4(c2, CH + 1), ALU.mult)
            lk.wait()
            tt(V, V, vt, ALU.subtract)
            tt(Wpre, b4(Tre[:, 0:16, 0:CH], CH), c4(Bb1, CH), ALU.mult)
            lk.wait()
            tt(wt, b4(tims, CH), c4(Bb2, CH), ALU.mult)
            lk.wait()
            eng.tensor_tensor(Wpre, Wpre, wt, ALU.add).then_inc(prep_ready, 1)
            eng.wait_ge(prep_ready, l + 1)

        @block.gpsimd
        def _(pool):
            lk = Steps(pool, pool_step)
            g = nc.gpsimd
            g.memset(Mt, 0.0).then_inc(pool_z, 1)
            g.memset(Hs[:, :, 0], 0.0).then_inc(pool_z, 1)
            g.memset(mg[:, :, 0], 0.0).then_inc(pool_z, 1)
            g.memset(Tre[:, :, 0], 1.0).then_inc(pool_z, 1)
            g.memset(Tim[:, :, 0], 0.0).then_inc(pool_z, 1)
            g.memset(cosT[:, :, 0], 1.0).then_inc(pool_z, 1)
            g.memset(sinT[:, :, 0], 0.0).then_inc(pool_z, 1)

            def inv_root(dst, src, n, scale, eps, done, done_by=1):
                lk.link(g.tensor_scalar(src, src, scale, eps, ALU.mult, ALU.add))
                g.tensor_tensor(dst, src, C("mhalf")[:, 0:n], ALU.pow).then_inc(done, done_by)

            def norm_root(n):
                pool.wait_ge(ss_ready, NT * (n + 1))
                inv_root(st[:, 2:4], st[:, 0:2], NT, 1.0 / D, EPS, rstd_ready)

            def poles(l):
                S = lambda n: pv[:, n, :]
                mag, rden, dt, la, th, nn, red, den = S(0), S(3), S(4), S(5), S(6), S(7), S(8), S(18)
                q = S(19)
                are, aim = R(l, "are"), R(l, "aim")
                lk.add(g.tensor_tensor(dt, C("euler"), R(l, "logdt"), ALU.pow))
                lk.add(g.tensor_tensor(den, are, are, ALU.mult))
                lk.add(g.tensor_tensor(q, aim, aim, ALU.mult))
                lk.wait()
                lk.add(g.tensor_tensor(la, are, dt, ALU.mult))
                lk.add(g.tensor_tensor(th, aim, dt, ALU.mult))
                lk.add(g.tensor_tensor(den, den, q, ALU.add))
                lk.wait()
                lk.link(g.tensor_scalar(nn, th, float(1 / (2 * np.pi)), 12582912.0, ALU.mult, ALU.add))
                lk.link(g.tensor_scalar(nn, nn, -12582912.0, None, ALU.add))
                rest = 2 * np.pi
                src = th
                for k in range(3):
                    part = float(np.float32(np.round(rest * 2 ** (7 + 10 * k)) / 2 ** (7 + 10 * k))) if k < 2 \
                        else float(np.float32(rest))
                    rest -= part
                    lk.link(g.tensor_scalar(q, nn, -part, None, ALU.mult))
                    lk.link(g.tensor_tensor(red, src, q, ALU.add))
                    src = red
                g.tensor_scalar(red, red, 3.1415925, -3.1415925, ALU.min, ALU.max).then_inc(sincos_arg, 1)
                lk.add(g.tensor_tensor(mag, C("euler"), la, ALU.pow))
                lk.add(g.tensor_tensor(rden, den, C("mone"), ALU.pow))
                lk.wait()
                pool.wait_ge(trig_ready, 2 * (l + 1))
                cs = S(2)
                lk.link(g.tensor_tensor(cs, cs, cs, ALU.mult))
                g.tensor_scalar(cs, cs, -2.0, 1.0, ALU.mult, ALU.add).then_inc(poles_ready, 1)
                pool.wait_ge(poles_ready, l + 1)

            pool.wait_ge(cst_in, 16)
            norm_root(0)
            pool.wait_ge(par_in, 16)
            pool.wait_ge(pool_z, 7)
            poles(0)
            for l in range(2):
                pool.wait_ge(u_ready, 2 * (l + 1))
                pool.dma_start(scr_u.rearrange("(f p) n -> p f n", p=P),
                               uTr.rearrange("p f s k -> p f (s k)")).then_inc(u_out, 16)
                pool.wait_ge(u_out, 16 * (l + 1))
                for s in range(CH):
                    src = scr_u.rearrange("(g c) (s k) -> s c g k", c=GC, k=NCH)[CH - 1 - s]
                    pool.dma_start(U[GC * s:GC * (s + 1), :, :], src).then_inc(u_in, 16)
                pool.wait_ge(ssq_ready, l + 1)
                inv_root(st[:, 32:48], st[:, 16:32], 16, 1.0 / HD, EPS, rq_ready)
                pool.wait_ge(K_raw, 4 * (l + 1))
                g.tensor_tensor(Kall[0:GC, :, 0, :], Kall[0:GC, :, 0, :], R(l, "dskip", GROUPS, GC)[0:GC],
                                ALU.add).then_inc(K_ready, 1)
                pool.wait_ge(K_ready, l + 1)
                for s in range(CH):
                    pool.dma_start(Mt[GC * s:GC * (s + 1), :, CH - 1 - s:CH, :],
                                   Kall[0:GC, :, 0:s + 1, :]).then_inc(toep_in, 16)
                pool.wait_ge(gelu_ready, l + 1)
                ysb = G
                for t in range(CH):
                    dst = scr_y.rearrange("(g c) (s k) -> s c g k", c=GC, k=NCH)[t]
                    pool.dma_start(dst, ysb[GC * t:GC * (t + 1), :, :]).then_inc(y_out, 16)
                pool.wait_ge(y_out, 16 * CH * (l + 1))
                pool.dma_start(zT.rearrange("p f s k -> p f (s k)"),
                               scr_y.rearrange("(f p) n -> p f n", p=P)).then_inc(z_in, 16)
                pool.wait_ge(var_ready, l + 1)
                inv_root(st[:, 72:80], st[:, 64:72], 8, 1.0, 1e-5, rvar_ready)
                norm_root(2 * l + 1)
                if l == 0:
                    poles(1)
                    s5_setup(1, g, lk)
                    norm_root(2)

        @block.scalar
        def _(act):
            lk = Steps(act, act_step)
            s = nc.scalar

            def norm(n):
                l = n // 2
                for t in range(NT):
                    s.activation(xs[:, t, :], h[:, t, :], ACT.Square, accum_out=st[:, t:t + 1]).then_inc(ss_ready, 1)
                act.wait_ge(rstd_ready, n + 1)
                for t in range(NT):
                    s.activation(xs[:, t, :], h[:, t, :], ACT.Copy, scale=st[:, 2 + t:3 + t]).then_inc(xs_ready, 1)
                for kc in range(KC):
                    if kc % 2 == 0:
                        act.wait_ge(nT_ps, 4 * n + kc // 2 + 1)
                    gain = R(l, "g1" if n % 2 == 0 else "g2")[:, kc:kc + 1]
                    s.activation(xnT[:, kc, :], PB[kc // 2][:, 256 * (kc % 2):256 * (kc % 2) + 256],
                                 ACT.Copy, scale=gain).then_inc(xnT_ready, 1)

            act.wait_ge(x_in, 16)
            act.wait_ge(cst_in, 16)
            act.wait_ge(par_in, 16)

            def trig(l):
                act.wait_ge(sincos_arg, l + 1)
                s.activation(pv[:, 1, :], pv[:, 8, :], ACT.Sin).then_inc(trig_ready, 1)
                s.activation(pv[:, 2, :], pv[:, 8, :], ACT.Sin, scale=0.5).then_inc(trig_ready, 1)

            def blk(l, b):
                idx = {4: 0, 0: 1, 1: 2, 2: 3, 3: 4}[b]
                act.wait_ge(tile_used, BASE[l] + 2 * (idx + 1))
                for t in range(NT):
                    bank = {4: 4, 0: 0, 1: 2, 2: 4, 3: 0}[b] + t
                    if b == 4:
                        s.activation(proj[:, t, 2048:2304], PB[bank][:, 0:256], ACT.Silu).then_inc(proj_ready, 1)
                    elif b == 3:
                        s.activation(proj[:, t, 1536:1792], PB[bank][:, 0:256], ACT.Copy).then_inc(proj_ready, 1)
                        s.activation(proj[:, t, 1792:2048], PB[bank][:, 256:512], ACT.Silu).then_inc(proj_ready, 1)
                    else:
                        s.activation(proj[:, t, b * BLK:(b + 1) * BLK], PB[bank], ACT.Copy).then_inc(proj_ready, 1)

            norm(0)
            trig(0)
            for l in range(2):
                PR = 12 * l
                if l == 1:
                    act.wait_ge(h2_ready, 4)
                    norm(2)
                blk(l, 4)
                blk(l, 0)
                act.wait_ge(proj_ready, PR + 4)
                s.activation(xs[:, :, 0:512], proj[:, :, 0:512], ACT.Square).then_inc(sq_ready, 1)
                blk(l, 1)
                for q in range(4):
                    act.wait_ge(prepT_ps, 8 * l + q + 1)
                    s.activation(Wl[:, 4 * q:4 * q + 4, :].rearrange("p a b -> p (a b)"), PB[6 + q % 2],
                                 ACT.Copy).then_inc(prepT_ev, 1)
                for q in range(4):
                    act.wait_ge(prepT_ps, 8 * l + 4 + q + 1)
                    s.activation(Kall[0:GC, 4 * q:4 * q + 4, :, :].rearrange("p g a b -> p (g a b)"),
                                 PB[6 + q % 2][0:GC, :], ACT.Copy).then_inc(K_raw, 1)
                blk(l, 2)
                for q in range(2):
                    act.wait_ge(qkT_ps, 4 * l + q + 1)
                    s.activation(qkT[:, 2 * q:2 * q + 2, :].rearrange("p a b -> p (a b)"), PB[2 + q],
                                 ACT.Copy).then_inc(qkT_ready, 1)
                blk(l, 3)
                for t in range(NT):
                    for hh in range(HEADS):
                        if t == 0 and hh == 0:
                            act.wait_ge(negm_ready, l + 1)
                        c0, c1 = (0, 128) if t == 0 else (128, 384)
                        s.activation(E[:, hh, c0:c1], E[:, hh, c0:c1], ACT.Exp,
                                     bias=st[:, 88 + 4 * t + hh:89 + 4 * t + hh]).then_inc(exp_ready, 1)
                for q in range(2):
                    act.wait_ge(qkT_ps, 4 * l + 2 + q + 1)
                    s.activation(qkT[:, 4 + 2 * q:6 + 2 * q, :].rearrange("p a b -> p (a b)"), PB[4 + q],
                                 ACT.Copy).then_inc(qkT_ready, 1)
                act.wait_ge(y_ps, l + 1)
                s.activation(G.rearrange("p a b -> p (a b)"), PB[7], ACT.Gelu_apprx_tanh).then_inc(gelu_ready, 1)
                for hh in range(HEADS):
                    act.wait_ge(pT_ps, 4 * l + hh + 1)
                    s.activation(PT[:, hh, :], PB[2 + hh % 2][:, 0:384], ACT.Copy).then_inc(PT_ready, 1)
                for j in range(2):
                    act.wait_ge(glu_ps, l + 1)
                    s.activation(sgm[:, j, :, :].rearrange("p a b -> p (a b)"), PB[6][:, 256 * j:256 * j + 256],
                                 ACT.Sigmoid, bias=R(l, "glub")[:, j:j + 1]).then_inc(sgm_ready, 1)
                for c in range(6):
                    act.wait_ge(mT_ps, 3 * l + c // 2 + 1)
                    src = PB[c // 2][:, 256 * (c % 2):256 * (c % 2) + 256]
                    if c < 2:
                        s.activation(xnT[:, c, :], src, ACT.Copy).then_inc(mixT_ready, 1)
                    else:
                        s.activation(xnT[:, c, :], src, ACT.Copy,
                                     scale=R(l, "gn")[:, c - 2:c - 1]).then_inc(mixT_ready, 1)
                act.wait_ge(h1_ready, 4 * (l + 1))
                norm(2 * l + 1)
                if l == 0:
                    trig(1)

                    def silu(used, p):
                        act.wait_ge(tile_used, used)
                        s.activation(fsil[p], PB[p], ACT.Silu).then_inc(sil_ready, 1)

                    silu(gu_at(0), 0)
                    silu(gu_at(1), 1)
                    with act.Fori(0, PAIRS - 1) as i:
                        for j in range(2):
                            act.wait_ge(hT_ready, i * 2 + (j + 1))
                            silu(i * 6 + gu_at(j + 2), j)
                    act.wait_ge(hT_ready, FU - 2)
                    silu(gu_at(FU - 1), 0)

            act.wait_ge(lgm_ready, 1)
            s.activation(rt[:, 0:16], rt[:, 0:16], ACT.Exp).then_inc(lge_ready, 1)

            def expert_pass(ps):
                for q in range(4):
                    act.wait_ge(gT_ps, 4 * ps + q + 1)
                    s.activation(PTg[:, 2 * q:2 * q + 2, :].rearrange("p a b -> p (a b)"), PB[4 + q],
                                 ACT.Copy).then_inc(PTg_ready, 1)

                def gathered(val):
                    act.wait_ge(xg_ps, val)
                    for kc in range(4):
                        s.activation(xgT[:, kc, :], PB[1][:, 128 * kc:128 * kc + 128], ACT.Copy,
                                     scale=R(1, "g2")[:, kc:kc + 1]).then_inc(xgA_ready, 1)

                gathered(2 * (NE + 1) * ps + 1)
                with act.Fori(0, NE) as e:
                    n0, k0 = ps * NE * MU, ps * NE * ET

                    def silu(u):
                        act.wait_ge(mtile_used, e * ET + (k0 + mgu_at(u)))
                        s.activation(msil[u % 2], PB[u % 2], ACT.Silu).then_inc(msil_ready, 1)

                    def turned(u):
                        act.wait_ge(mhT_ps, e * MU + (n0 + u + 1))
                        s.activation(mhT[:, u % 2, :, :].rearrange("p a b -> p (a b)"), PB[6],
                                     ACT.Copy).then_inc(mhT_ready, 1)

                    silu(0)
                    for u in range(1, MU):
                        if u >= 2:
                            act.wait_ge(mh_ready, e * MU + (n0 + u - 1))
                        silu(u)
                        turned(u - 1)
                    gathered(e * 2 + (2 * (NE + 1) * ps + 3))
                    turned(MU - 1)
                    act.wait_ge(mh_ready, e * MU + (n0 + MU))
                    act.wait_ge(mtile_used, e * ET + (k0 + ET))
                    s.activation(yb[:, 0:BLK], PB[4], ACT.Copy).then_inc(yA_ready, 1)

            act.wait_ge(flag_ready, 1)
            more = act.value_load(flag[0:1, 0:1], min_val=0, max_val=1)
            expert_pass(0)
            with act.If(more > 0):
                expert_pass(1)

        @block.vector
        def _(dve):
            lk = Steps(dve, dve_step)
            v = nc.vector
            dve.wait_ge(par_in, 16)
            dve.wait_ge(cst_in, 16)
            dve.wait_ge(pool_z, 7)
            dve.wait_ge(poles_ready, 1)
            s5_setup(0, v, lk)
            for l in range(2):
                PR = 12 * l
                for f in range(2):
                    dve.wait_ge(tile_used, BASE[l] + 2)
                    if l:
                        dve.wait_ge(u_out, 16 * l)
                    v.tensor_copy(uTr[:, f, :, :].rearrange("p s k -> p k s"),
                                  PB[6 + f][:, 0:256].rearrange("p (k s) -> p k s", s=CH)).then_inc(u_ready, 1)
                dve.wait_ge(sq_ready, l + 1)
                v.tensor_reduce(st[:, 16:32].rearrange("p (t h) -> p t h", t=NT), xs[:, :, 0:512].rearrange("p t (h d) -> p t h d", d=HD),
                                AX_X, ALU.add).then_inc(ssq_ready, 1)
                dve.wait_ge(rq_ready, l + 1)
                rs = st[:, 32:48].rearrange("p (t h) -> p t h", t=NT)
                for t in range(NT):
                    qk = proj[:, t, 0:512].rearrange("p (h d) -> p h d", d=HD)
                    lk.add(v.tensor_tensor(qk, qk, rs[:, t, :].unsqueeze(2).to_broadcast([P, 8, HD]), ALU.mult))
                lk.wait()
                for t in range(NT):
                    qk = proj[:, t, 0:512].rearrange("p (w h d) -> p w h d", w=2, d=HD)
                    gain = R(l, "qkg", 2, HD).unsqueeze(2).to_broadcast([P, 2, HEADS, HD])
                    lk.add(v.tensor_tensor(qk, qk, gain, ALU.mult))
                lk.wait()

                def rope(col, half, cos, sin, tmp, done, val):
                    n = 8 * half
                    for t in range(NT):
                        xx = proj[:, t, col:col + 512].rearrange("p (h d) -> p h d", d=HD)
                        x1, x2 = xx[:, :, 0:half], xx[:, :, half:2 * half]
                        co = cos[:, t, :].unsqueeze(1).to_broadcast([P, 8, half])
                        si = sin[:, t, :].unsqueeze(1).to_broadcast([P, 8, half])
                        q = [tmp[k].rearrange("p (h d) -> p h d", d=half) for k in range(4)]
                        if t:
                            lk.wait()
                        lk.add(v.tensor_tensor(q[0], x1, co, ALU.mult))
                        lk.add(v.tensor_tensor(q[1], x2, si, ALU.mult))
                        lk.add(v.tensor_tensor(q[2], x2, co, ALU.mult))
                        lk.add(v.tensor_tensor(q[3], x1, si, ALU.mult))
                        lk.wait()
                        v.tensor_tensor(x1, q[0], q[1], ALU.subtract).then_inc(done, 1)
                        v.tensor_tensor(x2, q[2], q[3], ALU.add).then_inc(done, 1)
                        dve.wait_ge(done, val + 2 * t + 2)

                rope(QC, 8, C("cosA", NT, 8), C("sinA", NT, 8),
                     [rtA[:, k, 0:64] for k in range(4)], qk_ready, 4 * l)

                flat = lambda w: w.rearrange("p a b -> p (a b)")
                dve.wait_ge(x_ps, l + 1)
                v.tensor_copy(flat(xsb), PB[6]).then_inc(x_sb, 1)
                dve.wait_ge(x_sb, l + 1)
                lk.add(v.tensor_tensor(flat(t1), flat(xsb), flat(cosT), ALU.mult))
                dve.wait_ge(perm_ps, 2 * l + 1)
                lk.add(v.tensor_tensor(flat(t2), PB[7], flat(sinT), ALU.mult))
                lk.wait()
                lk.link(v.tensor_tensor(flat(t1), flat(t1), flat(t2), ALU.add))
                if l:
                    dve.wait_ge(y_out, 16 * CH * l)
                v.tensor_tensor_scan(flat(G), flat(mg), flat(t1), 0.0, ALU.mult, ALU.add).then_inc(scan_ready, 1)
                dve.wait_ge(scan_ready, l + 1)
                dve.wait_ge(proj_ready, PR + 8)
                rope(QR, 32, C("cosR", NT, 32), C("sinR", NT, 32),
                     [xs[:, 0, 256 * k:256 * k + 256] for k in range(4)], qr_ready, 4 * l)
                lk.add(v.tensor_tensor(flat(t1), flat(G), flat(cosT), ALU.mult))
                dve.wait_ge(perm_ps, 2 * l + 2)
                lk.add(v.tensor_tensor(flat(t2), PB[6], flat(sinT), ALU.mult))
                lk.wait()
                v.tensor_tensor(Hs[:, :, 1:NCH + 1], t1, t2, ALU.subtract).then_inc(hs_ready, 1)
                for hh in range(HEADS):
                    dve.wait_ge(s_ps, 4 * l + hh + 1)
                    if hh == 0:
                        dve.wait_ge(toep_in, 16 * CH * (l + 1))
                    v.scalar_tensor_tensor(E[:, hh, :], PB[hh][:, 0:384], HD ** -0.5, C("mask"),
                                           ALU.mult, ALU.add).then_inc(s_masked, 1)
                dve.wait_ge(s_masked, 4 * (l + 1))
                lk.add(v.tensor_reduce(st[:, 80:84], E[:, :, 0:128], AX_X, ALU.max))
                lk.add(v.tensor_reduce(st[:, 84:88], E[:, :, 128:384], AX_X, ALU.max))
                lk.wait()
                v.tensor_scalar(st[:, 88:96], st[:, 80:88], -1.0, None, ALU.mult).then_inc(negm_ready, 1)
                for hh in range(2):
                    dve.wait_ge(rs_ps, 4 * l + hh + 1)
                    v.tensor_tensor(AT[:, hh, :], PB[4 + hh][:, 0:384], C("decay", 4, 384)[:, hh, :],
                                    ALU.mult).then_inc(AT_ready, 1)
                dve.wait_ge(exp_ready, 8 * (l + 1))
                v.tensor_tensor(E, E, C("count").unsqueeze(1).to_broadcast([P, HEADS, 384]),
                                ALU.mult).then_inc(p_ready, 1)
                for hh in range(2, 4):
                    dve.wait_ge(rs_ps, 4 * l + hh + 1)
                    v.tensor_tensor(AT[:, hh, :], PB[hh - 2][:, 0:384], C("decay", 4, 384)[:, hh, :],
                                    ALU.mult).then_inc(AT_ready, 1)
                dve.wait_ge(p_ready, l + 1)
                lk.add(v.tensor_reduce(st[:, 96:100], E[:, :, 0:128], AX_X, ALU.add))
                lk.add(v.tensor_reduce(st[:, 100:104], E[:, :, 128:384], AX_X, ALU.add))
                lk.wait()
                lk.link(v.reciprocal(st[:, 104:112], st[:, 96:104]))
                mv = st[:, 48:64].rearrange("p (n c) -> p n c", c=2)
                for t in range(NT):
                    dve.wait_ge(ry_ps, 2 * l + t + 1)
                    for hh in range(HEADS):
                        lk.add(v.bn_stats(st[:, 112 + 6 * (4 * t + hh):118 + 6 * (4 * t + hh)],
                                          PB[4 + t][:, 128 * hh:128 * hh + 128]))
                lk.wait()
                for n in range(8):
                    lk.add(v.bn_aggr(mv[:, n, :], st[:, 112 + 6 * n:118 + 6 * n]))
                lk.wait()
                v.tensor_copy(st[:, 64:72], mv[:, :, 1]).then_inc(var_ready, 1)
                dve.wait_ge(att_ps, l + 1)
                rl = st[:, 104:112].rearrange("p (t h) -> p t h", t=NT)
                for t in range(NT):
                    v.tensor_tensor(xs[:, t, 0:256].rearrange("p (h d) -> p h d", d=HD),
                                    PB[7][:, 256 * t:256 * t + 256].rearrange("p (h d) -> p h d", d=HD),
                                    rl[:, t, :].unsqueeze(2).to_broadcast([P, HEADS, HD]),
                                    ALU.mult).then_inc(mixed_ready, 1)
                dve.wait_ge(proj_ready, PR + 12)
                for t in range(NT):
                    for hh in range(HEADS):
                        gcol = GR + 128 * hh
                        lk.add(v.scalar_tensor_tensor(xs[:, t, 256 + 128 * hh:384 + 128 * hh],
                                                      PB[4 + t][:, 128 * hh:128 * hh + 128],
                                                      mv[:, 4 * t + hh, 0:1], proj[:, t, gcol:gcol + 128],
                                                      ALU.subtract, ALU.mult))
                lk.wait()
                dve.wait_ge(rvar_ready, l + 1)
                rv = st[:, 72:80].rearrange("p (t h) -> p t h", t=NT)
                for t in range(NT):
                    z = xs[:, t, 256:768].rearrange("p (h d) -> p h d", d=RV)
                    v.tensor_tensor(z, z, rv[:, t, :].unsqueeze(2).to_broadcast([P, HEADS, RV]),
                                    ALU.mult).then_inc(mixed_ready, 1)
                dve.wait_ge(sgm_ready, 2 * (l + 1))
                dve.wait_ge(z_in, 16 * (l + 1))
                for j in range(2):
                    v.tensor_tensor(xnT[:, 6 + j, :].rearrange("p (k s) -> p s k", s=CH), zT[:, j, :, :],
                                    sgm[:, j, :, :], ALU.mult).then_inc(mixS_ready, 1)
                for n in range(2):
                    dve.wait_ge(tile_used, BASE[l] + MIX - 1 + n)
                    for t in range(NT):
                        hn = h[:, t, n * BLK:(n + 1) * BLK]
                        v.tensor_tensor(hn, hn, PB[4 + 2 * n + t], ALU.add).then_inc(h1_ready, 1)
                if l == 0:
                    def product(val, p):
                        dve.wait_ge(sil_ready, val)
                        v.tensor_tensor(fhT[p].rearrange("p a b -> p (a b)"), fsil[p], PB[2 + p],
                                        ALU.mult).then_inc(hT_ready, 1)

                    product(1, 0)
                    product(2, 1)
                    with dve.Fori(0, PAIRS - 1) as i:
                        for j in range(2):
                            dve.wait_ge(tile_used, i * 6 + d_at(j))
                            product(i * 2 + (j + 3), j)
                    dve.wait_ge(tile_used, d_at(FU - 3))
                    product(FU, 0)
                    dve.wait_ge(h1_ready, 4)
                    dve.wait_ge(tile_used, d_at(FU - 1))
                    for n in range(2):
                        for t in range(NT):
                            hn = h[:, t, n * BLK:(n + 1) * BLK]
                            v.tensor_tensor(hn, hn, PB[4 + 2 * n + t], ALU.add).then_inc(h2_ready, 1)

            lg = rt[:, 0:16].rearrange("p (t e) -> p t e", t=NT)
            pr = lg
            S2 = lambda k: rt[:, 16 + 2 * k:18 + 2 * k]
            S16 = lambda k: rt[:, 48 + 16 * k:64 + 16 * k].rearrange("p (t e) -> p t e", t=NT)
            e8 = lambda w: w.unsqueeze(2).to_broadcast([P, NT, NE])
            rev = C("rev").unsqueeze(1).to_broadcast([P, NT, NE])
            dve.wait_ge(lg_ps, 1)
            lk.link(v.tensor_reduce(S2(0), PB[4][:, 0:16].rearrange("p (t e) -> p t e", t=NT), AX_X, ALU.max))
            v.tensor_tensor(lg, PB[4][:, 0:16].rearrange("p (t e) -> p t e", t=NT), e8(S2(0)),
                            ALU.subtract).then_inc(lgm_ready, 1)
            dve.wait_ge(lge_ready, 1)
            lk.link(v.tensor_reduce(S2(1), lg, AX_X, ALU.add))
            lk.link(v.reciprocal(S2(2), S2(1)))
            lk.link(v.tensor_tensor(pr, lg, e8(S2(2)), ALU.mult))

            def best(src, top_, one, tmp, k):
                lk.link(v.tensor_reduce(top_, src, AX_X, ALU.max))
                lk.link(v.tensor_tensor(tmp, src, e8(top_), ALU.is_ge))
                lk.link(v.tensor_tensor(tmp, tmp, rev, ALU.mult))
                lk.link(v.tensor_reduce(S2(k), tmp, AX_X, ALU.max))
                lk.link(v.tensor_tensor(one, tmp, e8(S2(k)), ALU.is_ge))

            best(pr, S2(3), S16(0), S16(1), 4)
            lk.link(v.scalar_tensor_tensor(S16(2), S16(0), -2.0, pr, ALU.mult, ALU.add))
            best(S16(2), S2(5), S16(3), S16(1), 6)
            mask = S16(4)
            v.tensor_tensor(mask, S16(0), S16(3), ALU.add).then_inc(mask_ready, 1)
            lk.link(v.tensor_tensor(S2(7), S2(3), S2(5), ALU.add))
            lk.link(v.reciprocal(S2(8), S2(7)))
            lk.add(v.tensor_tensor(S2(9), S2(3), S2(8), ALU.mult))
            lk.add(v.tensor_tensor(S2(10), S2(5), S2(8), ALU.mult))
            lk.wait()
            gate = S16(5)
            lk.add(v.tensor_tensor(gate, S16(0), e8(S2(9)), ALU.mult))
            lk.add(v.tensor_tensor(S16(6), S16(3), e8(S2(10)), ALU.mult))
            lk.wait()
            lk.link(v.tensor_tensor(gate, gate, S16(6), ALU.add))
            slot = S16(7)
            dve.wait_ge(mask_ready, 1)
            dve.wait_ge(pos_ps, 1)
            lk.link(v.scalar_tensor_tensor(slot, PB[5][:, 0:16].rearrange("p (t e) -> p t e", t=NT), 1.0, mask,
                                           ALU.add, ALU.mult))
            lk.link(v.tensor_scalar(slot, slot, -1.0, None, ALU.add))
            lk.link(v.tensor_reduce(S2(11)[:, 0:1], PB[5][:, 16:24], AX_X, ALU.max))
            v.tensor_scalar(flag[:, 0:1], S2(11)[:, 0:1], float(P), None, ALU.is_gt).then_inc(flag_ready, 1)
            v.memset(PH[:, :, NE, :], 0.0).then_inc(first_y, 1)

            def expert_pass(ps):
                if ps:
                    lk.link(v.tensor_scalar(slot, slot, -float(P), None, ALU.add))
                for e in range(NE):
                    for t in range(NT):
                        v.tensor_scalar(PH[:, t, e, :], C("iota"), slot[:, t, e:e + 1], None,
                                        ALU.is_equal).then_inc(hot_ready, 1)
                        v.tensor_scalar(PG[:, t, e, :], C("iota"), slot[:, t, e:e + 1], gate[:, t, e:e + 1],
                                        ALU.is_equal, ALU.mult).then_inc(hot_ready, 1)
                v.memset(yb[:, 0:BLK], 0.0).then_inc(yA_ready, 1)
                v.memset(yb[:, BLK:D], 0.0).then_inc(yD_ready, 1)
                v.memset(PTcur, 0.0).then_inc(yD_ready, 1)

                def gathered(val):
                    dve.wait_ge(xg_ps, val)
                    for kc in range(4, KC):
                        v.tensor_scalar(xgT[:, kc, :], PB[3][:, 128 * (kc - 4):128 * (kc - 3)],
                                        R(1, "g2")[:, kc:kc + 1], None, ALU.mult).then_inc(xgD_ready, 1)

                def scattered(q, val):
                    t, n = q // 2, q % 2
                    dve.wait_ge(sc_ps, val)
                    hn = h[:, t, n * BLK:(n + 1) * BLK]
                    v.tensor_tensor(hn, hn, PB[7], ALU.add).then_inc(sc_done, 1)

                dve.wait_ge(h1_ready, 8)
                gathered(2 * (NE + 1) * ps + 2)
                with dve.Fori(0, NE) as e:
                    n0 = ps * NE * MU
                    s0 = ps * 4 * (NE + 1)
                    for u in range(MU):
                        dve.wait_ge(msil_ready, e * MU + (n0 + u + 1))
                        if u >= 2:
                            dve.wait_ge(mhT_ps, e * MU + (n0 + u - 1))
                        v.tensor_tensor(mh[:, u % 2, :], msil[u % 2], PB[2 + u % 2],
                                        ALU.mult).then_inc(mh_ready, 1)
                        if u < 4:
                            if u:
                                dve.wait_ge(sc_done, e * 4 + (s0 + u))
                            scattered(u, e * 4 + (s0 + u + 1))
                    gathered(e * 2 + (2 * (NE + 1) * ps + 4))
                    dve.wait_ge(mtile_used, e * ET + (ps * NE * ET + ET))
                    v.tensor_copy(yb[:, BLK:D], PB[5]).then_inc(yD_ready, 1)
                    dve.wait_ge(PTg_ready, 4 * (ps + 1))
                    v.tensor_copy(PTcur, PTg[:, bass.ds(e, 1), :].rearrange("p a b -> p (a b)")).then_inc(yD_ready, 1)
                for q in range(4):
                    dve.wait_ge(sc_done, ps * 4 * (NE + 1) + 4 * NE + q)
                    scattered(q, ps * 4 * (NE + 1) + 4 * NE + q + 1)
                dve.wait_ge(sc_done, (ps + 1) * 4 * (NE + 1))

            dve.wait_ge(flag_ready, 1)
            more = dve.value_load(flag[0:1, 0:1], min_val=0, max_val=1)
            expert_pass(0)
            with dve.If(more > 0):
                expert_pass(1)
            v.memset(rt[:, 0:16], 0.0).then_inc(out_ready, 1)

        @block.tensor
        def _(pe):
            m = nc.tensor.matmul
            tr = nc.tensor.transpose
            pe.wait_ge(cst_in, 16)

            def norm_turn(n):
                for q in range(4):
                    for c in range(2):
                        for t in range(NT):
                            if q == 0 and c == 0:
                                pe.wait_ge(xs_ready, NT * n + t + 1)
                            kc = 2 * q + c
                            last = tr(PB[q][:, 256 * c + 128 * t:256 * c + 128 * t + 128],
                                      xs[:, t, kc * P:(kc + 1) * P], ident)
                    last.then_inc(nT_ps, 1)

            def arrived(k):
                pe.wait_ge(tile_in[k % RA], 16 * (k // RA + 1))

            def block_of(l, b, idx):
                b0 = {4: 4, 0: 0, 1: 2, 2: 4, 3: 0}[b]
                for kh in range(2):
                    k = BASE[l] + 2 * idx + kh
                    arrived(k)
                    w = ringA[k % RA].rearrange("p (c n) -> p c n", c=4)
                    for c in range(4):
                        kc = 4 * kh + c
                        if idx == 0:
                            pe.wait_ge(xnT_ready, KC * 2 * l + kc + 1)
                        a_, z_ = kc == 0, kc == KC - 1
                        for t in range(NT):
                            n = 256 if b == 4 else BLK
                            last = m(PB[b0 + t][:, 0:n], xnT[:, kc, t * P:(t + 1) * P], w[:, c, 0:n],
                                     start=a_, stop=z_)
                        if b == 4:
                            for f in range(2):
                                last = m(PB[6 + f][:, 0:256], w[:, c, 256 + f * P:256 + (f + 1) * P],
                                         xnT[:, kc, :], start=a_, stop=z_)
                    if kh == 0:
                        last.then_inc(tile_used, 1)
                last.then_inc(tile_used, 1)

            for l in range(2):
                PR = 12 * l
                norm_turn(2 * l)
                block_of(l, 4, 0)
                block_of(l, 0, 1)
                block_of(l, 1, 2)
                pe.wait_ge(prep_ready, l + 1)
                pe.wait_ge(u_ready, 2 * (l + 1))
                for q in range(4):
                    if q >= 2:
                        pe.wait_ge(prepT_ev, 4 * l + q - 1)
                    for k in range(4):
                        last = tr(PB[6 + q % 2][:, 128 * k:128 * k + 128],
                                  Wpre[:, 4 * q + k, :, :].rearrange("p a b -> p (a b)"), ident)
                    last.then_inc(prepT_ps, 1)
                for q in range(4):
                    if q < 2:
                        pe.wait_ge(prepT_ev, 4 * l + 3 + q)
                    else:
                        pe.wait_ge(K_raw, 4 * l + q - 1)
                    for k in range(4):
                        gq = 4 * q + k
                        last = m(PB[6 + q % 2][0:GC, 128 * k:128 * k + 128], Bb1[:, gq, :],
                                 V[:, gq, 0:CH, :].rearrange("p a b -> p (a b)"), start=True, stop=True)
                    last.then_inc(prepT_ps, 1)
                pe.wait_ge(u_in, 16 * CH * (l + 1))
                pe.wait_ge(K_raw, 4 * l + 3)
                for gq in range(GROUPS):
                    last = m(PB[6][:, NCH * gq:NCH * (gq + 1)], Wl[:, gq, :], U[:, gq, :],
                             start=True, stop=True)
                last.then_inc(x_ps, 1)
                pe.wait_ge(proj_ready, PR + 2)
                block_of(l, 2, 3)
                pe.wait_ge(x_sb, l + 1)
                pe.wait_ge(K_raw, 4 * l + 4)
                m(PB[7], C("swap"), xsb.rearrange("p a b -> p (a b)"), start=True, stop=True).then_inc(perm_ps, 1)

                def turn_qk(c0, bank):
                    for c in range(2):
                        for t in range(NT):
                            col = c0 + 128 * c
                            last = tr(PB[bank][:, 256 * c + 128 * t:256 * c + 128 * t + 128],
                                      proj[:, t, col:col + 128], ident)
                    last.then_inc(qkT_ps, 1)

                pe.wait_ge(qk_ready, 4 * (l + 1))
                pe.wait_ge(proj_ready, PR + 6)
                turn_qk(QC, 2)
                turn_qk(QC + 256, 3)
                block_of(l, 3, 4)
                pe.wait_ge(scan_ready, l + 1)
                m(PB[6], C("swap"), G.rearrange("p a b -> p (a b)"), start=True, stop=True).then_inc(perm_ps, 1)
                pe.wait_ge(proj_ready, PR + 12)
                pe.wait_ge(qkT_ready, 4 * l + 2)
                for hh in range(HEADS):
                    lo = 64 * (hh % 2)
                    q_, k_ = qkT[lo:lo + 64, hh // 2, :], qkT[lo:lo + 64, 2 + hh // 2, :]
                    m(PB[hh][:, 0:128], q_[:, 0:128], k_[:, 0:128], start=True, stop=True)
                    m(PB[hh][:, 128:384], q_[:, 128:256], k_, start=True, stop=True).then_inc(s_ps, 1)
                pe.wait_ge(qr_ready, 4 * (l + 1))
                turn_qk(QR, 4)
                turn_qk(KR, 5)
                pe.wait_ge(toep_in, 16 * CH * (l + 1))
                pe.wait_ge(hs_ready, l + 1)
                for gq in range(GROUPS):
                    y_ = PB[7][:, NCH * gq:NCH * (gq + 1)]
                    m(y_, Mt[:, gq, :, :].rearrange("p a b -> p (a b)"), U[:, gq, :], start=True, stop=False)
                    last = m(y_, V[:, gq, 1:CH + 1, :].rearrange("p a b -> p (a b)"), Hs[:, gq, 0:NCH],
                             start=False, stop=True)
                last.then_inc(y_ps, 1)
                for hh in range(HEADS):
                    if hh == 0:
                        pe.wait_ge(qkT_ready, 4 * (l + 1))
                    if hh == 2:
                        pe.wait_ge(s_masked, 4 * l + 2)
                    bank = PB[(4, 5, 0, 1)[hh]]
                    lo = 64 * (hh % 2)
                    q_, k_ = qkT[lo:lo + 64, 4 + hh // 2, :], qkT[lo:lo + 64, 6 + hh // 2, :]
                    m(bank[:, 0:256], k_[:, 0:128], q_, start=True, stop=True)
                    m(bank[:, 256:384], k_[:, 128:256], q_[:, 128:256], start=True, stop=True).then_inc(rs_ps, 1)
                pe.wait_ge(p_ready, l + 1)
                for hh in range(HEADS):
                    if hh >= 2:
                        pe.wait_ge(PT_ready, 4 * l + hh - 1)
                    for k in range(3):
                        last = tr(PB[2 + hh % 2][:, 128 * k:128 * k + 128], E[:, hh, 128 * k:128 * k + 128], ident)
                    last.then_inc(pT_ps, 1)
                pe.wait_ge(AT_ready, 4 * (l + 1))
                for t in range(NT):
                    for hh in range(HEADS):
                        o = PB[4 + t][:, 128 * hh:128 * hh + 128]
                        c0 = VR + RV * hh
                        last = m(o, AT[:, hh, 128 * t:128 * t + 128], proj[:, 0, c0:c0 + RV],
                                 start=True, stop=t == 0)
                        if t:
                            last = m(o, AT[:, hh, 256:384], proj[:, 1, c0:c0 + RV], start=False, stop=True)
                    last.then_inc(ry_ps, 1)
                pe.wait_ge(gelu_ready, l + 1)
                pe.wait_ge(PT_ready, 4 * (l + 1))
                for t in range(NT):
                    for hh in range(HEADS):
                        o = PB[7][:, 256 * t + HD * hh:256 * t + HD * (hh + 1)]
                        c0 = VC + HD * hh
                        last = m(o, PT[:, hh, 128 * t:128 * t + 128], proj[:, 0, c0:c0 + HD],
                                 start=True, stop=t == 0)
                        if t:
                            last = m(o, PT[:, hh, 256:384], proj[:, 1, c0:c0 + HD], start=False, stop=True)
                last.then_inc(att_ps, 1)
                pe.wait_ge(z_in, 16 * (l + 1))
                gw = R(l, "gluw", 2, 256)
                for j in range(2):
                    for f in range(2):
                        last = m(PB[6][:, 256 * j:256 * j + 256], gw[:, f, 128 * j:128 * j + 128],
                                 zT[:, f, :, :].rearrange("p a b -> p (a b)"), start=f == 0, stop=f == 1)
                last.then_inc(glu_ps, 1)
                pe.wait_ge(mixed_ready, 4 * (l + 1))
                for q in range(3):
                    for c in range(2):
                        for t in range(NT):
                            cc = 2 * q + c
                            last = tr(PB[q][:, 256 * c + 128 * t:256 * c + 128 * t + 128],
                                      xs[:, t, cc * P:(cc + 1) * P], ident)
                    last.then_inc(mT_ps, 1)
                pe.wait_ge(sgm_ready, 2 * (l + 1))
                for j in range(4):
                    k, kh, n = BASE[l] + 10 + j, j // 2, j % 2
                    arrived(k)
                    w = ringA[k % RA].rearrange("p (c n) -> p c n", c=4)
                    for c in range(4):
                        cc = 4 * kh + c
                        if n == 0:
                            if cc < 6:
                                pe.wait_ge(mixT_ready, 6 * l + cc + 1)
                            else:
                                pe.wait_ge(mixS_ready, 2 * l + cc - 5)
                        for t in range(NT):
                            last = m(PB[4 + 2 * n + t], xnT[:, cc, t * P:(t + 1) * P], w[:, c, :],
                                     start=cc == 0, stop=cc == KC - 1)
                    last.then_inc(tile_used, 1)
                norm_turn(2 * l + 1)
                if l == 0:
                    def turns_in(kk, i):
                        pe.wait_ge(tile_in[kk % RA], (16 * (kk // RA + 1)) if i is None else i * 16 + 16 * (kk // RA + 1))
                        return ringA[kk % RA]

                    def gate_up(kk, i, p, first):
                        for which in range(2):
                            w = turns_in(kk + which, i).rearrange("p (c n) -> p c n", c=KC)
                            for j in range(2):
                                for kc in range(KC):
                                    if first and which == 0 and j == 0:
                                        pe.wait_ge(xnT_ready, KC + max(kc + 1, 2))
                                    last = m(PB[2 * which + p][:, 256 * j:256 * j + 256],
                                             w[:, kc, P * j:P * (j + 1)], xnT[:, kc, :],
                                             start=kc == 0, stop=kc == KC - 1)
                            last.then_inc(tile_used, 1)

                    def down(kk, i, p, first, final):
                        w = turns_in(kk, i).rearrange("p (c n) -> p c n", c=2)
                        for j in range(2):
                            for t in range(NT):
                                for n in range(2):
                                    last = m(PB[4 + 2 * n + t], fhT[p][:, j, t * P:(t + 1) * P],
                                             w[:, j, n * BLK:(n + 1) * BLK], start=first and j == 0,
                                             stop=final and j == 1, skip_group_check=True)
                        last.then_inc(tile_used, 1)

                    gate_up(MIX, None, 0, True)
                    gate_up(MIX + 2, None, 1, False)
                    pe.wait_ge(hT_ready, 1)
                    down(MIX + 4, None, 0, True, False)
                    with pe.Fori(0, PAIRS - 1) as i:
                        for j in range(2):
                            u = j + 2
                            gate_up(MIX + 3 * u - 1, i, u % 2, False)
                            pe.wait_ge(hT_ready, i * 2 + u)
                            down(MIX + 3 * u + 1, i, (u - 1) % 2, False, False)
                    u = FU - 1
                    gate_up(MIX + 3 * u - 1, None, 0, False)
                    pe.wait_ge(hT_ready, u)
                    down(MIX + 3 * u + 1, None, 1, False, False)
                    pe.wait_ge(hT_ready, FU)
                    down(MIX + 3 * u + 2, None, 0, False, True)

            pe.wait_ge(router_in, 16)
            for t in range(NT):
                for kc in range(KC):
                    if t == 0:
                        pe.wait_ge(xnT_ready, 3 * KC + kc + 1)
                    last = m(PB[4][:, 8 * t:8 * t + 8], xnT[:, kc, t * P:(t + 1) * P], router[:, kc, :],
                             start=kc == 0, stop=kc == KC - 1)
            last.then_inc(lg_ps, 1)
            pe.wait_ge(mask_ready, 1)
            chosen = rt[:, 48 + 64:48 + 80].rearrange("p (t e) -> p t e", t=NT)
            m(PB[5][:, 0:8], C("tri"), chosen[:, 0, :], start=True, stop=True)
            m(PB[5][:, 8:16], C("ones"), chosen[:, 0, :], start=True, stop=False)
            m(PB[5][:, 8:16], C("tri"), chosen[:, 1, :], start=False, stop=True)
            m(PB[5][:, 16:24], C("ones"), chosen[:, 0, :], start=True, stop=False)
            m(PB[5][:, 16:24], C("ones"), chosen[:, 1, :], start=False, stop=True).then_inc(pos_ps, 1)

            def expert_pass(ps):
                G0 = (NE + 1) * ps

                def gather(e):
                    for half in range(2):
                        for c in range(4):
                            kc = 4 * half + c
                            for t in range(NT):
                                hot = (PH[:, t, e, :] if isinstance(e, int)
                                       else PH[:, t, bass.ds(e, 1), :].rearrange("p a b -> p (a b)"))
                                last = m(PB[1 + 2 * half][:, 128 * c:128 * c + 128], xs[:, t, kc * P:(kc + 1) * P],
                                         hot, start=t == 0, stop=t == NT - 1)
                        last.then_inc(xg_ps, 1)

                def scatter(q):
                    t, n = q // 2, q % 2
                    m(PB[7], PTcur[:, t * P:(t + 1) * P], yb[:, n * BLK:(n + 1) * BLK],
                      start=True, stop=True).then_inc(sc_ps, 1)

                pe.wait_ge(first_y, 1)
                pe.wait_ge(hot_ready, 32 * ps + 4)
                gather(0)
                pe.wait_ge(hot_ready, 32 * ps + 32)
                for e in range(NE):
                    for t in range(NT):
                        c0 = 256 * (e % 2) + 128 * t
                        last = tr(PB[4 + e // 2][:, c0:c0 + 128], PG[:, t, e, :], ident)
                    if e % 2:
                        last.then_inc(gT_ps, 1)
                pe.wait_ge(PTg_ready, 4 * (ps + 1))
                with pe.Fori(0, NE) as e:
                    n0, s0 = ps * NE * MU, ps * 4 * (NE + 1)

                    def came(mt):
                        pe.wait_ge(mtile_in[mt % RM], e * (16 * ER) + 16 * (ps * NE * ER + mt // RM + 1))
                        return ringM[mt % RM]

                    def gate_up(u):
                        mt = 0 if u == 0 else 6 * u - 2
                        if u >= 2:
                            pe.wait_ge(mh_ready, e * MU + (n0 + u - 1))
                        for which in range(2):
                            for half in range(2):
                                w = came(mt + 2 * which + half).rearrange("p (c n) -> p c n", c=4)
                                for c in range(4):
                                    kc = 4 * half + c
                                    if u == 0 and which == 0:
                                        pe.wait_ge(xgD_ready if half else xgA_ready, e * 4 + (4 * G0 + c + 1))
                                    last = m(PB[2 * which + u % 2], xgT[:, kc, :], w[:, c, :],
                                             start=kc == 0, stop=kc == KC - 1)
                                last.then_inc(mtile_used, 1)

                    def turn(u):
                        pe.wait_ge(mh_ready, e * MU + (n0 + u + 1))
                        for k in range(4):
                            last = tr(PB[6][:, 128 * k:128 * k + 128], mh[:, u % 2, 128 * k:128 * k + 128], ident)
                        last.then_inc(mhT_ps, 1)

                    def down(u):
                        mt = 6 * u + 8 if u < MU - 1 else 6 * u + 4
                        pe.wait_ge(mhT_ready, e * MU + (n0 + u + 1))
                        for half in range(2):
                            w = came(mt + half).rearrange("p (c n) -> p c n", c=2)
                            for c in range(2):
                                j = 2 * half + c
                                for n in range(2):
                                    last = m(PB[4 + n], mhT[:, u % 2, j, :], w[:, c, n * BLK:(n + 1) * BLK],
                                             start=u == 0 and j == 0, stop=u == MU - 1 and j == 3,
                                             skip_group_check=True)
                            last.then_inc(mtile_used, 1)

                    for u in range(MU):
                        gate_up(u)
                        if u == 0:
                            pe.wait_ge(yA_ready, e + (G0 + 1))
                            pe.wait_ge(yD_ready, e * 2 + (2 * G0 + 2))
                        if u < 4:
                            if u:
                                pe.wait_ge(sc_done, e * 4 + (s0 + u))
                            scatter(u)
                        if u:
                            turn(u - 1)
                            down(u - 1)
                    pe.wait_ge(sc_done, e * 4 + (s0 + 4))
                    gather(e + 1)
                    turn(MU - 1)
                    down(MU - 1)
                pe.wait_ge(yA_ready, NE + G0 + 1)
                pe.wait_ge(yD_ready, 2 * (NE + G0 + 1))
                for q in range(4):
                    if q:
                        pe.wait_ge(sc_done, 4 * (NE + G0) + q)
                    scatter(q)
                pe.wait_ge(sc_done, 4 * (NE + G0 + 1))
                pe.wait_ge(xgA_ready, 4 * (NE + G0 + 1))
                pe.wait_ge(xgD_ready, 4 * (NE + G0 + 1))

            pe.wait_ge(flag_ready, 1)
            more = pe.value_load(flag[0:1, 0:1], min_val=0, max_val=1)
            expert_pass(0)
            with pe.If(more > 0):
                expert_pass(1)


_WEIGHTS = ["x", "w_in", "w_out", "ffn_w_gate", "ffn_w_up", "ffn_w_down", "moe_w_gate", "moe_w_up", "moe_w_down"]


def small_params(i):
    def cols(v):
        return v.reshape(-1, P).T

    def both(a, b):
        return np.concatenate([a, b], 0).reshape(P, -1)

    def rows(v):
        return np.broadcast_to(v.reshape(1, -1), (P, v.size))

    layers = []
    for l in range(2):
        br, bi = (i[n][l].transpose(1, 0, 2).reshape(STATES, -1) for n in ("ssm_b_re", "ssm_b_im"))
        cr, ci = (i[n][l].transpose(2, 0, 1).reshape(STATES, -1) for n in ("ssm_c_re", "ssm_c_im"))
        skip = np.zeros((P, GROUPS, GC), np.float32)
        for c in range(GC):
            skip[c, :, c] = i["ssm_d"][l].reshape(GROUPS, GC)[:, c]
        layers.append(np.concatenate([
            cols(i["norm1_g"][l]), cols(i["norm2_g"][l]), cols(i["ret_gn_g"][l]), cols(i["ssm_glu_b"][l]),
            rows(i["q_norm_g"][l]), rows(i["k_norm_g"][l]),
            both(i["ssm_a_re"][l].T, i["ssm_a_re"][l].T), both(i["ssm_a_im"][l].T, i["ssm_a_im"][l].T),
            rows(i["ssm_log_dt"][l]), both(br, bi), both(bi, br), both(cr, ci), both(ci, cr),
            i["ssm_glu_w"][l].reshape(2, P, 256).transpose(1, 0, 2).reshape(P, -1), skip.reshape(P, -1),
        ], 1))
    return np.ascontiguousarray(np.stack(layers, 1), dtype=np.float32)


def kernel(**inputs):
    import concourse.bacc as _bacc
    from concourse.bass_utils import run_bass_kernel_spmd as _run

    i = {k: np.asarray(v) for k, v in inputs.items()}
    nc = _bacc.Bacc("TRN2", target_bir_lowering=False, num_devices=1)
    arrays = {n: np.ascontiguousarray(i[n]) for n in _WEIGHTS}
    arrays["consts"] = constants()
    arrays["params"] = small_params(i)
    arrays["router"] = np.ascontiguousarray(
        i["moe_router"][0].reshape(KC, P, NE).transpose(1, 0, 2))
    args = {n: nc.dram_tensor(f"in_{n}", v.shape, F32, kind="ExternalInput").ap() for n, v in arrays.items()}
    out = nc.dram_tensor("out_0", (1, SEQ, D), F32, kind="ExternalOutput").ap()
    trunk(nc, args, out)
    r = _run(nc, [{f"in_{n}": v for n, v in arrays.items()}], core_ids=[0])
    return r.results[0]["out_0"]
```

```python
from contextlib import ExitStack

import numpy as np

import concourse.bass as bass
from concourse import mybir

F32 = mybir.dt.float32
F32R = mybir.dt.float32r
I32 = mybir.dt.int32
ALU = mybir.AluOpType
ACT = mybir.ActivationFunctionType
AX_X = mybir.AxisListType.X

P = 128
SEQ, D = 256, 1024
NT = SEQ // P
KC = D // P
HD = 64
HEADS = 4
RV = 128
GROUPS, GC, STATES = 16, 16, 64
CH = 8
NCH = SEQ // CH
EPS = 1e-6
BLK = 512
PROJ = 2304
NE = 8
QC, VC, QR, KR, VR, GR = 0, 512, 768, 1024, 1280, 1792

CO = {}
_at = 0
for _name, _n in (("ident", 128), ("swap", 128), ("tri", 128), ("ones", 128), ("iota", 128),
                  ("cosA", 16), ("sinA", 16), ("cosR", 64), ("sinR", 64), ("count", 384), ("mask", 384),
                  ("decay", 4 * 384), ("sg", 2), ("rev", 8), ("mhalf", 16), ("mone", 16), ("euler", 16)):
    CO[_name] = (_at, _n)
    _at += _n
NCONST = _at
PO = {}
_at = 0
for _name, _n in (("g1", 8), ("g2", 8), ("gn", 4), ("glub", 2), ("qkg", 128), ("are", 16), ("aim", 16),
                  ("logdt", 16), ("b1", 256), ("b2", 256), ("c1", 256), ("c2", 256), ("gluw", 512),
                  ("dskip", 256)):
    PO[_name] = (_at, _n)
    _at += _n
NPAR = _at


def constants():
    f = np.float32
    c = np.zeros((P, NCONST), f)

    def put(name, a):
        o, n = CO[name]
        c[:, o:o + n] = np.asarray(a, f).reshape(P, n)

    p = np.arange(P)
    put("ident", np.eye(P))
    put("swap", np.eye(P)[(p + 64) % P])
    put("tri", p[:, None] < p[None, :])
    put("ones", np.ones((P, P)))
    put("iota", np.tile(p, (P, 1)))
    pos = np.arange(SEQ, dtype=f)
    for nm, theta, rot in (("A", 500000.0, 16), ("R", 10000.0, 64)):
        half = rot // 2
        inv = np.power(f(theta), -np.arange(half, dtype=f) * f(2.0) / f(rot)).astype(f)
        ang = (pos[:, None] * inv[None, :]).astype(f)
        put("cos" + nm, np.cos(ang).reshape(NT, P, half).transpose(1, 0, 2))
        put("sin" + nm, np.sin(ang).reshape(NT, P, half).transpose(1, 0, 2))
    i, j = np.arange(SEQ)[:, None], np.arange(SEQ)[None, :]
    d = i - j
    cnt = sum(((d >= 0) & (d <= 128 * r) & (d % r == 0)).astype(f) for r in (1, 4, 16))
    msk = np.where(cnt > 0, 0.0, -1e30).astype(f)
    for nm, a in (("count", cnt), ("mask", msk)):
        put(nm, np.concatenate([a[0:P, 0:P], a[P:, :]], 1))
    lg = np.log1p(-np.exp2(-5.0 - np.arange(HEADS)))
    dec = np.where(d >= 0, np.exp(lg[:, None, None] * np.maximum(d, 0)), 0.0) * HD ** -0.5
    dT = dec.transpose(0, 2, 1)
    put("decay", np.stack([np.concatenate([dT[h, 0:P, :], dT[h, P:, P:]], 1) for h in range(HEADS)], 1))
    put("sg", np.stack([np.where(p < 64, -1, 1), np.where(p < 64, 1, -1)], 1))
    put("rev", np.tile(np.arange(NE, 0, -1), (P, 1)))
    put("mhalf", np.full((P, 16), -0.5))
    put("mone", np.full((P, 16), -1.0))
    put("euler", np.full((P, 16), np.e))
    return c


def ring_order():
    def mixer(l):
        return ([("in", l, b, kh) for b in (4, 0, 1, 2, 3) for kh in range(2)]
                + [("out", l, n, kh) for kh in range(2) for n in range(2)])
    return mixer(0), mixer(1)


def trunk(nc, a, out):
    x, w_in, w_out = a["x"], a["w_in"], a["w_out"]
    w_gate, w_up, w_down = a["ffn_w_gate"], a["ffn_w_up"], a["ffn_w_down"]
    m_gate, m_up, m_down = a["moe_w_gate"], a["moe_w_up"], a["moe_w_down"]
    FU = w_gate.shape[2] // 256
    MU = m_gate.shape[3] // BLK
    assert FU % 2 == 1 and MU % 2 == 1 and FU >= 3 and MU >= 5
    PAIRS = (FU - 1) // 2
    ET = 6 * MU
    RA, RM = 6, 7
    RS = 3
    assert ET % RM == 0 and ET % RS == 0
    ER = ET // RM
    MIX = 14
    FFN_TILES = 3 * FU
    BASE = [0, MIX + FFN_TILES]

    gu_at = lambda u: MIX + 2 if u == 0 else MIX + 3 * u + 1
    d_at = lambda u: MIX + 3 * u + (5 if u < FU - 1 else 3)
    mgu_at = lambda u: 4 if u == 0 else 6 * u + 2
    md_at = lambda u: 6 * u + (10 if u < MU - 1 else 6)

    with ExitStack() as ctx:
        def sem(name):
            return ctx.enter_context(nc.semaphore(name))

        psum = ctx.enter_context(nc.psum_tensor("psum", [P, 8, BLK], F32))
        PB = [psum[:, b, :] for b in range(8)]
        top = [0]
        ARENA = 53152
        base = -(-nc.sbuf_base // 64) * 64
        flag = nc.alloc_sbuf_tensor_at("flag", [P, 2], I32, offset=base + 4 * ARENA)
        scr_u = nc.dram_tensor("scratch_u", [256, 256], F32, kind="Internal").ap()
        scr_y = nc.dram_tensor("scratch_y", [256, 256], F32, kind="Internal").ap()

        def take(name, *shape, at=None, dtype=F32):
            n = int(np.prod(shape))
            if at is None:
                at = top[0]
                top[0] += -(-n // 8) * 8
            assert at + n <= ARENA, (name, at + n, ARENA)
            t = nc.alloc_sbuf_tensor_at(name, [P, *shape], dtype, offset=base + 4 * at)
            return t[tuple(slice(None) for _ in range(len(shape) + 1))]

        def take_r(name, *shape):
            return take(name, *shape, dtype=F32R)

        h = take("h", NT, D)
        cst = take("cst", NCONST)
        par = take("par", 2, NPAR)
        router = take("router", KC, NE)
        xs = take("xs", NT, D)
        xnT = take("xnT", KC, SEQ)
        st = take("st", 256)
        ringA_at = top[0]
        ringA = [take(f"ringA{k}", 2048) for k in range(RA)]
        mix_at = top[0]
        proj = take("proj", NT, PROJ)
        qk_at = top[0]
        qkT = take("qkT", 8, SEQ)
        top[0] += 256
        vt = take("vt", GROUPS, CH + 1, GC, at=qk_at)
        wt = take("wt", GROUPS, CH, GC, at=qk_at)
        E_at = top[0]
        E = take("E", HEADS, 384)
        PT = take("PT", HEADS, 384)
        AT = take("AT", HEADS, 384)
        Wpre = take("Wpre", GROUPS, CH, GC, at=E_at)
        Kall = take("Kall", GROUPS, CH, GC, at=E_at + 2048)
        uTr = take("uTr", 2, CH, NCH)
        U = take("U", GROUPS, NCH)
        xsb = take("xsb", GROUPS, NCH)
        t1 = take("t1", GROUPS, NCH)
        t2 = take("t2", GROUPS, NCH)
        G = take("G", GROUPS, NCH)
        Hs = take("Hs", GROUPS, NCH + 1)
        zT = take("zT", 2, CH, NCH)
        sgm = take("sgm", 2, CH, NCH)
        cosT = take("cosT", GROUPS, NCH)
        sinT = take("sinT", GROUPS, NCH)
        mg = take("mg", GROUPS, NCH)
        Mt = take("Mt", GROUPS, CH, GC)
        Wl = take("Wl", GROUPS, P)
        V = take("V", GROUPS, CH + 1, GC)
        Tre = take("Tre", 32, CH + 1)
        Tim = take("Tim", 32, CH + 1)
        ptmp = take("ptmp", 4, 256)
        pv = take("pv", 24, GROUPS)
        prs = take("prs", GROUPS, CH + 1)
        tims = take("tims", GROUPS, CH)
        Bb1 = take("Bb1", GROUPS, GC)
        Bb2 = take("Bb2", GROUPS, GC)
        rtA = xs[:, 1, 512:1024].rearrange("p (a b) -> p a b", a=4)
        fsil = [take(f"fsil{i}", BLK, at=mix_at + 512 * i) for i in range(2)]
        fhT = [take(f"fhT{i}", 2, SEQ, at=mix_at + 1024 + 512 * i) for i in range(2)]
        moe_at = mix_at + (RM - RA) * 2048
        ringM = ringA + [take(f"ringM{i}", 2048, at=mix_at + 2048 * i) for i in range(RM - RA)]
        top[0] = -(-moe_at // 16) * 16
        whi, wlo = take_r("whi", RS, 2048), take_r("wlo", RS, 2048)
        xgh, xgl = take_r("xgh", KC, P), take_r("xgl", KC, P)
        mhh, mhl = take_r("mhh", 2, 4, P), take_r("mhl", 2, 4, P)
        PH = take("PH", NT, NE + 1, P)
        PG_at = top[0]
        PG = take("PG", NT, NE, P)
        PTg = take("PTg", NE, SEQ)
        PTcur = take("PTcur", SEQ)
        msil = [take(f"msil{i}", BLK, at=PG_at + BLK * i) for i in range(2)]
        mh = take("mh", 2, BLK, at=PG_at + 2 * BLK)
        yb = take("yb", D)
        rt = take("rt", 320)
        assert top[0] <= ARENA, top[0]

        def C(name, *shape):
            o, n = CO[name]
            v = cst[:, o:o + n]
            if len(shape) > 1:
                names = "abcd"[:len(shape)]
                v = v.rearrange(f"p ({' '.join(names)}) -> p {' '.join(names)}",
                                **{k: s for k, s in zip(names, shape)})
            return v

        def R(l, name, *shape):
            o, n = PO[name]
            v = par[:, l, o:o + n]
            if len(shape) > 1:
                names = "abcd"[:len(shape)]
                v = v.rearrange(f"p ({' '.join(names)}) -> p {' '.join(names)}",
                                **{k: s for k, s in zip(names, shape)})
            return v

        ident = C("ident")

        x_in, cst_in, par_in, router_in = sem("x_in"), sem("cst_in"), sem("par_in"), sem("router_in")
        tile_in = [sem(f"tile_in{s}") for s in range(RA)]
        tile_used = sem("tile_used")
        mtile_in = [sem(f"mtile_in{s}") for s in range(RM)]
        mtile_used = sem("mtile_used")
        ss_ready, rstd_ready, xs_ready = sem("ss_ready"), sem("rstd_ready"), sem("xs_ready")
        nT_ps, xnT_ready = sem("nT_ps"), sem("xnT_ready")
        proj_ready, u_ready = sem("proj_ready"), sem("u_ready")
        u_out, u_in = sem("u_out"), sem("u_in")
        sincos_arg, trig_ready, poles_ready, prep_ready = (
            sem("sincos_arg"), sem("trig_ready"), sem("poles_ready"), sem("prep_ready"))
        prepT_ps, prepT_ev, K_raw, K_ready, toep_in = (
            sem("prepT_ps"), sem("prepT_ev"), sem("K_raw"), sem("K_ready"), sem("toep_in"))
        x_ps, x_sb, scan_ready, hs_ready, y_ps = (
            sem("x_ps"), sem("x_sb"), sem("scan_ready"), sem("hs_ready"), sem("y_ps"))
        perm_ps, gelu_ready, y_out, z_in = sem("perm_ps"), sem("gelu_ready"), sem("y_out"), sem("z_in")
        glu_ps, sgm_ready, mixS_ready = sem("glu_ps"), sem("sgm_ready"), sem("mixS_ready")
        sq_ready, ssq_ready, rq_ready = sem("sq_ready"), sem("ssq_ready"), sem("rq_ready")
        qk_ready, qr_ready, qkT_ps, qkT_ready = sem("qk_ready"), sem("qr_ready"), sem("qkT_ps"), sem("qkT_ready")
        s_ps, s_masked, negm_ready, exp_ready, p_ready = (
            sem("s_ps"), sem("s_masked"), sem("negm_ready"), sem("exp_ready"), sem("p_ready"))
        pT_ps, PT_ready, att_ps = sem("pT_ps"), sem("PT_ready"), sem("att_ps")
        rs_ps, AT_ready, ry_ps = sem("rs_ps"), sem("AT_ready"), sem("ry_ps")
        var_ready, rvar_ready, mixed_ready = sem("var_ready"), sem("rvar_ready"), sem("mixed_ready")
        mT_ps, mixT_ready, h1_ready = sem("mT_ps"), sem("mixT_ready"), sem("h1_ready")
        sil_ready, hT_ready, h2_ready = sem("sil_ready"), sem("hT_ready"), sem("h2_ready")
        lg_ps, lgm_ready, lge_ready, mask_ready, pos_ps, hot_ready, flag_ready = (
            sem("lg_ps"), sem("lgm_ready"), sem("lge_ready"), sem("mask_ready"), sem("pos_ps"),
            sem("hot_ready"), sem("flag_ready"))
        gT_ps, PTg_ready, first_y = sem("gT_ps"), sem("PTg_ready"), sem("first_y")
        xg_ps, xgh_ready, xgl_ready = sem("xg_ps"), sem("xgh_ready"), sem("xgl_ready")
        whi_ready, wlo_ready = sem("whi_ready"), sem("wlo_ready")
        msil_ready, mh_ready, mhT_ps, mhh_ready, mhl_ready = (
            sem("msil_ready"), sem("mh_ready"), sem("mhT_ps"), sem("mhh_ready"), sem("mhl_ready"))
        yA_ready, yD_ready, sc_ps, sc_done, out_ready, out_done = (
            sem("yA_ready"), sem("yD_ready"), sem("sc_ps"), sem("sc_done"), sem("out_ready"), sem("out_done"))
        dve_step, act_step, pool_step, pool_z = sem("dve_step"), sem("act_step"), sem("pool_step"), sem("pool_z")

        block = ctx.enter_context(nc.Block())

        class Steps:

            def __init__(self, eng, s):
                self.eng, self.s, self.n = eng, s, 0

            def add(self, ins):
                ins.then_inc(self.s, 1)
                self.n += 1

            def wait(self):
                self.eng.wait_ge(self.s, self.n)

            def link(self, ins):
                self.add(ins)
                self.wait()

        @block.sync
        def _(sp):
            sp.dma_start(h[:, :, :], x[0].rearrange("(t p) d -> p t d", p=P)).then_inc(x_in, 16)
            sp.dma_start(cst, a["consts"]).then_inc(cst_in, 16)
            sp.dma_start(par[:, :, :], a["params"]).then_inc(par_in, 16)
            sp.dma_start(router, a["router"]).then_inc(router_in, 16)

            def tile(k, dst_shape, src):
                if k >= RA:
                    sp.wait_ge(tile_used, k - RA + 1)
                v = ringA[k % RA].rearrange("p (c n) -> p c n", c=dst_shape)
                sp.dma_start(v, src).then_inc(tile_in[k % RA], 16)

            def rows(w, r0, nchunk, c0, nc_):
                return w[r0 * P:(r0 + nchunk) * P, c0:c0 + nc_].rearrange("(c p) n -> p c n", p=P)

            def mixer_tiles(l):
                for k, (kind, _, b, kh) in enumerate(ring_order()[l]):
                    w = w_in if kind == "in" else w_out
                    tile(BASE[l] + k, 4, rows(w[l], 4 * kh, 4, b * BLK, BLK))

            def ffn_unit(k, u, ud):
                yield k, KC, w_gate, u
                yield k + 1, KC, w_up, u
                yield k + 2, 2, w_down, ud

            mixer_tiles(0)
            k0 = MIX
            tile(k0, KC, rows(w_gate[0], 0, KC, 0, 256))
            tile(k0 + 1, KC, rows(w_up[0], 0, KC, 0, 256))
            with sp.Fori(0, PAIRS) as i:
                for j in range(2):
                    for m, w in ((0, w_gate), (1, w_up), (2, w_down)):
                        kk = k0 + 2 + 3 * j + m
                        sp.wait_ge(tile_used, i * 6 + (kk - RA + 1))
                        v = ringA[kk % RA].rearrange("p (c n) -> p c n", c=2 if m == 2 else KC)
                        if m == 2:
                            src = w[0].rearrange("(u c p) n -> u p c n", c=2, p=P)[i * 2 + j]
                        else:
                            src = w[0].rearrange("(c p) (u n) -> u p c n", p=P, n=256)[i * 2 + j + 1]
                        sp.dma_start(v, src).then_inc(tile_in[kk % RA], 16)
            tile(k0 + FFN_TILES - 1, 2, w_down[0].rearrange("(u c p) n -> u p c n", c=2, p=P)[FU - 1])
            mixer_tiles(1)

            def mtile(m, e):
                if m < 4:
                    kind, u, half = "gu"[m // 2], 0, m % 2
                elif m >= ET - 2:
                    kind, u, half = "d", MU - 1, m % 2
                else:
                    r = (m - 4) % 6
                    u = (m - 4) // 6 + 1
                    kind, half = "gud"[r // 2], r % 2
                    if kind == "d":
                        u -= 1
                if kind == "d":
                    r0 = (4 * u + 2 * half) * P
                    return 2, m_down[0].rearrange("e r n -> e r n")[e, r0:r0 + 2 * P, :].rearrange(
                        "(c p) n -> p c n", p=P)
                w = m_gate if kind == "g" else m_up
                return 4, w[0][e, half * 4 * P:(half + 1) * 4 * P, u * BLK:(u + 1) * BLK].rearrange(
                    "(c p) n -> p c n", p=P)

            def mload(m, e):
                c, src = mtile(m, e)
                sp.dma_start(ringM[m % RM].rearrange("p (c n) -> p c n", c=c), src).then_inc(mtile_in[m % RM], 16)

            def expert_pass(ps):
                used0 = ps * NE * ET
                for m in range(RM):
                    if ps == 0 and m < RA:
                        last = max(k for k in range(BASE[1] + MIX) if k % RA == m)
                        sp.wait_ge(tile_used, last + 1)
                    elif ps == 0:
                        sp.wait_ge(h1_ready, 4 * 2)
                    else:
                        sp.wait_ge(wlo_ready, used0 - RM + m + 1)
                    mload(m, 0)
                with sp.Fori(0, NE - 1) as e:
                    for m in range(ET):
                        n = m + RM
                        if n != 8:
                            sp.wait_ge(wlo_ready, e * ET + (used0 + m + 1 + (n == 7)))
                        mload(n % ET, e + n // ET)
                for m in range(ET - RM):
                    sp.wait_ge(wlo_ready, (NE - 1) * ET + used0 + m + 1)
                    mload(m + RM, NE - 1)

            expert_pass(0)
            sp.wait_ge(flag_ready, 1)
            more = sp.value_load(flag[0:1, 0:1], min_val=0, max_val=1)
            with sp.If(more > 0):
                expert_pass(1)
            sp.wait_ge(out_ready, 1)
            sp.dma_start(out[0].rearrange("(t p) d -> p t d", p=P), h[:, :, :]).then_inc(out_done, 16)
            sp.wait_ge(out_done, 16)

        def s5_setup(l, eng, lk):
            def tt(o, x0, x1, op):
                lk.add(eng.tensor_tensor(o, x0, x1, op))

            def ts(o, x0, s1, s2=None, o0=ALU.mult, o1=None):
                lk.add(eng.tensor_scalar(o, x0, s1, s2, o0, o1) if o1 is not None
                       else eng.tensor_scalar(o, x0, s1, None, o0))

            sg, sg2 = C("sg")[:, 0:1], C("sg")[:, 1:2]
            S = lambda n: pv[:, n, :]
            mag, sn, cs, rden = S(0), S(1), S(2), S(3)
            nr, f1, f2, f3, f4, fre, fim, fs, fns = (S(n) for n in range(9, 18))
            are, aim = R(l, "are"), R(l, "aim")
            b1, b2 = R(l, "b1", GROUPS, GC), R(l, "b2", GROUPS, GC)
            c1, c2 = R(l, "c1", GROUPS, GC), R(l, "c2", GROUPS, GC)

            A = Tre[:, 0:16, 1]
            tt(A, mag, cs, ALU.mult)
            tt(Tim[:, 0:16, 1], mag, sn, ALU.mult)
            lk.add(eng.tensor_copy(Tre[:, 16:32, 1], cs))
            lk.add(eng.tensor_copy(Tim[:, 16:32, 1], sn))
            lk.wait()
            ts(nr, A, -1.0, o0=ALU.add)
            lk.wait()
            tt(f1, nr, are, ALU.mult)
            tt(f2, Tim[:, 0:16, 1], aim, ALU.mult)
            tt(f3, Tim[:, 0:16, 1], are, ALU.mult)
            tt(f4, nr, aim, ALU.mult)
            lk.wait()
            tt(f1, f1, f2, ALU.add)
            tt(f3, f3, f4, ALU.subtract)
            lk.wait()
            tt(fre, f1, rden, ALU.mult)
            tt(fim, f3, rden, ALU.mult)
            lk.wait()
            ts(fs, fim, sg)
            ts(fns, fim, sg2)
            lk.wait()
            wide = lambda v: v.unsqueeze(2).to_broadcast([P, GROUPS, GC])
            q1, q2 = ptmp[:, 0, :], ptmp[:, 1, :]
            q1, q2 = (q.rearrange("p (a b) -> p a b", a=GROUPS) for q in (q1, q2))
            tt(Bb1, wide(fre), b1, ALU.mult)
            tt(q1, wide(fs), b2, ALU.mult)
            tt(Bb2, wide(fre), b2, ALU.mult)
            tt(q2, wide(fns), b1, ALU.mult)
            lk.wait()
            tt(Bb1, Bb1, q1, ALU.add)
            tt(Bb2, Bb2, q2, ALU.add)
            lk.wait()

            def powers(re, im, rows, n, cnt):
                b = lambda v: v[:, :, n:n + 1].to_broadcast([P, rows, cnt])
                q = [ptmp[:, k, 0:rows * cnt].rearrange("p (a b) -> p a b", a=rows) for k in range(4)]
                r, i = re[:, :, 1:cnt + 1], im[:, :, 1:cnt + 1]
                tt(q[0], r, b(re), ALU.mult)
                tt(q[1], i, b(im), ALU.mult)
                tt(q[2], r, b(im), ALU.mult)
                tt(q[3], i, b(re), ALU.mult)
                lk.wait()
                tt(re[:, :, n + 1:n + cnt + 1], q[0], q[1], ALU.subtract)
                tt(im[:, :, n + 1:n + cnt + 1], q[2], q[3], ALU.add)
                lk.wait()

            for n in (1, 2, 4):
                powers(Tre, Tim, 32, n, n)
            lk.add(eng.tensor_copy(cosT[:, :, 1], Tre[:, 16:32, CH]))
            lk.add(eng.tensor_copy(sinT[:, :, 1], Tim[:, 16:32, CH]))
            lk.wait()
            for n, cnt in ((1, 1), (2, 2), (4, 4), (8, 8), (16, 15)):
                powers(cosT, sinT, GROUPS, n, cnt)
            ts(sinT, sinT, sg2)
            tt(f1, mag, mag, ALU.mult)
            lk.wait()
            tt(f2, f1, f1, ALU.mult)
            lk.wait()
            tt(f3, f2, f2, ALU.mult)
            lk.wait()
            lk.add(eng.tensor_copy(mg[:, :, 1:NCH], f3.unsqueeze(2).to_broadcast([P, GROUPS, NCH - 1])))
            ts(prs, Tre[:, 0:16, :], sg2)
            ts(tims, Tim[:, 0:16, 0:CH], sg)
            lk.wait()
            b4 = lambda v, n: v.unsqueeze(3).to_broadcast([P, GROUPS, n, GC])
            c4 = lambda v, n: v.unsqueeze(2).to_broadcast([P, GROUPS, n, GC])
            tt(V, b4(prs, CH + 1), c4(c1, CH + 1), ALU.mult)
            tt(vt, b4(Tim[:, 0:16, :], CH + 1), c4(c2, CH + 1), ALU.mult)
            lk.wait()
            tt(V, V, vt, ALU.subtract)
            tt(Wpre, b4(Tre[:, 0:16, 0:CH], CH), c4(Bb1, CH), ALU.mult)
            lk.wait()
            tt(wt, b4(tims, CH), c4(Bb2, CH), ALU.mult)
            lk.wait()
            eng.tensor_tensor(Wpre, Wpre, wt, ALU.add).then_inc(prep_ready, 1)
            eng.wait_ge(prep_ready, l + 1)

        @block.gpsimd
        def _(pool):
            lk = Steps(pool, pool_step)
            g = nc.gpsimd
            g.memset(Mt, 0.0).then_inc(pool_z, 1)
            g.memset(Hs[:, :, 0], 0.0).then_inc(pool_z, 1)
            g.memset(mg[:, :, 0], 0.0).then_inc(pool_z, 1)
            g.memset(Tre[:, :, 0], 1.0).then_inc(pool_z, 1)
            g.memset(Tim[:, :, 0], 0.0).then_inc(pool_z, 1)
            g.memset(cosT[:, :, 0], 1.0).then_inc(pool_z, 1)
            g.memset(sinT[:, :, 0], 0.0).then_inc(pool_z, 1)

            def inv_root(dst, src, n, scale, eps, done, done_by=1):
                lk.link(g.tensor_scalar(src, src, scale, eps, ALU.mult, ALU.add))
                g.tensor_tensor(dst, src, C("mhalf")[:, 0:n], ALU.pow).then_inc(done, done_by)

            def norm_root(n):
                pool.wait_ge(ss_ready, NT * (n + 1))
                inv_root(st[:, 2:4], st[:, 0:2], NT, 1.0 / D, EPS, rstd_ready)

            def poles(l):
                S = lambda n: pv[:, n, :]
                mag, rden, dt, la, th, nn, red, den = S(0), S(3), S(4), S(5), S(6), S(7), S(8), S(18)
                q = S(19)
                are, aim = R(l, "are"), R(l, "aim")
                lk.add(g.tensor_tensor(dt, C("euler"), R(l, "logdt"), ALU.pow))
                lk.add(g.tensor_tensor(den, are, are, ALU.mult))
                lk.add(g.tensor_tensor(q, aim, aim, ALU.mult))
                lk.wait()
                lk.add(g.tensor_tensor(la, are, dt, ALU.mult))
                lk.add(g.tensor_tensor(th, aim, dt, ALU.mult))
                lk.add(g.tensor_tensor(den, den, q, ALU.add))
                lk.wait()
                lk.link(g.tensor_scalar(nn, th, float(1 / (2 * np.pi)), 12582912.0, ALU.mult, ALU.add))
                lk.link(g.tensor_scalar(nn, nn, -12582912.0, None, ALU.add))
                rest = 2 * np.pi
                src = th
                for k in range(3):
                    part = float(np.float32(np.round(rest * 2 ** (7 + 10 * k)) / 2 ** (7 + 10 * k))) if k < 2 \
                        else float(np.float32(rest))
                    rest -= part
                    lk.link(g.tensor_scalar(q, nn, -part, None, ALU.mult))
                    lk.link(g.tensor_tensor(red, src, q, ALU.add))
                    src = red
                g.tensor_scalar(red, red, 3.1415925, -3.1415925, ALU.min, ALU.max).then_inc(sincos_arg, 1)
                lk.add(g.tensor_tensor(mag, C("euler"), la, ALU.pow))
                lk.add(g.tensor_tensor(rden, den, C("mone"), ALU.pow))
                lk.wait()
                pool.wait_ge(trig_ready, 2 * (l + 1))
                cs = S(2)
                lk.link(g.tensor_tensor(cs, cs, cs, ALU.mult))
                g.tensor_scalar(cs, cs, -2.0, 1.0, ALU.mult, ALU.add).then_inc(poles_ready, 1)
                pool.wait_ge(poles_ready, l + 1)

            pool.wait_ge(cst_in, 16)
            norm_root(0)
            pool.wait_ge(par_in, 16)
            pool.wait_ge(pool_z, 7)
            poles(0)
            for l in range(2):
                pool.wait_ge(u_ready, 2 * (l + 1))
                pool.dma_start(scr_u.rearrange("(f p) n -> p f n", p=P),
                               uTr.rearrange("p f s k -> p f (s k)")).then_inc(u_out, 16)
                pool.wait_ge(u_out, 16 * (l + 1))
                for s in range(CH):
                    src = scr_u.rearrange("(g c) (s k) -> s c g k", c=GC, k=NCH)[CH - 1 - s]
                    pool.dma_start(U[GC * s:GC * (s + 1), :, :], src).then_inc(u_in, 16)
                pool.wait_ge(ssq_ready, l + 1)
                inv_root(st[:, 32:48], st[:, 16:32], 16, 1.0 / HD, EPS, rq_ready)
                pool.wait_ge(K_raw, 4 * (l + 1))
                g.tensor_tensor(Kall[0:GC, :, 0, :], Kall[0:GC, :, 0, :], R(l, "dskip", GROUPS, GC)[0:GC],
                                ALU.add).then_inc(K_ready, 1)
                pool.wait_ge(K_ready, l + 1)
                for s in range(CH):
                    pool.dma_start(Mt[GC * s:GC * (s + 1), :, CH - 1 - s:CH, :],
                                   Kall[0:GC, :, 0:s + 1, :]).then_inc(toep_in, 16)
                pool.wait_ge(gelu_ready, l + 1)
                ysb = G
                for t in range(CH):
                    dst = scr_y.rearrange("(g c) (s k) -> s c g k", c=GC, k=NCH)[t]
                    pool.dma_start(dst, ysb[GC * t:GC * (t + 1), :, :]).then_inc(y_out, 16)
                pool.wait_ge(y_out, 16 * CH * (l + 1))
                pool.dma_start(zT.rearrange("p f s k -> p f (s k)"),
                               scr_y.rearrange("(f p) n -> p f n", p=P)).then_inc(z_in, 16)
                pool.wait_ge(var_ready, l + 1)
                inv_root(st[:, 72:80], st[:, 64:72], 8, 1.0, 1e-5, rvar_ready)
                norm_root(2 * l + 1)
                if l == 0:
                    poles(1)
                    s5_setup(1, g, lk)
                    norm_root(2)

        @block.scalar
        def _(act):
            lk = Steps(act, act_step)
            s = nc.scalar

            def norm(n):
                l = n // 2
                for t in range(NT):
                    s.activation(xs[:, t, :], h[:, t, :], ACT.Square, accum_out=st[:, t:t + 1]).then_inc(ss_ready, 1)
                act.wait_ge(rstd_ready, n + 1)
                for t in range(NT):
                    s.activation(xs[:, t, :], h[:, t, :], ACT.Copy, scale=st[:, 2 + t:3 + t]).then_inc(xs_ready, 1)
                for kc in range(KC):
                    if kc % 2 == 0:
                        act.wait_ge(nT_ps, 4 * n + kc // 2 + 1)
                    gain = R(l, "g1" if n % 2 == 0 else "g2")[:, kc:kc + 1]
                    s.activation(xnT[:, kc, :], PB[kc // 2][:, 256 * (kc % 2):256 * (kc % 2) + 256],
                                 ACT.Copy, scale=gain).then_inc(xnT_ready, 1)

            act.wait_ge(x_in, 16)
            act.wait_ge(cst_in, 16)
            act.wait_ge(par_in, 16)

            def trig(l):
                act.wait_ge(sincos_arg, l + 1)
                s.activation(pv[:, 1, :], pv[:, 8, :], ACT.Sin).then_inc(trig_ready, 1)
                s.activation(pv[:, 2, :], pv[:, 8, :], ACT.Sin, scale=0.5).then_inc(trig_ready, 1)

            def blk(l, b):
                idx = {4: 0, 0: 1, 1: 2, 2: 3, 3: 4}[b]
                act.wait_ge(tile_used, BASE[l] + 2 * (idx + 1))
                for t in range(NT):
                    bank = {4: 4, 0: 0, 1: 2, 2: 4, 3: 0}[b] + t
                    if b == 4:
                        s.activation(proj[:, t, 2048:2304], PB[bank][:, 0:256], ACT.Silu).then_inc(proj_ready, 1)
                    elif b == 3:
                        s.activation(proj[:, t, 1536:1792], PB[bank][:, 0:256], ACT.Copy).then_inc(proj_ready, 1)
                        s.activation(proj[:, t, 1792:2048], PB[bank][:, 256:512], ACT.Silu).then_inc(proj_ready, 1)
                    else:
                        s.activation(proj[:, t, b * BLK:(b + 1) * BLK], PB[bank], ACT.Copy).then_inc(proj_ready, 1)

            norm(0)
            trig(0)
            for l in range(2):
                PR = 12 * l
                if l == 1:
                    act.wait_ge(h2_ready, 4)
                    norm(2)
                blk(l, 4)
                blk(l, 0)
                act.wait_ge(proj_ready, PR + 4)
                s.activation(xs[:, :, 0:512], proj[:, :, 0:512], ACT.Square).then_inc(sq_ready, 1)
                blk(l, 1)
                for q in range(4):
                    act.wait_ge(prepT_ps, 8 * l + q + 1)
                    s.activation(Wl[:, 4 * q:4 * q + 4, :].rearrange("p a b -> p (a b)"), PB[6 + q % 2],
                                 ACT.Copy).then_inc(prepT_ev, 1)
                for q in range(4):
                    act.wait_ge(prepT_ps, 8 * l + 4 + q + 1)
                    s.activation(Kall[0:GC, 4 * q:4 * q + 4, :, :].rearrange("p g a b -> p (g a b)"),
                                 PB[6 + q % 2][0:GC, :], ACT.Copy).then_inc(K_raw, 1)
                blk(l, 2)
                for q in range(2):
                    act.wait_ge(qkT_ps, 4 * l + q + 1)
                    s.activation(qkT[:, 2 * q:2 * q + 2, :].rearrange("p a b -> p (a b)"), PB[2 + q],
                                 ACT.Copy).then_inc(qkT_ready, 1)
                blk(l, 3)
                for t in range(NT):
                    for hh in range(HEADS):
                        if t == 0 and hh == 0:
                            act.wait_ge(negm_ready, l + 1)
                        c0, c1 = (0, 128) if t == 0 else (128, 384)
                        s.activation(E[:, hh, c0:c1], E[:, hh, c0:c1], ACT.Exp,
                                     bias=st[:, 88 + 4 * t + hh:89 + 4 * t + hh]).then_inc(exp_ready, 1)
                for q in range(2):
                    act.wait_ge(qkT_ps, 4 * l + 2 + q + 1)
                    s.activation(qkT[:, 4 + 2 * q:6 + 2 * q, :].rearrange("p a b -> p (a b)"), PB[4 + q],
                                 ACT.Copy).then_inc(qkT_ready, 1)
                act.wait_ge(y_ps, l + 1)
                s.activation(G.rearrange("p a b -> p (a b)"), PB[7], ACT.Gelu_apprx_tanh).then_inc(gelu_ready, 1)
                for hh in range(HEADS):
                    act.wait_ge(pT_ps, 4 * l + hh + 1)
                    s.activation(PT[:, hh, :], PB[2 + hh % 2][:, 0:384], ACT.Copy).then_inc(PT_ready, 1)
                for j in range(2):
                    act.wait_ge(glu_ps, l + 1)
                    s.activation(sgm[:, j, :, :].rearrange("p a b -> p (a b)"), PB[6][:, 256 * j:256 * j + 256],
                                 ACT.Sigmoid, bias=R(l, "glub")[:, j:j + 1]).then_inc(sgm_ready, 1)
                for c in range(6):
                    act.wait_ge(mT_ps, 3 * l + c // 2 + 1)
                    src = PB[c // 2][:, 256 * (c % 2):256 * (c % 2) + 256]
                    if c < 2:
                        s.activation(xnT[:, c, :], src, ACT.Copy).then_inc(mixT_ready, 1)
                    else:
                        s.activation(xnT[:, c, :], src, ACT.Copy,
                                     scale=R(l, "gn")[:, c - 2:c - 1]).then_inc(mixT_ready, 1)
                act.wait_ge(h1_ready, 4 * (l + 1))
                norm(2 * l + 1)
                if l == 0:
                    trig(1)

                    def silu(used, p):
                        act.wait_ge(tile_used, used)
                        s.activation(fsil[p], PB[p], ACT.Silu).then_inc(sil_ready, 1)

                    silu(gu_at(0), 0)
                    silu(gu_at(1), 1)
                    with act.Fori(0, PAIRS - 1) as i:
                        for j in range(2):
                            act.wait_ge(hT_ready, i * 2 + (j + 1))
                            silu(i * 6 + gu_at(j + 2), j)
                    act.wait_ge(hT_ready, FU - 2)
                    silu(gu_at(FU - 1), 0)

            act.wait_ge(lgm_ready, 1)
            s.activation(rt[:, 0:16], rt[:, 0:16], ACT.Exp).then_inc(lge_ready, 1)

            def expert_pass(ps):
                n0, k0, G0 = ps * NE * MU, ps * NE * ET, ps * (NE + 1)

                def high(e, mt):
                    if isinstance(e, int) and k0 + e * ET + mt < RS:
                        pass
                    else:
                        act.wait_ge(mtile_used, e * ET + (k0 + mt - RS + 1))
                    act.wait_ge(mtile_in[mt % RM], e * (16 * ER) + 16 * (ps * NE * ER + mt // RM + 1))
                    s.activation(whi[:, mt % RS, :], ringM[mt % RM], ACT.Copy).then_inc(whi_ready, 1)

                def gathered(e):
                    for kc in range(KC):
                        if kc % 4 == 0:
                            act.wait_ge(xg_ps, e * 2 + (2 * G0 + kc // 4 + 1))
                        s.activation(xgh[:, kc, :], PB[1 + 2 * (kc // 4)][:, 128 * (kc % 4):128 * (kc % 4) + 128],
                                     ACT.Copy, scale=R(1, "g2")[:, kc:kc + 1]).then_inc(xgh_ready, 1)

                def silu(e, u):
                    act.wait_ge(mtile_used, e * ET + (k0 + mgu_at(u)))
                    if u >= 2:
                        act.wait_ge(mh_ready, e * MU + (n0 + u - 1))
                    s.activation(msil[u % 2], PB[u % 2], ACT.Silu).then_inc(msil_ready, 1)

                def turned(e, u):
                    act.wait_ge(mhT_ps, e * MU + (n0 + u + 1))
                    s.activation(mhh[:, u % 2, :, :].rearrange("p a b -> p (a b)"), PB[6],
                                 ACT.Copy).then_inc(mhh_ready, 1)

                def expert(e, final):
                    for c in range(ET):
                        if c + RS - 1 < ET or not final:
                            high(e, c + RS - 1)
                        for u in range(MU):
                            if mgu_at(u) == c + 1:
                                silu(e, u)
                            if u and mgu_at(u) - 2 == c + 1:
                                turned(e, u - 1)
                        if c + 1 == mgu_at(MU - 1):
                            gathered(e + 1)
                            turned(e, MU - 1)
                    act.wait_ge(mh_ready, e * MU + (n0 + MU))
                    act.wait_ge(mtile_used, e * ET + (k0 + ET))
                    s.activation(yb[:, 0:BLK], PB[4], ACT.Copy).then_inc(yA_ready, 1)

                for mt in range(RS - 1):
                    high(0, mt)
                for q in range(4):
                    act.wait_ge(gT_ps, 4 * ps + q + 1)
                    s.activation(PTg[:, 2 * q:2 * q + 2, :].rearrange("p a b -> p (a b)"), PB[4 + q],
                                 ACT.Copy).then_inc(PTg_ready, 1)
                gathered(0)
                with act.Fori(0, NE - 1) as e:
                    expert(e, False)
                expert(NE - 1, True)

            act.wait_ge(flag_ready, 1)
            more = act.value_load(flag[0:1, 0:1], min_val=0, max_val=1)
            expert_pass(0)
            with act.If(more > 0):
                expert_pass(1)

        @block.vector
        def _(dve):
            lk = Steps(dve, dve_step)
            v = nc.vector
            dve.wait_ge(par_in, 16)
            dve.wait_ge(cst_in, 16)
            dve.wait_ge(pool_z, 7)
            dve.wait_ge(poles_ready, 1)
            s5_setup(0, v, lk)
            for l in range(2):
                PR = 12 * l
                for f in range(2):
                    dve.wait_ge(tile_used, BASE[l] + 2)
                    if l:
                        dve.wait_ge(u_out, 16 * l)
                    v.tensor_copy(uTr[:, f, :, :].rearrange("p s k -> p k s"),
                                  PB[6 + f][:, 0:256].rearrange("p (k s) -> p k s", s=CH)).then_inc(u_ready, 1)
                dve.wait_ge(sq_ready, l + 1)
                v.tensor_reduce(st[:, 16:32].rearrange("p (t h) -> p t h", t=NT), xs[:, :, 0:512].rearrange("p t (h d) -> p t h d", d=HD),
                                AX_X, ALU.add).then_inc(ssq_ready, 1)
                dve.wait_ge(rq_ready, l + 1)
                rs = st[:, 32:48].rearrange("p (t h) -> p t h", t=NT)
                for t in range(NT):
                    qk = proj[:, t, 0:512].rearrange("p (h d) -> p h d", d=HD)
                    lk.add(v.tensor_tensor(qk, qk, rs[:, t, :].unsqueeze(2).to_broadcast([P, 8, HD]), ALU.mult))
                lk.wait()
                for t in range(NT):
                    qk = proj[:, t, 0:512].rearrange("p (w h d) -> p w h d", w=2, d=HD)
                    gain = R(l, "qkg", 2, HD).unsqueeze(2).to_broadcast([P, 2, HEADS, HD])
                    lk.add(v.tensor_tensor(qk, qk, gain, ALU.mult))
                lk.wait()

                def rope(col, half, cos, sin, tmp, done, val):
                    n = 8 * half
                    for t in range(NT):
                        xx = proj[:, t, col:col + 512].rearrange("p (h d) -> p h d", d=HD)
                        x1, x2 = xx[:, :, 0:half], xx[:, :, half:2 * half]
                        co = cos[:, t, :].unsqueeze(1).to_broadcast([P, 8, half])
                        si = sin[:, t, :].unsqueeze(1).to_broadcast([P, 8, half])
                        q = [tmp[k].rearrange("p (h d) -> p h d", d=half) for k in range(4)]
                        if t:
                            lk.wait()
                        lk.add(v.tensor_tensor(q[0], x1, co, ALU.mult))
                        lk.add(v.tensor_tensor(q[1], x2, si, ALU.mult))
                        lk.add(v.tensor_tensor(q[2], x2, co, ALU.mult))
                        lk.add(v.tensor_tensor(q[3], x1, si, ALU.mult))
                        lk.wait()
                        v.tensor_tensor(x1, q[0], q[1], ALU.subtract).then_inc(done, 1)
                        v.tensor_tensor(x2, q[2], q[3], ALU.add).then_inc(done, 1)
                        dve.wait_ge(done, val + 2 * t + 2)

                rope(QC, 8, C("cosA", NT, 8), C("sinA", NT, 8),
                     [rtA[:, k, 0:64] for k in range(4)], qk_ready, 4 * l)

                flat = lambda w: w.rearrange("p a b -> p (a b)")
                dve.wait_ge(x_ps, l + 1)
                v.tensor_copy(flat(xsb), PB[6]).then_inc(x_sb, 1)
                dve.wait_ge(x_sb, l + 1)
                lk.add(v.tensor_tensor(flat(t1), flat(xsb), flat(cosT), ALU.mult))
                dve.wait_ge(perm_ps, 2 * l + 1)
                lk.add(v.tensor_tensor(flat(t2), PB[7], flat(sinT), ALU.mult))
                lk.wait()
                lk.link(v.tensor_tensor(flat(t1), flat(t1), flat(t2), ALU.add))
                if l:
                    dve.wait_ge(y_out, 16 * CH * l)
                v.tensor_tensor_scan(flat(G), flat(mg), flat(t1), 0.0, ALU.mult, ALU.add).then_inc(scan_ready, 1)
                dve.wait_ge(scan_ready, l + 1)
                dve.wait_ge(proj_ready, PR + 8)
                rope(QR, 32, C("cosR", NT, 32), C("sinR", NT, 32),
                     [xs[:, 0, 256 * k:256 * k + 256] for k in range(4)], qr_ready, 4 * l)
                lk.add(v.tensor_tensor(flat(t1), flat(G), flat(cosT), ALU.mult))
                dve.wait_ge(perm_ps, 2 * l + 2)
                lk.add(v.tensor_tensor(flat(t2), PB[6], flat(sinT), ALU.mult))
                lk.wait()
                v.tensor_tensor(Hs[:, :, 1:NCH + 1], t1, t2, ALU.subtract).then_inc(hs_ready, 1)
                for hh in range(HEADS):
                    dve.wait_ge(s_ps, 4 * l + hh + 1)
                    if hh == 0:
                        dve.wait_ge(toep_in, 16 * CH * (l + 1))
                    v.scalar_tensor_tensor(E[:, hh, :], PB[hh][:, 0:384], HD ** -0.5, C("mask"),
                                           ALU.mult, ALU.add).then_inc(s_masked, 1)
                dve.wait_ge(s_masked, 4 * (l + 1))
                lk.add(v.tensor_reduce(st[:, 80:84], E[:, :, 0:128], AX_X, ALU.max))
                lk.add(v.tensor_reduce(st[:, 84:88], E[:, :, 128:384], AX_X, ALU.max))
                lk.wait()
                v.tensor_scalar(st[:, 88:96], st[:, 80:88], -1.0, None, ALU.mult).then_inc(negm_ready, 1)
                for hh in range(2):
                    dve.wait_ge(rs_ps, 4 * l + hh + 1)
                    v.tensor_tensor(AT[:, hh, :], PB[4 + hh][:, 0:384], C("decay", 4, 384)[:, hh, :],
                                    ALU.mult).then_inc(AT_ready, 1)
                dve.wait_ge(exp_ready, 8 * (l + 1))
                v.tensor_tensor(E, E, C("count").unsqueeze(1).to_broadcast([P, HEADS, 384]),
                                ALU.mult).then_inc(p_ready, 1)
                for hh in range(2, 4):
                    dve.wait_ge(rs_ps, 4 * l + hh + 1)
                    v.tensor_tensor(AT[:, hh, :], PB[hh - 2][:, 0:384], C("decay", 4, 384)[:, hh, :],
                                    ALU.mult).then_inc(AT_ready, 1)
                dve.wait_ge(p_ready, l + 1)
                lk.add(v.tensor_reduce(st[:, 96:100], E[:, :, 0:128], AX_X, ALU.add))
                lk.add(v.tensor_reduce(st[:, 100:104], E[:, :, 128:384], AX_X, ALU.add))
                lk.wait()
                lk.link(v.reciprocal(st[:, 104:112], st[:, 96:104]))
                mv = st[:, 48:64].rearrange("p (n c) -> p n c", c=2)
                for t in range(NT):
                    dve.wait_ge(ry_ps, 2 * l + t + 1)
                    for hh in range(HEADS):
                        lk.add(v.bn_stats(st[:, 112 + 6 * (4 * t + hh):118 + 6 * (4 * t + hh)],
                                          PB[4 + t][:, 128 * hh:128 * hh + 128]))
                lk.wait()
                for n in range(8):
                    lk.add(v.bn_aggr(mv[:, n, :], st[:, 112 + 6 * n:118 + 6 * n]))
                lk.wait()
                v.tensor_copy(st[:, 64:72], mv[:, :, 1]).then_inc(var_ready, 1)
                dve.wait_ge(att_ps, l + 1)
                rl = st[:, 104:112].rearrange("p (t h) -> p t h", t=NT)
                for t in range(NT):
                    v.tensor_tensor(xs[:, t, 0:256].rearrange("p (h d) -> p h d", d=HD),
                                    PB[7][:, 256 * t:256 * t + 256].rearrange("p (h d) -> p h d", d=HD),
                                    rl[:, t, :].unsqueeze(2).to_broadcast([P, HEADS, HD]),
                                    ALU.mult).then_inc(mixed_ready, 1)
                dve.wait_ge(proj_ready, PR + 12)
                for t in range(NT):
                    for hh in range(HEADS):
                        gcol = GR + 128 * hh
                        lk.add(v.scalar_tensor_tensor(xs[:, t, 256 + 128 * hh:384 + 128 * hh],
                                                      PB[4 + t][:, 128 * hh:128 * hh + 128],
                                                      mv[:, 4 * t + hh, 0:1], proj[:, t, gcol:gcol + 128],
                                                      ALU.subtract, ALU.mult))
                lk.wait()
                dve.wait_ge(rvar_ready, l + 1)
                rv = st[:, 72:80].rearrange("p (t h) -> p t h", t=NT)
                for t in range(NT):
                    z = xs[:, t, 256:768].rearrange("p (h d) -> p h d", d=RV)
                    v.tensor_tensor(z, z, rv[:, t, :].unsqueeze(2).to_broadcast([P, HEADS, RV]),
                                    ALU.mult).then_inc(mixed_ready, 1)
                dve.wait_ge(sgm_ready, 2 * (l + 1))
                dve.wait_ge(z_in, 16 * (l + 1))
                for j in range(2):
                    v.tensor_tensor(xnT[:, 6 + j, :].rearrange("p (k s) -> p s k", s=CH), zT[:, j, :, :],
                                    sgm[:, j, :, :], ALU.mult).then_inc(mixS_ready, 1)
                for n in range(2):
                    dve.wait_ge(tile_used, BASE[l] + MIX - 1 + n)
                    for t in range(NT):
                        hn = h[:, t, n * BLK:(n + 1) * BLK]
                        v.tensor_tensor(hn, hn, PB[4 + 2 * n + t], ALU.add).then_inc(h1_ready, 1)
                if l == 0:
                    def product(val, p):
                        dve.wait_ge(sil_ready, val)
                        v.tensor_tensor(fhT[p].rearrange("p a b -> p (a b)"), fsil[p], PB[2 + p],
                                        ALU.mult).then_inc(hT_ready, 1)

                    product(1, 0)
                    product(2, 1)
                    with dve.Fori(0, PAIRS - 1) as i:
                        for j in range(2):
                            dve.wait_ge(tile_used, i * 6 + d_at(j))
                            product(i * 2 + (j + 3), j)
                    dve.wait_ge(tile_used, d_at(FU - 3))
                    product(FU, 0)
                    dve.wait_ge(h1_ready, 4)
                    dve.wait_ge(tile_used, d_at(FU - 1))
                    for n in range(2):
                        for t in range(NT):
                            hn = h[:, t, n * BLK:(n + 1) * BLK]
                            v.tensor_tensor(hn, hn, PB[4 + 2 * n + t], ALU.add).then_inc(h2_ready, 1)

            lg = rt[:, 0:16].rearrange("p (t e) -> p t e", t=NT)
            pr = lg
            S2 = lambda k: rt[:, 16 + 2 * k:18 + 2 * k]
            S16 = lambda k: rt[:, 48 + 16 * k:64 + 16 * k].rearrange("p (t e) -> p t e", t=NT)
            e8 = lambda w: w.unsqueeze(2).to_broadcast([P, NT, NE])
            rev = C("rev").unsqueeze(1).to_broadcast([P, NT, NE])
            dve.wait_ge(lg_ps, 1)
            lk.link(v.tensor_reduce(S2(0), PB[4][:, 0:16].rearrange("p (t e) -> p t e", t=NT), AX_X, ALU.max))
            v.tensor_tensor(lg, PB[4][:, 0:16].rearrange("p (t e) -> p t e", t=NT), e8(S2(0)),
                            ALU.subtract).then_inc(lgm_ready, 1)
            dve.wait_ge(lge_ready, 1)
            lk.link(v.tensor_reduce(S2(1), lg, AX_X, ALU.add))
            lk.link(v.reciprocal(S2(2), S2(1)))
            lk.link(v.tensor_tensor(pr, lg, e8(S2(2)), ALU.mult))

            def best(src, top_, one, tmp, k):
                lk.link(v.tensor_reduce(top_, src, AX_X, ALU.max))
                lk.link(v.tensor_tensor(tmp, src, e8(top_), ALU.is_ge))
                lk.link(v.tensor_tensor(tmp, tmp, rev, ALU.mult))
                lk.link(v.tensor_reduce(S2(k), tmp, AX_X, ALU.max))
                lk.link(v.tensor_tensor(one, tmp, e8(S2(k)), ALU.is_ge))

            best(pr, S2(3), S16(0), S16(1), 4)
            lk.link(v.scalar_tensor_tensor(S16(2), S16(0), -2.0, pr, ALU.mult, ALU.add))
            best(S16(2), S2(5), S16(3), S16(1), 6)
            mask = S16(4)
            v.tensor_tensor(mask, S16(0), S16(3), ALU.add).then_inc(mask_ready, 1)
            lk.link(v.tensor_tensor(S2(7), S2(3), S2(5), ALU.add))
            lk.link(v.reciprocal(S2(8), S2(7)))
            lk.add(v.tensor_tensor(S2(9), S2(3), S2(8), ALU.mult))
            lk.add(v.tensor_tensor(S2(10), S2(5), S2(8), ALU.mult))
            lk.wait()
            gate = S16(5)
            lk.add(v.tensor_tensor(gate, S16(0), e8(S2(9)), ALU.mult))
            lk.add(v.tensor_tensor(S16(6), S16(3), e8(S2(10)), ALU.mult))
            lk.wait()
            lk.link(v.tensor_tensor(gate, gate, S16(6), ALU.add))
            slot = S16(7)
            dve.wait_ge(mask_ready, 1)
            dve.wait_ge(pos_ps, 1)
            lk.link(v.scalar_tensor_tensor(slot, PB[5][:, 0:16].rearrange("p (t e) -> p t e", t=NT), 1.0, mask,
                                           ALU.add, ALU.mult))
            lk.link(v.tensor_scalar(slot, slot, -1.0, None, ALU.add))
            lk.link(v.tensor_reduce(S2(11)[:, 0:1], PB[5][:, 16:24], AX_X, ALU.max))
            v.tensor_scalar(flag[:, 0:1], S2(11)[:, 0:1], float(P), None, ALU.is_gt).then_inc(flag_ready, 1)
            v.memset(PH[:, :, NE, :], 0.0).then_inc(first_y, 1)

            def expert_pass(ps):
                if ps:
                    lk.link(v.tensor_scalar(slot, slot, -float(P), None, ALU.add))
                for e in range(NE):
                    for t in range(NT):
                        v.tensor_scalar(PH[:, t, e, :], C("iota"), slot[:, t, e:e + 1], None,
                                        ALU.is_equal).then_inc(hot_ready, 1)
                        v.tensor_scalar(PG[:, t, e, :], C("iota"), slot[:, t, e:e + 1], gate[:, t, e:e + 1],
                                        ALU.is_equal, ALU.mult).then_inc(hot_ready, 1)
                v.memset(yb[:, 0:BLK], 0.0).then_inc(yA_ready, 1)
                v.memset(yb[:, BLK:D], 0.0).then_inc(yD_ready, 1)
                v.memset(PTcur, 0.0).then_inc(yD_ready, 1)
                n0, k0, G0 = ps * NE * MU, ps * NE * ET, ps * (NE + 1)
                s0 = 4 * G0

                def low(e, mt):
                    dve.wait_ge(whi_ready, e * ET + (k0 + mt + 1))
                    v.tensor_tensor(wlo[:, mt % RS, :], ringM[mt % RM], whi[:, mt % RS, :].bitcast(F32),
                                    ALU.subtract).then_inc(wlo_ready, 1)

                def gathered(e):
                    for kc in range(KC):
                        if kc % 4 == 0:
                            dve.wait_ge(xgh_ready, e * KC + (KC * G0 + kc + 4))
                        v.scalar_tensor_tensor(xgl[:, kc, :], PB[1 + 2 * (kc // 4)][:, 128 * (kc % 4):128 * (kc % 4) + 128],
                                               R(1, "g2")[:, kc:kc + 1], xgh[:, kc, :].bitcast(F32),
                                               ALU.mult, ALU.subtract).then_inc(xgl_ready, 1)

                def product(e, u):
                    dve.wait_ge(msil_ready, e * MU + (n0 + u + 1))
                    if u >= 2:
                        dve.wait_ge(mhT_ps, e * MU + (n0 + u - 1))
                    v.tensor_tensor(mh[:, u % 2, :], msil[u % 2], PB[2 + u % 2], ALU.mult).then_inc(mh_ready, 1)

                def turned(e, u):
                    dve.wait_ge(mhh_ready, e * MU + (n0 + u + 1))
                    v.tensor_tensor(mhl[:, u % 2, :, :].rearrange("p a b -> p (a b)"), PB[6],
                                    mhh[:, u % 2, :, :].rearrange("p a b -> p (a b)").bitcast(F32),
                                    ALU.subtract).then_inc(mhl_ready, 1)

                def scattered(q, val):
                    t, n = q // 2, q % 2
                    dve.wait_ge(sc_ps, val)
                    hn = h[:, t, n * BLK:(n + 1) * BLK]
                    v.tensor_tensor(hn, hn, PB[7], ALU.add).then_inc(sc_done, 1)

                def expert(e, final):
                    for c in range(ET):
                        if c + RS - 1 < ET or not final:
                            low(e, c + RS - 1)
                        for u in range(MU):
                            if mgu_at(u) == c + 1:
                                product(e, u)
                            if u and mgu_at(u) - 2 == c + 1:
                                if u <= 4:
                                    if u > 1:
                                        dve.wait_ge(sc_done, e * 4 + (s0 + u - 1))
                                    scattered(u - 1, e * 4 + (s0 + u))
                                turned(e, u - 1)
                        if c + 1 == mgu_at(MU - 1):
                            gathered(e + 1)
                            turned(e, MU - 1)
                    dve.wait_ge(mtile_used, e * ET + (k0 + ET))
                    v.tensor_copy(yb[:, BLK:D], PB[5]).then_inc(yD_ready, 1)
                    hot = PTg[:, e, :] if isinstance(e, int) else PTg[:, bass.ds(e, 1), :].rearrange("p a b -> p (a b)")
                    v.tensor_copy(PTcur, hot).then_inc(yD_ready, 1)

                dve.wait_ge(h1_ready, 8)
                for mt in range(RS - 1):
                    low(0, mt)
                gathered(0)
                dve.wait_ge(PTg_ready, 4 * (ps + 1))
                with dve.Fori(0, NE - 1) as e:
                    expert(e, False)
                expert(NE - 1, True)
                for q in range(4):
                    dve.wait_ge(sc_done, s0 + 4 * NE + q)
                    scattered(q, s0 + 4 * NE + q + 1)
                dve.wait_ge(sc_done, s0 + 4 * (NE + 1))

            dve.wait_ge(flag_ready, 1)
            more = dve.value_load(flag[0:1, 0:1], min_val=0, max_val=1)
            expert_pass(0)
            with dve.If(more > 0):
                expert_pass(1)
            v.memset(rt[:, 0:16], 0.0).then_inc(out_ready, 1)

        @block.tensor
        def _(pe):
            m = nc.tensor.matmul
            tr = nc.tensor.transpose
            pe.wait_ge(cst_in, 16)

            def norm_turn(n):
                for q in range(4):
                    for c in range(2):
                        for t in range(NT):
                            if q == 0 and c == 0:
                                pe.wait_ge(xs_ready, NT * n + t + 1)
                            kc = 2 * q + c
                            last = tr(PB[q][:, 256 * c + 128 * t:256 * c + 128 * t + 128],
                                      xs[:, t, kc * P:(kc + 1) * P], ident)
                    last.then_inc(nT_ps, 1)

            def arrived(k):
                pe.wait_ge(tile_in[k % RA], 16 * (k // RA + 1))

            def block_of(l, b, idx):
                b0 = {4: 4, 0: 0, 1: 2, 2: 4, 3: 0}[b]
                for kh in range(2):
                    k = BASE[l] + 2 * idx + kh
                    arrived(k)
                    w = ringA[k % RA].rearrange("p (c n) -> p c n", c=4)
                    for c in range(4):
                        kc = 4 * kh + c
                        if idx == 0:
                            pe.wait_ge(xnT_ready, KC * 2 * l + kc + 1)
                        a_, z_ = kc == 0, kc == KC - 1
                        for t in range(NT):
                            n = 256 if b == 4 else BLK
                            last = m(PB[b0 + t][:, 0:n], xnT[:, kc, t * P:(t + 1) * P], w[:, c, 0:n],
                                     start=a_, stop=z_)
                        if b == 4:
                            for f in range(2):
                                last = m(PB[6 + f][:, 0:256], w[:, c, 256 + f * P:256 + (f + 1) * P],
                                         xnT[:, kc, :], start=a_, stop=z_)
                    if kh == 0:
                        last.then_inc(tile_used, 1)
                last.then_inc(tile_used, 1)

            for l in range(2):
                PR = 12 * l
                norm_turn(2 * l)
                block_of(l, 4, 0)
                block_of(l, 0, 1)
                block_of(l, 1, 2)
                pe.wait_ge(prep_ready, l + 1)
                pe.wait_ge(u_ready, 2 * (l + 1))
                for q in range(4):
                    if q >= 2:
                        pe.wait_ge(prepT_ev, 4 * l + q - 1)
                    for k in range(4):
                        last = tr(PB[6 + q % 2][:, 128 * k:128 * k + 128],
                                  Wpre[:, 4 * q + k, :, :].rearrange("p a b -> p (a b)"), ident)
                    last.then_inc(prepT_ps, 1)
                for q in range(4):
                    if q < 2:
                        pe.wait_ge(prepT_ev, 4 * l + 3 + q)
                    else:
                        pe.wait_ge(K_raw, 4 * l + q - 1)
                    for k in range(4):
                        gq = 4 * q + k
                        last = m(PB[6 + q % 2][0:GC, 128 * k:128 * k + 128], Bb1[:, gq, :],
                                 V[:, gq, 0:CH, :].rearrange("p a b -> p (a b)"), start=True, stop=True)
                    last.then_inc(prepT_ps, 1)
                pe.wait_ge(u_in, 16 * CH * (l + 1))
                pe.wait_ge(K_raw, 4 * l + 3)
                for gq in range(GROUPS):
                    last = m(PB[6][:, NCH * gq:NCH * (gq + 1)], Wl[:, gq, :], U[:, gq, :],
                             start=True, stop=True)
                last.then_inc(x_ps, 1)
                pe.wait_ge(proj_ready, PR + 2)
                block_of(l, 2, 3)
                pe.wait_ge(x_sb, l + 1)
                pe.wait_ge(K_raw, 4 * l + 4)
                m(PB[7], C("swap"), xsb.rearrange("p a b -> p (a b)"), start=True, stop=True).then_inc(perm_ps, 1)

                def turn_qk(c0, bank):
                    for c in range(2):
                        for t in range(NT):
                            col = c0 + 128 * c
                            last = tr(PB[bank][:, 256 * c + 128 * t:256 * c + 128 * t + 128],
                                      proj[:, t, col:col + 128], ident)
                    last.then_inc(qkT_ps, 1)

                pe.wait_ge(qk_ready, 4 * (l + 1))
                pe.wait_ge(proj_ready, PR + 6)
                turn_qk(QC, 2)
                turn_qk(QC + 256, 3)
                block_of(l, 3, 4)
                pe.wait_ge(scan_ready, l + 1)
                m(PB[6], C("swap"), G.rearrange("p a b -> p (a b)"), start=True, stop=True).then_inc(perm_ps, 1)
                pe.wait_ge(proj_ready, PR + 12)
                pe.wait_ge(qkT_ready, 4 * l + 2)
                for hh in range(HEADS):
                    lo = 64 * (hh % 2)
                    q_, k_ = qkT[lo:lo + 64, hh // 2, :], qkT[lo:lo + 64, 2 + hh // 2, :]
                    m(PB[hh][:, 0:128], q_[:, 0:128], k_[:, 0:128], start=True, stop=True)
                    m(PB[hh][:, 128:384], q_[:, 128:256], k_, start=True, stop=True).then_inc(s_ps, 1)
                pe.wait_ge(qr_ready, 4 * (l + 1))
                turn_qk(QR, 4)
                turn_qk(KR, 5)
                pe.wait_ge(toep_in, 16 * CH * (l + 1))
                pe.wait_ge(hs_ready, l + 1)
                for gq in range(GROUPS):
                    y_ = PB[7][:, NCH * gq:NCH * (gq + 1)]
                    m(y_, Mt[:, gq, :, :].rearrange("p a b -> p (a b)"), U[:, gq, :], start=True, stop=False)
                    last = m(y_, V[:, gq, 1:CH + 1, :].rearrange("p a b -> p (a b)"), Hs[:, gq, 0:NCH],
                             start=False, stop=True)
                last.then_inc(y_ps, 1)
                for hh in range(HEADS):
                    if hh == 0:
                        pe.wait_ge(qkT_ready, 4 * (l + 1))
                    if hh == 2:
                        pe.wait_ge(s_masked, 4 * l + 2)
                    bank = PB[(4, 5, 0, 1)[hh]]
                    lo = 64 * (hh % 2)
                    q_, k_ = qkT[lo:lo + 64, 4 + hh // 2, :], qkT[lo:lo + 64, 6 + hh // 2, :]
                    m(bank[:, 0:256], k_[:, 0:128], q_, start=True, stop=True)
                    m(bank[:, 256:384], k_[:, 128:256], q_[:, 128:256], start=True, stop=True).then_inc(rs_ps, 1)
                pe.wait_ge(p_ready, l + 1)
                for hh in range(HEADS):
                    if hh >= 2:
                        pe.wait_ge(PT_ready, 4 * l + hh - 1)
                    for k in range(3):
                        last = tr(PB[2 + hh % 2][:, 128 * k:128 * k + 128], E[:, hh, 128 * k:128 * k + 128], ident)
                    last.then_inc(pT_ps, 1)
                pe.wait_ge(AT_ready, 4 * (l + 1))
                for t in range(NT):
                    for hh in range(HEADS):
                        o = PB[4 + t][:, 128 * hh:128 * hh + 128]
                        c0 = VR + RV * hh
                        last = m(o, AT[:, hh, 128 * t:128 * t + 128], proj[:, 0, c0:c0 + RV],
                                 start=True, stop=t == 0)
                        if t:
                            last = m(o, AT[:, hh, 256:384], proj[:, 1, c0:c0 + RV], start=False, stop=True)
                    last.then_inc(ry_ps, 1)
                pe.wait_ge(gelu_ready, l + 1)
                pe.wait_ge(PT_ready, 4 * (l + 1))
                for t in range(NT):
                    for hh in range(HEADS):
                        o = PB[7][:, 256 * t + HD * hh:256 * t + HD * (hh + 1)]
                        c0 = VC + HD * hh
                        last = m(o, PT[:, hh, 128 * t:128 * t + 128], proj[:, 0, c0:c0 + HD],
                                 start=True, stop=t == 0)
                        if t:
                            last = m(o, PT[:, hh, 256:384], proj[:, 1, c0:c0 + HD], start=False, stop=True)
                last.then_inc(att_ps, 1)
                pe.wait_ge(z_in, 16 * (l + 1))
                gw = R(l, "gluw", 2, 256)
                for j in range(2):
                    for f in range(2):
                        last = m(PB[6][:, 256 * j:256 * j + 256], gw[:, f, 128 * j:128 * j + 128],
                                 zT[:, f, :, :].rearrange("p a b -> p (a b)"), start=f == 0, stop=f == 1)
                last.then_inc(glu_ps, 1)
                pe.wait_ge(mixed_ready, 4 * (l + 1))
                for q in range(3):
                    for c in range(2):
                        for t in range(NT):
                            cc = 2 * q + c
                            last = tr(PB[q][:, 256 * c + 128 * t:256 * c + 128 * t + 128],
                                      xs[:, t, cc * P:(cc + 1) * P], ident)
                    last.then_inc(mT_ps, 1)
                pe.wait_ge(sgm_ready, 2 * (l + 1))
                for j in range(4):
                    k, kh, n = BASE[l] + 10 + j, j // 2, j % 2
                    arrived(k)
                    w = ringA[k % RA].rearrange("p (c n) -> p c n", c=4)
                    for c in range(4):
                        cc = 4 * kh + c
                        if n == 0:
                            if cc < 6:
                                pe.wait_ge(mixT_ready, 6 * l + cc + 1)
                            else:
                                pe.wait_ge(mixS_ready, 2 * l + cc - 5)
                        for t in range(NT):
                            last = m(PB[4 + 2 * n + t], xnT[:, cc, t * P:(t + 1) * P], w[:, c, :],
                                     start=cc == 0, stop=cc == KC - 1)
                    last.then_inc(tile_used, 1)
                norm_turn(2 * l + 1)
                if l == 0:
                    def turns_in(kk, i):
                        pe.wait_ge(tile_in[kk % RA], (16 * (kk // RA + 1)) if i is None else i * 16 + 16 * (kk // RA + 1))
                        return ringA[kk % RA]

                    def gate_up(kk, i, p, first):
                        for which in range(2):
                            w = turns_in(kk + which, i).rearrange("p (c n) -> p c n", c=KC)
                            for j in range(2):
                                for kc in range(KC):
                                    if first and which == 0 and j == 0:
                                        pe.wait_ge(xnT_ready, KC + max(kc + 1, 2))
                                    last = m(PB[2 * which + p][:, 256 * j:256 * j + 256],
                                             w[:, kc, P * j:P * (j + 1)], xnT[:, kc, :],
                                             start=kc == 0, stop=kc == KC - 1)
                            last.then_inc(tile_used, 1)

                    def down(kk, i, p, first, final):
                        w = turns_in(kk, i).rearrange("p (c n) -> p c n", c=2)
                        for j in range(2):
                            for t in range(NT):
                                for n in range(2):
                                    last = m(PB[4 + 2 * n + t], fhT[p][:, j, t * P:(t + 1) * P],
                                             w[:, j, n * BLK:(n + 1) * BLK], start=first and j == 0,
                                             stop=final and j == 1, skip_group_check=True)
                        last.then_inc(tile_used, 1)

                    gate_up(MIX, None, 0, True)
                    gate_up(MIX + 2, None, 1, False)
                    pe.wait_ge(hT_ready, 1)
                    down(MIX + 4, None, 0, True, False)
                    with pe.Fori(0, PAIRS - 1) as i:
                        for j in range(2):
                            u = j + 2
                            gate_up(MIX + 3 * u - 1, i, u % 2, False)
                            pe.wait_ge(hT_ready, i * 2 + u)
                            down(MIX + 3 * u + 1, i, (u - 1) % 2, False, False)
                    u = FU - 1
                    gate_up(MIX + 3 * u - 1, None, 0, False)
                    pe.wait_ge(hT_ready, u)
                    down(MIX + 3 * u + 1, None, 1, False, False)
                    pe.wait_ge(hT_ready, FU)
                    down(MIX + 3 * u + 2, None, 0, False, True)

            pe.wait_ge(router_in, 16)
            for t in range(NT):
                for kc in range(KC):
                    if t == 0:
                        pe.wait_ge(xnT_ready, 3 * KC + kc + 1)
                    last = m(PB[4][:, 8 * t:8 * t + 8], xnT[:, kc, t * P:(t + 1) * P], router[:, kc, :],
                             start=kc == 0, stop=kc == KC - 1)
            last.then_inc(lg_ps, 1)
            pe.wait_ge(mask_ready, 1)
            chosen = rt[:, 48 + 64:48 + 80].rearrange("p (t e) -> p t e", t=NT)
            m(PB[5][:, 0:8], C("tri"), chosen[:, 0, :], start=True, stop=True)
            m(PB[5][:, 8:16], C("ones"), chosen[:, 0, :], start=True, stop=False)
            m(PB[5][:, 8:16], C("tri"), chosen[:, 1, :], start=False, stop=True)
            m(PB[5][:, 16:24], C("ones"), chosen[:, 0, :], start=True, stop=False)
            m(PB[5][:, 16:24], C("ones"), chosen[:, 1, :], start=False, stop=True).then_inc(pos_ps, 1)

            def expert_pass(ps):
                G0 = (NE + 1) * ps

                def gather(e):
                    for half in range(2):
                        for c in range(4):
                            kc = 4 * half + c
                            for t in range(NT):
                                hot = (PH[:, t, e, :] if isinstance(e, int)
                                       else PH[:, t, bass.ds(e, 1), :].rearrange("p a b -> p (a b)"))
                                last = m(PB[1 + 2 * half][:, 128 * c:128 * c + 128], xs[:, t, kc * P:(kc + 1) * P],
                                         hot, start=t == 0, stop=t == NT - 1)
                        last.then_inc(xg_ps, 1)

                def scatter(q):
                    t, n = q // 2, q % 2
                    m(PB[7], PTcur[:, t * P:(t + 1) * P], yb[:, n * BLK:(n + 1) * BLK],
                      start=True, stop=True).then_inc(sc_ps, 1)

                pe.wait_ge(first_y, 1)
                pe.wait_ge(hot_ready, 32 * ps + 4)
                gather(0)
                pe.wait_ge(hot_ready, 32 * ps + 32)
                for e in range(NE):
                    for t in range(NT):
                        c0 = 256 * (e % 2) + 128 * t
                        last = tr(PB[4 + e // 2][:, c0:c0 + 128], PG[:, t, e, :], ident)
                    if e % 2:
                        last.then_inc(gT_ps, 1)
                pe.wait_ge(PTg_ready, 4 * (ps + 1))
                with pe.Fori(0, NE) as e:
                    n0, s0 = ps * NE * MU, ps * 4 * (NE + 1)

                    def came(mt):
                        pe.wait_ge(wlo_ready, e * ET + (ps * NE * ET + mt + 1))
                        return whi[:, mt % RS, :], wlo[:, mt % RS, :]

                    def three(o, ah, al, bh, bl, start, stop):
                        m(o, ah, bh, start=start, stop=False, skip_group_check=True)
                        m(o, ah, bl, start=False, stop=False, skip_group_check=True)
                        return m(o, al, bh, start=False, stop=stop, skip_group_check=True)

                    def gate_or_up(u, which):
                        mt = (0 if u == 0 else 6 * u - 2) + 2 * which
                        for half in range(2):
                            wh, wl = (w.rearrange("p (c n) -> p c n", c=4) for w in came(mt + half))
                            for c in range(4):
                                kc = 4 * half + c
                                if u == 0 and which == 0:
                                    pe.wait_ge(xgl_ready, e * KC + (KC * G0 + kc + 1))
                                last = three(PB[2 * which + u % 2], xgh[:, kc, :], xgl[:, kc, :],
                                             wh[:, c, :], wl[:, c, :], kc == 0, kc == KC - 1)
                            last.then_inc(mtile_used, 1)

                    def turn(u):
                        pe.wait_ge(mh_ready, e * MU + (n0 + u + 1))
                        for k in range(4):
                            last = tr(PB[6][:, 128 * k:128 * k + 128], mh[:, u % 2, 128 * k:128 * k + 128], ident)
                        last.then_inc(mhT_ps, 1)

                    def down(u):
                        mt = 6 * u + 8 if u < MU - 1 else 6 * u + 4
                        pe.wait_ge(mhl_ready, e * MU + (n0 + u + 1))
                        for half in range(2):
                            wh, wl = (w.rearrange("p (c n) -> p c n", c=2) for w in came(mt + half))
                            for c in range(2):
                                j = 2 * half + c
                                for n in range(2):
                                    cols = slice(n * BLK, (n + 1) * BLK)
                                    last = three(PB[4 + n], mhh[:, u % 2, j, :], mhl[:, u % 2, j, :],
                                                 wh[:, c, cols], wl[:, c, cols],
                                                 u == 0 and j == 0, u == MU - 1 and j == 3)
                            last.then_inc(mtile_used, 1)

                    gate_or_up(0, 0)
                    gate_or_up(0, 1)
                    for u in range(1, MU):
                        if u >= 2:
                            pe.wait_ge(mh_ready, e * MU + (n0 + u - 1))
                        else:
                            pe.wait_ge(xgl_ready, e * KC + (KC * G0 + KC))
                            pe.wait_ge(yA_ready, e + (G0 + 1))
                            pe.wait_ge(yD_ready, e * 2 + (2 * G0 + 2))
                        gate_or_up(u, 0)
                        if u <= 4:
                            if u > 1:
                                pe.wait_ge(sc_done, e * 4 + (s0 + u - 1))
                            scatter(u - 1)
                        turn(u - 1)
                        gate_or_up(u, 1)
                        down(u - 1)
                    pe.wait_ge(sc_done, e * 4 + (s0 + 4))
                    gather(e + 1)
                    turn(MU - 1)
                    down(MU - 1)
                pe.wait_ge(yA_ready, NE + G0 + 1)
                pe.wait_ge(yD_ready, 2 * (NE + G0 + 1))
                for q in range(4):
                    if q:
                        pe.wait_ge(sc_done, 4 * (NE + G0) + q)
                    scatter(q)
                pe.wait_ge(sc_done, 4 * (NE + G0 + 1))
                pe.wait_ge(xgl_ready, KC * (NE + G0 + 1))

            pe.wait_ge(flag_ready, 1)
            more = pe.value_load(flag[0:1, 0:1], min_val=0, max_val=1)
            expert_pass(0)
            with pe.If(more > 0):
                expert_pass(1)


_WEIGHTS = ["x", "w_in", "w_out", "ffn_w_gate", "ffn_w_up", "ffn_w_down", "moe_w_gate", "moe_w_up", "moe_w_down"]


def small_params(i):
    def cols(v):
        return v.reshape(-1, P).T

    def both(a, b):
        return np.concatenate([a, b], 0).reshape(P, -1)

    def rows(v):
        return np.broadcast_to(v.reshape(1, -1), (P, v.size))

    layers = []
    for l in range(2):
        br, bi = (i[n][l].transpose(1, 0, 2).reshape(STATES, -1) for n in ("ssm_b_re", "ssm_b_im"))
        cr, ci = (i[n][l].transpose(2, 0, 1).reshape(STATES, -1) for n in ("ssm_c_re", "ssm_c_im"))
        skip = np.zeros((P, GROUPS, GC), np.float32)
        for c in range(GC):
            skip[c, :, c] = i["ssm_d"][l].reshape(GROUPS, GC)[:, c]
        layers.append(np.concatenate([
            cols(i["norm1_g"][l]), cols(i["norm2_g"][l]), cols(i["ret_gn_g"][l]), cols(i["ssm_glu_b"][l]),
            rows(i["q_norm_g"][l]), rows(i["k_norm_g"][l]),
            both(i["ssm_a_re"][l].T, i["ssm_a_re"][l].T), both(i["ssm_a_im"][l].T, i["ssm_a_im"][l].T),
            rows(i["ssm_log_dt"][l]), both(br, bi), both(bi, br), both(cr, ci), both(ci, cr),
            i["ssm_glu_w"][l].reshape(2, P, 256).transpose(1, 0, 2).reshape(P, -1), skip.reshape(P, -1),
        ], 1))
    return np.ascontiguousarray(np.stack(layers, 1), dtype=np.float32)


def kernel(**inputs):
    import concourse.bacc as _bacc
    from concourse.bass_utils import run_bass_kernel_spmd as _run

    i = {k: np.asarray(v) for k, v in inputs.items()}
    nc = _bacc.Bacc("TRN2", target_bir_lowering=False, num_devices=1)
    arrays = {n: np.ascontiguousarray(i[n]) for n in _WEIGHTS}
    arrays["consts"] = constants()
    arrays["params"] = small_params(i)
    arrays["router"] = np.ascontiguousarray(
        i["moe_router"][0].reshape(KC, P, NE).transpose(1, 0, 2))
    args = {n: nc.dram_tensor(f"in_{n}", v.shape, F32, kind="ExternalInput").ap() for n, v in arrays.items()}
    out = nc.dram_tensor("out_0", (1, SEQ, D), F32, kind="ExternalOutput").ap()
    trunk(nc, args, out)
    r = _run(nc, [{f"in_{n}": v for n, v in arrays.items()}], core_ids=[0])
    return r.results[0]["out_0"]
```

```python
from contextlib import ExitStack

import numpy as np

import concourse.bass as bass
from concourse import mybir

F32 = mybir.dt.float32
F32R = mybir.dt.float32r
I32 = mybir.dt.int32
ALU = mybir.AluOpType
ACT = mybir.ActivationFunctionType
AX_X = mybir.AxisListType.X

P = 128
SEQ, D = 256, 1024
NT = SEQ // P
KC = D // P
HD = 64
HEADS = 4
RV = 128
GROUPS, GC, STATES = 16, 16, 64
CH = 8
NCH = SEQ // CH
EPS = 1e-6
BLK = 512
PROJ = 2304
NE = 8
QC, VC, QR, KR, VR, GR = 0, 512, 768, 1024, 1280, 1792

CO = {}
_at = 0
for _name, _n in (("ident", 128), ("mhalf", 16), ("mone", 16), ("euler", 16), ("sg", 2),
                  ("swap", 128), ("tri", 128), ("ones", 128), ("iota", 128),
                  ("cosA", 16), ("sinA", 16), ("cosR", 64), ("sinR", 64), ("count", 384), ("mask", 384),
                  ("decay", 4 * 384), ("rev", 8)):
    CO[_name] = (_at, _n)
    _at += _n
NCONST = _at
NFIRST = CO["swap"][0]
PO = {}
_at = 0
for _name, _n in (("g1", 8), ("g2", 8), ("gn", 4), ("glub", 2), ("qkg", 128), ("are", 16), ("aim", 16),
                  ("logdt", 16), ("b1", 256), ("b2", 256), ("c1", 256), ("c2", 256), ("gluw", 512),
                  ("dskip", 256)):
    PO[_name] = (_at, _n)
    _at += _n
NPAR = _at
NKEEP = PO["are"][0]


def constants():
    f = np.float32
    c = np.zeros((P, NCONST), f)

    def put(name, a):
        o, n = CO[name]
        c[:, o:o + n] = np.asarray(a, f).reshape(P, n)

    p = np.arange(P)
    put("ident", np.eye(P))
    put("swap", np.eye(P)[(p + 64) % P])
    put("tri", p[:, None] < p[None, :])
    put("ones", np.ones((P, P)))
    put("iota", np.tile(p, (P, 1)))
    pos = np.arange(SEQ, dtype=f)
    for nm, theta, rot in (("A", 500000.0, 16), ("R", 10000.0, 64)):
        half = rot // 2
        inv = np.power(f(theta), -np.arange(half, dtype=f) * f(2.0) / f(rot)).astype(f)
        ang = (pos[:, None] * inv[None, :]).astype(f)
        put("cos" + nm, np.cos(ang).reshape(NT, P, half).transpose(1, 0, 2))
        put("sin" + nm, np.sin(ang).reshape(NT, P, half).transpose(1, 0, 2))
    i, j = np.arange(SEQ)[:, None], np.arange(SEQ)[None, :]
    d = i - j
    cnt = sum(((d >= 0) & (d <= 128 * r) & (d % r == 0)).astype(f) for r in (1, 4, 16))
    msk = np.where(cnt > 0, 0.0, -1e30).astype(f)
    for nm, a in (("count", cnt), ("mask", msk)):
        put(nm, np.concatenate([a[0:P, 0:P], a[P:, :]], 1))
    lg = np.log1p(-np.exp2(-5.0 - np.arange(HEADS)))
    dec = np.where(d >= 0, np.exp(lg[:, None, None] * np.maximum(d, 0)), 0.0) * HD ** -0.5
    dT = dec.transpose(0, 2, 1)
    put("decay", np.stack([np.concatenate([dT[h, 0:P, :], dT[h, P:, P:]], 1) for h in range(HEADS)], 1))
    put("sg", np.stack([np.where(p < 64, -1, 1), np.where(p < 64, 1, -1)], 1))
    put("rev", np.tile(np.arange(NE, 0, -1), (P, 1)))
    put("mhalf", np.full((P, 16), -0.5))
    put("mone", np.full((P, 16), -1.0))
    put("euler", np.full((P, 16), np.e))
    return c


def ring_order():
    def mixer(l):
        return ([("in", l, b, kh) for b in (4, 0, 1, 2, 3) for kh in range(2)]
                + [("out", l, n, kh) for kh in range(2) for n in range(2)])
    return mixer(0), mixer(1)


def trunk(nc, a, out):
    x, w_in, w_out = a["x"], a["w_in"], a["w_out"]
    w_gate, w_up, w_down = a["ffn_w_gate"], a["ffn_w_up"], a["ffn_w_down"]
    m_gate, m_up, m_down = a["moe_w_gate"], a["moe_w_up"], a["moe_w_down"]
    FU = w_gate.shape[2] // 256
    MU = m_gate.shape[3] // BLK
    assert FU % 2 == 1 and MU % 2 == 1 and FU >= 3 and MU >= 5
    PAIRS = (FU - 1) // 2
    ET = 6 * MU
    RA, RM = 2, 7
    RL, RS = 2, 3
    assert 6 % RA == 0 and 6 % RL == 0
    assert ET % RM == 0 and ET % RS == 0
    ER = ET // RM
    MIX = 14
    FFN_TILES = 3 * FU
    BASE = [0, MIX + FFN_TILES]

    gu_at = lambda u: MIX + 2 if u == 0 else MIX + 3 * u + 1
    d_at = lambda u: MIX + 3 * u + (5 if u < FU - 1 else 3)
    mgu_at = lambda u: 4 if u == 0 else 6 * u + 2
    md_at = lambda u: 6 * u + (10 if u < MU - 1 else 6)

    with ExitStack() as ctx:
        def sem(name):
            return ctx.enter_context(nc.semaphore(name))

        psum = ctx.enter_context(nc.psum_tensor("psum", [P, 8, BLK], F32))
        PB = [psum[:, b, :] for b in range(8)]
        top = [0]
        ARENA = 53152
        base = -(-nc.sbuf_base // 64) * 64
        flag = nc.alloc_sbuf_tensor_at("flag", [P, 2], I32, offset=base + 4 * ARENA)
        scr_u = nc.dram_tensor("scratch_u", [256, 256], F32, kind="Internal").ap()
        scr_y = nc.dram_tensor("scratch_y", [256, 256], F32, kind="Internal").ap()

        def take(name, *shape, at=None, dtype=F32):
            n = int(np.prod(shape))
            if at is None:
                at = top[0]
                top[0] += -(-n // 8) * 8
            assert at + n <= ARENA, (name, at + n, ARENA)
            t = nc.alloc_sbuf_tensor_at(name, [P, *shape], dtype, offset=base + 4 * at)
            return t[tuple(slice(None) for _ in range(len(shape) + 1))]

        def take_r(name, *shape):
            return take(name, *shape, dtype=F32R)

        h = take("h", NT, D)
        cst = take("cst", NCONST)
        par = take("par", 2, NKEEP)
        par5 = take("par5", NPAR - NKEEP)
        router = take("router", KC, NE)
        xs = take("xs", NT, D)
        xnh, xnl = take_r("xnh", KC, SEQ), take_r("xnl", KC, SEQ)
        st = take("st", 256)
        ringA_at = top[0]
        ringA = [take(f"ringA{k}", 2048) for k in range(RA)]
        lhi = [take_r(f"lhi{k}", 2048) for k in range(RL)]
        llo = [take_r(f"llo{k}", 2048) for k in range(RL)]
        mix_at = top[0]
        proj = take("proj", NT, PROJ)
        qk_at = top[0]
        qkT = take("qkT", 8, SEQ)
        top[0] += 256
        vt = take("vt", GROUPS, CH + 1, GC, at=qk_at)
        wt = take("wt", GROUPS, CH, GC, at=qk_at)
        E_at = top[0]
        E = take("E", HEADS, 384)
        PT = take("PT", HEADS, 384)
        AT = take("AT", HEADS, 384)
        Wpre = take("Wpre", GROUPS, CH, GC, at=E_at)
        Kall = take("Kall", GROUPS, CH, GC, at=E_at + 2048)
        uTr = take("uTr", 2, CH, NCH)
        U = take("U", GROUPS, NCH)
        xsb = take("xsb", GROUPS, NCH)
        t1 = take("t1", GROUPS, NCH)
        t2 = take("t2", GROUPS, NCH)
        G = take("G", GROUPS, NCH)
        Hs = take("Hs", GROUPS, NCH + 1)
        zT = take("zT", 2, CH, NCH)
        sgm = take("sgm", 2, CH, NCH)
        cosT = take("cosT", GROUPS, NCH)
        sinT = take("sinT", GROUPS, NCH)
        mg = take("mg", GROUPS, NCH)
        Mt = take("Mt", GROUPS, CH, GC)
        Wl = take("Wl", GROUPS, P)
        V = take("V", GROUPS, CH + 1, GC)
        Tre = take("Tre", 32, CH + 1)
        Tim = take("Tim", 32, CH + 1)
        ptmp = take("ptmp", 4, 256)
        pv = take("pv", 24, GROUPS)
        prs = take("prs", GROUPS, CH + 1)
        tims = take("tims", GROUPS, CH)
        Bb1 = take("Bb1", GROUPS, GC)
        Bb2 = take("Bb2", GROUPS, GC)
        rtA = xs[:, 1, 512:1024].rearrange("p (a b) -> p a b", a=4)
        fsil = [take(f"fsil{i}", BLK, at=mix_at + 512 * i) for i in range(2)]
        ff = [take(f"ff{i}", 2, SEQ, at=mix_at + 1024 + 512 * i) for i in range(2)]
        fhh = [take(f"fhh{i}", 2, SEQ, at=mix_at + 2048 + 512 * i, dtype=F32R) for i in range(2)]
        fhl = [take(f"fhl{i}", 2, SEQ, at=mix_at + 3072 + 512 * i, dtype=F32R) for i in range(2)]
        moe_at = ringA_at + RM * 2048
        ringM = ringA + [take(f"ringM{i}", 2048, at=ringA_at + 2048 * i) for i in range(RA, RM)]
        top[0] = -(-moe_at // 16) * 16
        whi, wlo = take_r("whi", RS, 2048), take_r("wlo", RS, 2048)
        xgh, xgl = take_r("xgh", KC, P), take_r("xgl", KC, P)
        mhh, mhl = take_r("mhh", 2, 4, P), take_r("mhl", 2, 4, P)
        PH = take("PH", NT, NE + 1, P)
        PG_at = top[0]
        PG = take("PG", NT, NE, P)
        PTg = take("PTg", NE, SEQ)
        PTcur = take("PTcur", SEQ)
        rth, rtl = (take(n, KC * NE, at=PG_at + KC * NE * i, dtype=F32R) for i, n in enumerate(("rth", "rtl")))
        tri_r, ones_r = (take(n, P, at=PG_at + 2 * KC * NE + P * i, dtype=F32R) for i, n in enumerate(("tri_r", "ones_r")))
        lgT = take("lgT", SEQ, at=PG_at + 2 * KC * NE + 2 * P + 16)
        chosen = take("chosen", 2 * NE, at=PG_at + 2 * KC * NE + 2 * P, dtype=F32R)
        msil = [take(f"msil{i}", BLK, at=PG_at + BLK * i) for i in range(2)]
        mh = take("mh", 2, BLK, at=PG_at + 2 * BLK)
        yb = take("yb", D)
        rt = take("rt", 320)
        assert top[0] <= ARENA, top[0]

        def C(name, *shape):
            o, n = CO[name]
            v = cst[:, o:o + n]
            if len(shape) > 1:
                names = "abcd"[:len(shape)]
                v = v.rearrange(f"p ({' '.join(names)}) -> p {' '.join(names)}",
                                **{k: s for k, s in zip(names, shape)})
            return v

        def R(l, name, *shape):
            o, n = PO[name]
            v = par[:, l, o:o + n] if o < NKEEP else par5[:, o - NKEEP:o - NKEEP + n]
            if len(shape) > 1:
                names = "abcd"[:len(shape)]
                v = v.rearrange(f"p ({' '.join(names)}) -> p {' '.join(names)}",
                                **{k: s for k, s in zip(names, shape)})
            return v

        ident = C("ident")

        x_in = [sem(f"x_in{t}") for t in range(NT)]
        cst_in, par_in, router_in = sem("cst_in"), sem("par_in"), sem("router_in")
        lgT_ps, lgT_ready = sem("lgT_ps"), sem("lgT_ready")
        rows0_ps, rt_parts = sem("rows0_ps"), sem("rt_parts")
        cst2_in, tpow_ready, rot_ready = sem("cst2_in"), sem("tpow_ready"), sem("rot_ready")
        par5_in, lhi_ready, llo_ready, xnl_ready, mixL_ready, fhh_ready, fhl_ready = (
            sem("par5_in"), sem("lhi_ready"), sem("llo_ready"), sem("xnl_ready"), sem("mixL_ready"),
            sem("fhh_ready"), sem("fhl_ready"))
        tile_in = [sem(f"tile_in{s}") for s in range(RA)]
        tile_used = sem("tile_used")
        mtile_in = [sem(f"mtile_in{s}") for s in range(RM)]
        mtile_used = sem("mtile_used")
        ss_ready, rstd_ready, xs_ready = sem("ss_ready"), sem("rstd_ready"), sem("xs_ready")
        nT_ps, xnT_ready = sem("nT_ps"), sem("xnT_ready")
        proj_ready, u_ready = sem("proj_ready"), sem("u_ready")
        u_out, u_in = sem("u_out"), sem("u_in")
        sincos_arg, trig_ready, poles_ready, prep_ready = (
            sem("sincos_arg"), sem("trig_ready"), sem("poles_ready"), sem("prep_ready"))
        prepT_ps, prepT_ev, K_raw, K_ready, toep_in = (
            sem("prepT_ps"), sem("prepT_ev"), sem("K_raw"), sem("K_ready"), sem("toep_in"))
        x_ps, x_sb, scan_ready, hs_ready, y_ps = (
            sem("x_ps"), sem("x_sb"), sem("scan_ready"), sem("hs_ready"), sem("y_ps"))
        perm_ps, gelu_ready, y_out, z_in = sem("perm_ps"), sem("gelu_ready"), sem("y_out"), sem("z_in")
        y_out_sp = sem("y_out_sp")
        glu_ps, sgm_ready, mixS_ready = sem("glu_ps"), sem("sgm_ready"), sem("mixS_ready")
        sq_ready, ssq_ready, rq_ready = sem("sq_ready"), sem("ssq_ready"), sem("rq_ready")
        qk_ready, qr_ready, qkT_ps, qkT_ready = sem("qk_ready"), sem("qr_ready"), sem("qkT_ps"), sem("qkT_ready")
        s_ps, s_masked, negm_ready, exp_ready, p_ready = (
            sem("s_ps"), sem("s_masked"), sem("negm_ready"), sem("exp_ready"), sem("p_ready"))
        pT_ps, PT_ready, att_ps = sem("pT_ps"), sem("PT_ready"), sem("att_ps")
        rs_ps, AT_ready, ry_ps = sem("rs_ps"), sem("AT_ready"), sem("ry_ps")
        var_ready, rvar_ready, mixed_ready = sem("var_ready"), sem("rvar_ready"), sem("mixed_ready")
        mT_ps, mixT_ready, h1_ready = sem("mT_ps"), sem("mixT_ready"), sem("h1_ready")
        sil_ready, hT_ready, h2_ready = sem("sil_ready"), sem("hT_ready"), sem("h2_ready")
        lg_ps, lgm_ready, lge_ready, mask_ready, pos_ps, hot_ready, flag_ready = (
            sem("lg_ps"), sem("lgm_ready"), sem("lge_ready"), sem("mask_ready"), sem("pos_ps"),
            sem("hot_ready"), sem("flag_ready"))
        gT_ps, PTg_ready, first_y = sem("gT_ps"), sem("PTg_ready"), sem("first_y")
        xg_ps, xgh_ready, xgl_ready = sem("xg_ps"), sem("xgh_ready"), sem("xgl_ready")
        whi_ready, wlo_ready = sem("whi_ready"), sem("wlo_ready")
        msil_ready, mh_ready, mhT_ps, mhh_ready, mhl_ready = (
            sem("msil_ready"), sem("mh_ready"), sem("mhT_ps"), sem("mhh_ready"), sem("mhl_ready"))
        yA_ready, yD_ready, sc_ps, sc_done, out_ready, out_done = (
            sem("yA_ready"), sem("yD_ready"), sem("sc_ps"), sem("sc_done"), sem("out_ready"), sem("out_done"))
        dve_step, act_step, pool_step, pool_z = sem("dve_step"), sem("act_step"), sem("pool_step"), sem("pool_z")

        block = ctx.enter_context(nc.Block())

        class Steps:

            def __init__(self, eng, s):
                self.eng, self.s, self.n = eng, s, 0

            def add(self, ins):
                ins.then_inc(self.s, 1)
                self.n += 1

            def wait(self):
                self.eng.wait_ge(self.s, self.n)

            def link(self, ins):
                self.add(ins)
                self.wait()

        @block.sync
        def _(sp):
            for t in range(NT):
                sp.dma_start(h[:, t, :], x[0, t * P:(t + 1) * P, :]).then_inc(x_in[t], 16)
            sp.dma_start(cst[:, 0:NFIRST], a["consts"][:, 0:NFIRST]).then_inc(cst_in, 16)
            sp.dma_start(par[:, :, :], a["params"][:, :, 0:NKEEP]).then_inc(par_in, 16)

            def tile(k, dst_shape, src):
                if k >= RA:
                    sp.wait_ge(llo_ready, 2 * (k - RA + 1))
                v = ringA[k % RA].rearrange("p (c n) -> p c n", c=dst_shape)
                sp.dma_start(v, src).then_inc(tile_in[k % RA], 16)

            def rows(w, r0, nchunk, c0, nc_):
                return w[r0 * P:(r0 + nchunk) * P, c0:c0 + nc_].rearrange("(c p) n -> p c n", p=P)

            def mixer_tiles(l):
                for k, (kind, _, b, kh) in enumerate(ring_order()[l]):
                    if l == 0 and k == RA:
                        sp.dma_start(par5, a["params"][:, 0, NKEEP:NPAR]).then_inc(par5_in, 16)
                        sp.dma_start(cst[:, NFIRST:NCONST], a["consts"][:, NFIRST:NCONST]).then_inc(cst2_in, 16)
                    w = w_in if kind == "in" else w_out
                    tile(BASE[l] + k, 4, rows(w[l], 4 * kh, 4, b * BLK, BLK))

            def s5_rows_out(l):
                sp.wait_ge(gelu_ready, l + 1)
                for t in range(1, CH, 2):
                    dst = scr_y.rearrange("(g c) (s k) -> s c g k", c=GC, k=NCH)[t]
                    sp.dma_start(dst, G[GC * t:GC * (t + 1), :, :]).then_inc(y_out_sp, 16)

            mixer_tiles(0)
            s5_rows_out(0)
            sp.dma_start(router, a["router"]).then_inc(router_in, 16)
            sp.wait_ge(glu_ps, 1)
            sp.dma_start(par5, a["params"][:, 1, NKEEP:NPAR]).then_inc(par5_in, 16)
            k0 = MIX
            tile(k0, KC, rows(w_gate[0], 0, KC, 0, 256))
            tile(k0 + 1, KC, rows(w_up[0], 0, KC, 0, 256))
            with sp.Fori(0, PAIRS) as i:
                for j in range(2):
                    for m, w in ((0, w_gate), (1, w_up), (2, w_down)):
                        kk = k0 + 2 + 3 * j + m
                        sp.wait_ge(llo_ready, i * 12 + 2 * (kk - RA + 1))
                        v = ringA[kk % RA].rearrange("p (c n) -> p c n", c=2 if m == 2 else KC)
                        if m == 2:
                            src = w[0].rearrange("(u c p) n -> u p c n", c=2, p=P)[i * 2 + j]
                        else:
                            src = w[0].rearrange("(c p) (u n) -> u p c n", p=P, n=256)[i * 2 + j + 1]
                        sp.dma_start(v, src).then_inc(tile_in[kk % RA], 16)
            tile(k0 + FFN_TILES - 1, 2, w_down[0].rearrange("(u c p) n -> u p c n", c=2, p=P)[FU - 1])
            mixer_tiles(1)
            s5_rows_out(1)

            def mtile(m, e):
                if m < 4:
                    kind, u, half = "gu"[m // 2], 0, m % 2
                elif m >= ET - 2:
                    kind, u, half = "d", MU - 1, m % 2
                else:
                    r = (m - 4) % 6
                    u = (m - 4) // 6 + 1
                    kind, half = "gud"[r // 2], r % 2
                    if kind == "d":
                        u -= 1
                if kind == "d":
                    r0 = (4 * u + 2 * half) * P
                    return 2, m_down[0].rearrange("e r n -> e r n")[e, r0:r0 + 2 * P, :].rearrange(
                        "(c p) n -> p c n", p=P)
                w = m_gate if kind == "g" else m_up
                return 4, w[0][e, half * 4 * P:(half + 1) * 4 * P, u * BLK:(u + 1) * BLK].rearrange(
                    "(c p) n -> p c n", p=P)

            def mload(m, e):
                c, src = mtile(m, e)
                sp.dma_start(ringM[m % RM].rearrange("p (c n) -> p c n", c=c), src).then_inc(mtile_in[m % RM], 16)

            def expert_pass(ps):
                used0 = ps * NE * ET
                for m in range(RM):
                    if ps == 0 and m < RA:
                        last = max(k for k in range(BASE[1] + MIX) if k % RA == m)
                        sp.wait_ge(llo_ready, 2 * (last + 1))
                    elif ps == 0 and m < RA + 2 * RL:
                        sp.wait_ge(tile_used, BASE[1] + MIX)
                    elif ps == 0:
                        sp.wait_ge(h1_ready, 4 * 2)
                    else:
                        sp.wait_ge(wlo_ready, used0 - RM + m + 1)
                    mload(m, 0)
                with sp.Fori(0, NE - 1) as e:
                    for m in range(ET):
                        n = m + RM
                        if n != 8:
                            sp.wait_ge(wlo_ready, e * ET + (used0 + m + 1 + (n == 7)))
                        mload(n % ET, e + n // ET)
                for m in range(ET - RM):
                    sp.wait_ge(wlo_ready, (NE - 1) * ET + used0 + m + 1)
                    mload(m + RM, NE - 1)

            expert_pass(0)
            sp.wait_ge(flag_ready, 1)
            more = sp.value_load(flag[0:1, 0:1], min_val=0, max_val=1)
            with sp.If(more > 0):
                expert_pass(1)
            sp.wait_ge(out_ready, 1)
            sp.dma_start(out[0].rearrange("(t p) d -> p t d", p=P), h[:, :, :]).then_inc(out_done, 16)
            sp.wait_ge(out_done, 16)

        def s5_setup(l, eng, lk, between=lambda step: None):
            def tt(o, x0, x1, op):
                lk.add(eng.tensor_tensor(o, x0, x1, op))

            def ts(o, x0, s1, s2=None, o0=ALU.mult, o1=None):
                lk.add(eng.tensor_scalar(o, x0, s1, s2, o0, o1) if o1 is not None
                       else eng.tensor_scalar(o, x0, s1, None, o0))

            sg, sg2 = C("sg")[:, 0:1], C("sg")[:, 1:2]
            S = lambda n: pv[:, n, :]
            mag, sn, cs, rden = S(0), S(1), S(2), S(3)
            nr, f1, f2, f3, f4, fre, fim, fs, fns = (S(n) for n in range(9, 18))
            are, aim = R(l, "are"), R(l, "aim")
            b1, b2 = R(l, "b1", GROUPS, GC), R(l, "b2", GROUPS, GC)
            c1, c2 = R(l, "c1", GROUPS, GC), R(l, "c2", GROUPS, GC)

            A = Tre[:, 0:16, 1]
            tt(A, mag, cs, ALU.mult)
            tt(Tim[:, 0:16, 1], mag, sn, ALU.mult)
            lk.add(eng.tensor_copy(Tre[:, 16:32, 1], cs))
            lk.add(eng.tensor_copy(Tim[:, 16:32, 1], sn))
            lk.wait()
            ts(nr, A, -1.0, o0=ALU.add)
            lk.wait()
            tt(f1, nr, are, ALU.mult)
            tt(f2, Tim[:, 0:16, 1], aim, ALU.mult)
            tt(f3, Tim[:, 0:16, 1], are, ALU.mult)
            tt(f4, nr, aim, ALU.mult)
            lk.wait()
            tt(f1, f1, f2, ALU.add)
            tt(f3, f3, f4, ALU.subtract)
            lk.wait()
            tt(fre, f1, rden, ALU.mult)
            tt(fim, f3, rden, ALU.mult)
            lk.wait()
            ts(fs, fim, sg)
            ts(fns, fim, sg2)
            lk.wait()
            between(0)
            wide = lambda v: v.unsqueeze(2).to_broadcast([P, GROUPS, GC])
            q1, q2 = ptmp[:, 0, :], ptmp[:, 1, :]
            q1, q2 = (q.rearrange("p (a b) -> p a b", a=GROUPS) for q in (q1, q2))
            tt(Bb1, wide(fre), b1, ALU.mult)
            tt(q1, wide(fs), b2, ALU.mult)
            tt(Bb2, wide(fre), b2, ALU.mult)
            tt(q2, wide(fns), b1, ALU.mult)
            lk.wait()
            tt(Bb1, Bb1, q1, ALU.add)
            tt(Bb2, Bb2, q2, ALU.add)
            lk.wait()

            for n in (1, 2, 4):
                powers(eng, lk, [ptmp[:, k, :] for k in range(4)], Tre, Tim, 32, n, n)
                if n == 2:
                    between(1)
            eng.tensor_scalar(prs, Tre[:, 0:16, :], sg2, None, ALU.mult).then_inc(tpow_ready, 1)
            ts(tims, Tim[:, 0:16, 0:CH], sg)
            lk.wait()
            eng.wait_ge(tpow_ready, l + 1)
            between(2)
            b4 = lambda v, n: v.unsqueeze(3).to_broadcast([P, GROUPS, n, GC])
            c4 = lambda v, n: v.unsqueeze(2).to_broadcast([P, GROUPS, n, GC])
            tt(V, b4(prs, CH + 1), c4(c1, CH + 1), ALU.mult)
            tt(vt, b4(Tim[:, 0:16, :], CH + 1), c4(c2, CH + 1), ALU.mult)
            lk.wait()
            between(3)
            tt(V, V, vt, ALU.subtract)
            between(4)
            tt(Wpre, b4(Tre[:, 0:16, 0:CH], CH), c4(Bb1, CH), ALU.mult)
            lk.wait()
            tt(wt, b4(tims, CH), c4(Bb2, CH), ALU.mult)
            lk.wait()
            eng.tensor_tensor(Wpre, Wpre, wt, ALU.add).then_inc(prep_ready, 1)
            eng.wait_ge(prep_ready, l + 1)

        def powers(eng, lk, tmp, re, im, rows, n, cnt):
            b = lambda v: v[:, :, n:n + 1].to_broadcast([P, rows, cnt])
            q = [w[:, 0:rows * cnt].rearrange("p (a b) -> p a b", a=rows) for w in tmp]
            r, i = re[:, :, 1:cnt + 1], im[:, :, 1:cnt + 1]
            lk.add(eng.tensor_tensor(q[0], r, b(re), ALU.mult))
            lk.add(eng.tensor_tensor(q[1], i, b(im), ALU.mult))
            lk.add(eng.tensor_tensor(q[2], r, b(im), ALU.mult))
            lk.add(eng.tensor_tensor(q[3], i, b(re), ALU.mult))
            lk.wait()
            lk.add(eng.tensor_tensor(re[:, :, n + 1:n + cnt + 1], q[0], q[1], ALU.subtract))
            lk.add(eng.tensor_tensor(im[:, :, n + 1:n + cnt + 1], q[2], q[3], ALU.add))
            lk.wait()

        @block.gpsimd
        def _(pool):
            lk = Steps(pool, pool_step)
            g = nc.gpsimd
            g.memset(Mt, 0.0).then_inc(pool_z, 1)
            g.memset(Hs[:, :, 0], 0.0).then_inc(pool_z, 1)
            g.memset(mg[:, :, 0], 0.0).then_inc(pool_z, 1)
            g.memset(Tre[:, :, 0], 1.0).then_inc(pool_z, 1)
            g.memset(Tim[:, :, 0], 0.0).then_inc(pool_z, 1)
            g.memset(cosT[:, :, 0], 1.0).then_inc(pool_z, 1)
            g.memset(sinT[:, :, 0], 0.0).then_inc(pool_z, 1)

            def inv_root(dst, src, n, scale, eps, done, done_by=1):
                lk.link(g.tensor_scalar(src, src, scale, eps, ALU.mult, ALU.add))
                g.tensor_tensor(dst, src, C("mhalf")[:, 0:n], ALU.pow).then_inc(done, done_by)

            def norm_root(n):
                pool.wait_ge(ss_ready, NT * (n + 1))
                inv_root(st[:, 2:4], st[:, 0:2], NT, 1.0 / D, EPS, rstd_ready)

            def poles(l):
                S = lambda n: pv[:, n, :]
                mag, rden, dt, la, th, nn, red, den = S(0), S(3), S(4), S(5), S(6), S(7), S(8), S(18)
                q = S(19)
                are, aim = R(l, "are"), R(l, "aim")
                lk.add(g.tensor_tensor(dt, C("euler"), R(l, "logdt"), ALU.pow))
                lk.add(g.tensor_tensor(den, are, are, ALU.mult))
                lk.add(g.tensor_tensor(q, aim, aim, ALU.mult))
                lk.wait()
                lk.add(g.tensor_tensor(la, are, dt, ALU.mult))
                lk.add(g.tensor_tensor(th, aim, dt, ALU.mult))
                lk.add(g.tensor_tensor(den, den, q, ALU.add))
                lk.wait()
                lk.link(g.tensor_scalar(nn, th, float(1 / (2 * np.pi)), 12582912.0, ALU.mult, ALU.add))
                lk.link(g.tensor_scalar(nn, nn, -12582912.0, None, ALU.add))
                rest = 2 * np.pi
                src = th
                for k in range(3):
                    part = float(np.float32(np.round(rest * 2 ** (7 + 10 * k)) / 2 ** (7 + 10 * k))) if k < 2 \
                        else float(np.float32(rest))
                    rest -= part
                    lk.link(g.tensor_scalar(q, nn, -part, None, ALU.mult))
                    lk.link(g.tensor_tensor(red, src, q, ALU.add))
                    src = red
                g.tensor_scalar(red, red, 3.1415925, -3.1415925, ALU.min, ALU.max).then_inc(sincos_arg, 1)
                lk.add(g.tensor_tensor(mag, C("euler"), la, ALU.pow))
                if l:
                    lk.add(g.tensor_tensor(rden, den, C("mone"), ALU.pow))
                lk.wait()
                pool.wait_ge(trig_ready, 2 * (l + 1))
                cs = S(2)
                lk.link(g.tensor_tensor(cs, cs, cs, ALU.mult))
                g.tensor_scalar(cs, cs, -2.0, 1.0, ALU.mult, ALU.add).then_inc(poles_ready, 1)
                pool.wait_ge(poles_ready, l + 1)

            def rotation(l):
                mag, g1, g2, g3 = pv[:, 0, :], pv[:, 20, :], pv[:, 21, :], pv[:, 22, :]
                pool.wait_ge(tpow_ready, l + 1)
                lk.add(g.tensor_copy(cosT[:, :, 1], Tre[:, 16:32, CH]))
                lk.add(g.tensor_copy(sinT[:, :, 1], Tim[:, 16:32, CH]))
                lk.link(g.tensor_tensor(g1, mag, mag, ALU.mult))
                tmp = [w[:, k, :, :].rearrange("p a b -> p (a b)") for w in (zT, sgm) for k in range(2)]
                for n, cnt in ((1, 1), (2, 2), (4, 4), (8, 8), (16, 15)):
                    powers(g, lk, tmp, cosT, sinT, GROUPS, n, cnt)
                lk.add(g.tensor_scalar(sinT, sinT, C("sg")[:, 1:2], None, ALU.mult))
                lk.link(g.tensor_tensor(g2, g1, g1, ALU.mult))
                lk.link(g.tensor_tensor(g3, g2, g2, ALU.mult))
                g.tensor_copy(mg[:, :, 1:NCH], g3.unsqueeze(2).to_broadcast([P, GROUPS, NCH - 1])).then_inc(rot_ready, 1)
                pool.wait_ge(rot_ready, l + 1)

            pool.wait_ge(cst_in, 16)
            norm_root(0)
            pool.wait_ge(par5_in, 16)
            pool.wait_ge(pool_z, 7)
            poles(0)
            for l in range(2):
                pool.wait_ge(u_ready, 2 * (l + 1))
                pool.dma_start(scr_u.rearrange("(f p) n -> p f n", p=P),
                               uTr.rearrange("p f s k -> p f (s k)")).then_inc(u_out, 16)
                pool.wait_ge(u_out, 16 * (l + 1))
                for s in range(CH):
                    src = scr_u.rearrange("(g c) (s k) -> s c g k", c=GC, k=NCH)[CH - 1 - s]
                    pool.dma_start(U[GC * s:GC * (s + 1), :, :], src).then_inc(u_in, 16)
                if l == 0:
                    rotation(0)
                pool.wait_ge(ssq_ready, l + 1)
                inv_root(st[:, 32:48], st[:, 16:32], 16, 1.0 / HD, EPS, rq_ready)
                pool.wait_ge(K_raw, 4 * (l + 1))
                g.tensor_tensor(Kall[0:GC, :, 0, :], Kall[0:GC, :, 0, :], R(l, "dskip", GROUPS, GC)[0:GC],
                                ALU.add).then_inc(K_ready, 1)
                pool.wait_ge(K_ready, l + 1)
                for s in range(CH):
                    pool.dma_start(Mt[GC * s:GC * (s + 1), :, CH - 1 - s:CH, :],
                                   Kall[0:GC, :, 0:s + 1, :]).then_inc(toep_in, 16)
                pool.wait_ge(gelu_ready, l + 1)
                ysb = G
                for t in range(0, CH, 2):
                    dst = scr_y.rearrange("(g c) (s k) -> s c g k", c=GC, k=NCH)[t]
                    pool.dma_start(dst, ysb[GC * t:GC * (t + 1), :, :]).then_inc(y_out, 16)
                pool.wait_ge(y_out, 8 * CH * (l + 1))
                pool.wait_ge(y_out_sp, 8 * CH * (l + 1))
                pool.dma_start(zT.rearrange("p f s k -> p f (s k)"),
                               scr_y.rearrange("(f p) n -> p f n", p=P)).then_inc(z_in, 16)
                pool.wait_ge(var_ready, l + 1)
                inv_root(st[:, 72:80], st[:, 64:72], 8, 1.0, 1e-5, rvar_ready)
                norm_root(2 * l + 1)
                if l == 0:
                    pool.wait_ge(par5_in, 32)
                    poles(1)
                    s5_setup(1, g, lk)
                    rotation(1)
                    norm_root(2)

        @block.scalar
        def _(act):
            lk = Steps(act, act_step)
            s = nc.scalar

            def norm(n):
                l = n // 2
                for t in range(NT):
                    if n == 0:
                        act.wait_ge(x_in[t], 16)
                    elif n % 2:
                        act.wait_ge(h1_ready, 4 * l + 3 + t)
                    else:
                        act.wait_ge(h2_ready, 2 + 2 * t)
                    s.activation(xs[:, t, :], h[:, t, :], ACT.Square, accum_out=st[:, t:t + 1]).then_inc(ss_ready, 1)
                act.wait_ge(rstd_ready, n + 1)
                act.wait_ge(par_in, 16)
                for t in range(NT):
                    s.activation(xs[:, t, :], h[:, t, :], ACT.Copy, scale=st[:, 2 + t:3 + t]).then_inc(xs_ready, 1)
                if n == 0:
                    high_l(0)
                for kc in range(KC):
                    if kc % 2 == 0:
                        act.wait_ge(nT_ps, 4 * n + kc // 2 + 1)
                    gain = R(l, "g1" if n % 2 == 0 else "g2")[:, kc:kc + 1]
                    s.activation(xnh[:, kc, :],
                                 PB[kc // 2][:, 256 * (kc % 2):256 * (kc % 2) + 256],
                                 ACT.Copy, scale=gain).then_inc(xnT_ready, 1)


            def high_l(k, i=None):
                kk = k if i is None else i * 6 + k
                act.wait_ge(tile_in[k % RA], 16 * (k // RA + 1) if i is None
                            else i * (16 * 6 // RA) + 16 * (k // RA + 1))
                if k >= RL:
                    act.wait_ge(tile_used, kk - (RL - 1))
                for half in range(2):
                    part = slice(1024 * half, 1024 * half + 1024)
                    s.activation(lhi[k % RL][:, part], ringA[k % RA][:, part], ACT.Copy).then_inc(lhi_ready, 1)

            def trig(l):
                act.wait_ge(sincos_arg, l + 1)
                s.activation(pv[:, 1, :], pv[:, 8, :], ACT.Sin).then_inc(trig_ready, 1)
                s.activation(pv[:, 2, :], pv[:, 8, :], ACT.Sin, scale=0.5).then_inc(trig_ready, 1)

            def blk(l, b):
                idx = {4: 0, 0: 1, 1: 2, 2: 3, 3: 4}[b]
                high_l(BASE[l] + 2 * idx + 2)
                act.wait_ge(tile_used, BASE[l] + 2 * (idx + 1))
                for t in range(NT):
                    bank = {4: 4, 0: 0, 1: 2, 2: 4, 3: 0}[b] + t
                    if b == 4:
                        s.activation(proj[:, t, 2048:2304], PB[bank][:, 0:256], ACT.Silu).then_inc(proj_ready, 1)
                    elif b == 3:
                        s.activation(proj[:, t, 1536:1792], PB[bank][:, 0:256], ACT.Copy).then_inc(proj_ready, 1)
                        s.activation(proj[:, t, 1792:2048], PB[bank][:, 256:512], ACT.Silu).then_inc(proj_ready, 1)
                    else:
                        s.activation(proj[:, t, b * BLK:(b + 1) * BLK], PB[bank], ACT.Copy).then_inc(proj_ready, 1)
                if (b != 1 or l == 0) and (b != 2 or l):
                    high_l(BASE[l] + 2 * idx + 3)

            norm(0)
            high_l(1)
            trig(0)
            for l in range(2):
                PR = 12 * l
                if l == 1:
                    norm(2)
                    high_l(BASE[1] + 1)
                blk(l, 4)
                blk(l, 0)
                act.wait_ge(proj_ready, PR + 4)
                s.activation(xs[:, :, 0:512], proj[:, :, 0:512], ACT.Square).then_inc(sq_ready, 1)
                blk(l, 1)
                if l == 0:
                    blk(l, 2)
                for q in range(4):
                    act.wait_ge(prepT_ps, 8 * l + q + 1)
                    s.activation(Wl[:, 4 * q:4 * q + 4, :].rearrange("p a b -> p (a b)"), PB[6 + q % 2],
                                 ACT.Copy).then_inc(prepT_ev, 1)
                high_l(BASE[l] + (7 if l else 9))
                for q in range(4):
                    act.wait_ge(prepT_ps, 8 * l + 4 + q + 1)
                    s.activation(Kall[0:GC, 4 * q:4 * q + 4, :, :].rearrange("p g a b -> p (g a b)"),
                                 PB[6 + q % 2][0:GC, :], ACT.Copy).then_inc(K_raw, 1)
                if l:
                    blk(l, 2)
                for q in range(2):
                    act.wait_ge(qkT_ps, 4 * l + q + 1)
                    s.activation(qkT[:, 2 * q:2 * q + 2, :].rearrange("p a b -> p (a b)"), PB[2 + q],
                                 ACT.Copy).then_inc(qkT_ready, 1)
                blk(l, 3)
                for t in range(NT):
                    for hh in range(HEADS):
                        if t == 0 and hh == 0:
                            act.wait_ge(negm_ready, l + 1)
                        c0, c1 = (0, 128) if t == 0 else (128, 384)
                        s.activation(E[:, hh, c0:c1], E[:, hh, c0:c1], ACT.Exp,
                                     bias=st[:, 88 + 4 * t + hh:89 + 4 * t + hh]).then_inc(exp_ready, 1)
                for q in range(2):
                    act.wait_ge(qkT_ps, 4 * l + 2 + q + 1)
                    s.activation(qkT[:, 4 + 2 * q:6 + 2 * q, :].rearrange("p a b -> p (a b)"), PB[4 + q],
                                 ACT.Copy).then_inc(qkT_ready, 1)
                act.wait_ge(y_ps, l + 1)
                s.activation(G.rearrange("p a b -> p (a b)"), PB[7], ACT.Gelu_apprx_tanh).then_inc(gelu_ready, 1)
                for hh in range(HEADS):
                    act.wait_ge(pT_ps, 4 * l + hh + 1)
                    s.activation(PT[:, hh, :], PB[2 + hh % 2][:, 0:384], ACT.Copy).then_inc(PT_ready, 1)
                for j in range(2):
                    act.wait_ge(glu_ps, l + 1)
                    s.activation(sgm[:, j, :, :].rearrange("p a b -> p (a b)"), PB[6][:, 256 * j:256 * j + 256],
                                 ACT.Sigmoid, bias=R(l, "glub")[:, j:j + 1]).then_inc(sgm_ready, 1)
                for c in range(6):
                    act.wait_ge(mT_ps, 3 * l + c // 2 + 1)
                    src = PB[c // 2][:, 256 * (c % 2):256 * (c % 2) + 256]
                    if c < 2:
                        s.activation(xnh[:, c, :], src, ACT.Copy).then_inc(mixT_ready, 1)
                    else:
                        s.activation(xnh[:, c, :], src, ACT.Copy,
                                     scale=R(l, "gn")[:, c - 2:c - 1]).then_inc(mixT_ready, 1)
                for k in range(12, 15 if l == 0 else MIX):
                    high_l(BASE[l] + k)
                norm(2 * l + 1)
                if l == 0:
                    high_l(MIX + 1)
                    trig(1)

                    def silu(used, p):
                        act.wait_ge(tile_used, used)
                        s.activation(fsil[p], PB[p], ACT.Silu).then_inc(sil_ready, 1)

                    def hidden_high(val, p):
                        act.wait_ge(hT_ready, val)
                        s.activation(fhh[p].rearrange("p a b -> p (a b)"), ff[p].rearrange("p a b -> p (a b)"),
                                     ACT.Copy).then_inc(fhh_ready, 1)

                    def unit(u, i=None):
                        add = (lambda n, v: v) if i is None else (lambda n, v: i * n + v)
                        c = 3 * u + MIX - 1
                        high_l(c + 1, i)
                        hidden_high(add(2, u), (u - 1) % 2)
                        high_l(c + 2, i)
                        if u == FU - 1:
                            silu(gu_at(u), 0)
                            hidden_high(FU, 0)
                            high_l(c + 3)
                            return
                        high_l(c + 3, i)
                        silu(add(6, gu_at(u)), u % 2)

                    high_l(MIX + 2)
                    silu(gu_at(0), 0)
                    high_l(MIX + 3)
                    hidden_high(1, 0)
                    high_l(MIX + 4)
                    high_l(MIX + 5)
                    silu(gu_at(1), 1)
                    with act.Fori(0, PAIRS - 1) as i:
                        for j in range(2):
                            unit(j + 2, i)
                    unit(FU - 1)
                    high_l(BASE[1])

            def high(e, mt, ps):
                k0 = ps * NE * ET
                if isinstance(e, int) and k0 + e * ET + mt < RS:
                    pass
                else:
                    act.wait_ge(mtile_used, e * ET + (k0 + mt - RS + 1))
                act.wait_ge(mtile_in[mt % RM], e * (16 * ER) + 16 * (ps * NE * ER + mt // RM + 1))
                s.activation(whi[:, mt % RS, :], ringM[mt % RM], ACT.Copy).then_inc(whi_ready, 1)

            high(0, 0, 0)
            act.wait_ge(lgm_ready, 1)
            s.activation(rt[:, 0:16], rt[:, 0:16], ACT.Exp).then_inc(lge_ready, 1)

            def expert_pass(ps):
                n0, k0, G0 = ps * NE * MU, ps * NE * ET, ps * (NE + 1)

                def gathered(e):
                    for kc in range(KC):
                        if kc % 4 == 0:
                            act.wait_ge(xg_ps, e * 2 + (2 * G0 + kc // 4 + 1))
                        s.activation(xgh[:, kc, :], PB[1 + 2 * (kc // 4)][:, 128 * (kc % 4):128 * (kc % 4) + 128],
                                     ACT.Copy, scale=R(1, "g2")[:, kc:kc + 1]).then_inc(xgh_ready, 1)

                def silu(e, u):
                    act.wait_ge(mtile_used, e * ET + (k0 + mgu_at(u)))
                    if u >= 2:
                        act.wait_ge(mh_ready, e * MU + (n0 + u - 1))
                    s.activation(msil[u % 2], PB[u % 2], ACT.Silu).then_inc(msil_ready, 1)

                def turned(e, u):
                    act.wait_ge(mhT_ps, e * MU + (n0 + u + 1))
                    s.activation(mhh[:, u % 2, :, :].rearrange("p a b -> p (a b)"), PB[6],
                                 ACT.Copy).then_inc(mhh_ready, 1)

                def expert(e, final):
                    for c in range(ET):
                        if c + RS - 1 < ET or not final:
                            high(e, c + RS - 1, ps)
                        for u in range(MU):
                            if mgu_at(u) == c + 1:
                                silu(e, u)
                            if u and mgu_at(u) - 2 == c + 1:
                                turned(e, u - 1)
                        if c + 1 == ET - 2:
                            turned(e, MU - 1)
                            gathered(e + 1)
                    act.wait_ge(mh_ready, e * MU + (n0 + MU))
                    act.wait_ge(mtile_used, e * ET + (k0 + ET))
                    s.activation(yb[:, 0:BLK], PB[4], ACT.Copy).then_inc(yA_ready, 1)

                for mt in range(RS - 1):
                    if ps or mt:
                        high(0, mt, ps)
                gathered(0)
                for q in range(4):
                    act.wait_ge(gT_ps, 4 * ps + q + 1)
                    s.activation(PTg[:, 2 * q:2 * q + 2, :].rearrange("p a b -> p (a b)"), PB[4 + q],
                                 ACT.Copy).then_inc(PTg_ready, 1)
                with act.Fori(0, NE - 1) as e:
                    expert(e, False)
                expert(NE - 1, True)

            expert_pass(0)
            act.wait_ge(flag_ready, 1)
            more = act.value_load(flag[0:1, 0:1], min_val=0, max_val=1)
            with act.If(more > 0):
                expert_pass(1)

        @block.vector
        def _(dve):
            lk = Steps(dve, dve_step)
            v = nc.vector
            def low_l(k, i=None):
                for half in range(2):
                    part = slice(1024 * half, 1024 * half + 1024)
                    dve.wait_ge(lhi_ready, 2 * k + half + 1 if i is None else i * 12 + (2 * k + half + 1))
                    v.tensor_tensor(llo[k % RL][:, part], ringA[k % RA][:, part], lhi[k % RL][:, part].bitcast(F32),
                                    ALU.subtract).then_inc(llo_ready, 1)

            def norm_low(n):
                for kc in range(KC):
                    if kc % 2 == 0:
                        dve.wait_ge(xnT_ready, KC * n + kc + 2)
                    v.scalar_tensor_tensor(xnl[:, kc, :], PB[kc // 2][:, 256 * (kc % 2):256 * (kc % 2) + 256],
                                           R(n // 2, "g1" if n % 2 == 0 else "g2")[:, kc:kc + 1],
                                           xnh[:, kc, :].bitcast(F32), ALU.mult, ALU.subtract).then_inc(xnl_ready, 1)

            dve.wait_ge(par_in, 16)
            low_l(0)
            norm_low(0)
            low_l(1)
            dve.wait_ge(par5_in, 16)
            dve.wait_ge(cst_in, 16)
            dve.wait_ge(pool_z, 7)
            low_l(2)
            dve.wait_ge(poles_ready, 1)
            lk.link(v.reciprocal(pv[:, 3, :], pv[:, 18, :]))

            def between(step):
                low_l(3 + step)
                if step == 0:
                    u_out_of_psum(0)

            def u_out_of_psum(l):
                for f in range(2):
                    dve.wait_ge(tile_used, BASE[l] + 2)
                    if l:
                        dve.wait_ge(u_out, 16 * l)
                    v.tensor_copy(uTr[:, f, :, :].rearrange("p s k -> p k s"),
                                  PB[6 + f][:, 0:256].rearrange("p (k s) -> p k s", s=CH)).then_inc(u_ready, 1)

            s5_setup(0, v, lk, between)
            dve.wait_ge(cst2_in, 16)
            for l in range(2):
                PR = 12 * l
                if l:
                    low_l(BASE[l] + 2)
                    low_l(BASE[l] + 3)
                    u_out_of_psum(l)
                    low_l(BASE[l] + 4)
                    low_l(BASE[l] + 5)
                dve.wait_ge(sq_ready, l + 1)
                v.tensor_reduce(st[:, 16:32].rearrange("p (t h) -> p t h", t=NT), xs[:, :, 0:512].rearrange("p t (h d) -> p t h d", d=HD),
                                AX_X, ALU.add).then_inc(ssq_ready, 1)
                dve.wait_ge(rq_ready, l + 1)
                rs = st[:, 32:48].rearrange("p (t h) -> p t h", t=NT)
                for t in range(NT):
                    qk = proj[:, t, 0:512].rearrange("p (h d) -> p h d", d=HD)
                    lk.add(v.tensor_tensor(qk, qk, rs[:, t, :].unsqueeze(2).to_broadcast([P, 8, HD]), ALU.mult))
                lk.wait()
                for t in range(NT):
                    qk = proj[:, t, 0:512].rearrange("p (w h d) -> p w h d", w=2, d=HD)
                    gain = R(l, "qkg", 2, HD).unsqueeze(2).to_broadcast([P, 2, HEADS, HD])
                    lk.add(v.tensor_tensor(qk, qk, gain, ALU.mult))
                lk.wait()

                def rope(col, half, cos, sin, tmp, done, val):
                    n = 8 * half
                    for t in range(NT):
                        xx = proj[:, t, col:col + 512].rearrange("p (h d) -> p h d", d=HD)
                        x1, x2 = xx[:, :, 0:half], xx[:, :, half:2 * half]
                        co = cos[:, t, :].unsqueeze(1).to_broadcast([P, 8, half])
                        si = sin[:, t, :].unsqueeze(1).to_broadcast([P, 8, half])
                        q = [tmp[k].rearrange("p (h d) -> p h d", d=half) for k in range(4)]
                        if t:
                            lk.wait()
                        lk.add(v.tensor_tensor(q[0], x1, co, ALU.mult))
                        lk.add(v.tensor_tensor(q[1], x2, si, ALU.mult))
                        lk.add(v.tensor_tensor(q[2], x2, co, ALU.mult))
                        lk.add(v.tensor_tensor(q[3], x1, si, ALU.mult))
                        lk.wait()
                        v.tensor_tensor(x1, q[0], q[1], ALU.subtract).then_inc(done, 1)
                        v.tensor_tensor(x2, q[2], q[3], ALU.add).then_inc(done, 1)
                        dve.wait_ge(done, val + 2 * t + 2)

                rope(QC, 8, C("cosA", NT, 8), C("sinA", NT, 8),
                     [rtA[:, k, 0:64] for k in range(4)], qk_ready, 4 * l)

                if l:
                    low_l(BASE[l] + 6)
                    low_l(BASE[l] + 7)
                flat = lambda w: w.rearrange("p a b -> p (a b)")
                dve.wait_ge(x_ps, l + 1)
                v.tensor_copy(flat(xsb), PB[6]).then_inc(x_sb, 1)
                dve.wait_ge(x_sb, l + 1)
                dve.wait_ge(rot_ready, l + 1)
                lk.add(v.tensor_tensor(flat(t1), flat(xsb), flat(cosT), ALU.mult))
                low_l(BASE[l] + 8)
                dve.wait_ge(perm_ps, 2 * l + 1)
                lk.add(v.tensor_tensor(flat(t2), PB[7], flat(sinT), ALU.mult))
                lk.wait()
                lk.link(v.tensor_tensor(flat(t1), flat(t1), flat(t2), ALU.add))
                if l:
                    dve.wait_ge(y_out, 8 * CH * l)
                    dve.wait_ge(y_out_sp, 8 * CH * l)
                v.tensor_tensor_scan(flat(G), flat(mg), flat(t1), 0.0, ALU.mult, ALU.add).then_inc(scan_ready, 1)
                dve.wait_ge(scan_ready, l + 1)
                low_l(BASE[l] + 9)
                dve.wait_ge(proj_ready, PR + 8)
                rope(QR, 32, C("cosR", NT, 32), C("sinR", NT, 32),
                     [xs[:, 0, 256 * k:256 * k + 256] for k in range(4)], qr_ready, 4 * l)
                lk.add(v.tensor_tensor(flat(t1), flat(G), flat(cosT), ALU.mult))
                low_l(BASE[l] + 10)
                dve.wait_ge(perm_ps, 2 * l + 2)
                lk.add(v.tensor_tensor(flat(t2), PB[6], flat(sinT), ALU.mult))
                lk.wait()
                v.tensor_tensor(Hs[:, :, 1:NCH + 1], t1, t2, ALU.subtract).then_inc(hs_ready, 1)
                for hh in range(HEADS):
                    dve.wait_ge(s_ps, 4 * l + hh + 1)
                    if hh == 0:
                        dve.wait_ge(toep_in, 16 * CH * (l + 1))
                    v.scalar_tensor_tensor(E[:, hh, :], PB[hh][:, 0:384], HD ** -0.5, C("mask"),
                                           ALU.mult, ALU.add).then_inc(s_masked, 1)
                dve.wait_ge(s_masked, 4 * (l + 1))
                lk.add(v.tensor_reduce(st[:, 80:84], E[:, :, 0:128], AX_X, ALU.max))
                lk.add(v.tensor_reduce(st[:, 84:88], E[:, :, 128:384], AX_X, ALU.max))
                lk.wait()
                v.tensor_scalar(st[:, 88:96], st[:, 80:88], -1.0, None, ALU.mult).then_inc(negm_ready, 1)
                low_l(BASE[l] + 11)
                dve.wait_ge(exp_ready, 8 * (l + 1))
                v.tensor_tensor(E, E, C("count").unsqueeze(1).to_broadcast([P, HEADS, 384]),
                                ALU.mult).then_inc(p_ready, 1)
                dve.wait_ge(p_ready, l + 1)
                lk.add(v.tensor_reduce(st[:, 96:100], E[:, :, 0:128], AX_X, ALU.add))
                lk.add(v.tensor_reduce(st[:, 100:104], E[:, :, 128:384], AX_X, ALU.add))
                lk.wait()
                lk.link(v.reciprocal(st[:, 104:112], st[:, 96:104]))
                for hh in range(HEADS):
                    dve.wait_ge(rs_ps, 4 * l + hh + 1)
                    v.tensor_tensor(AT[:, hh, :], PB[(4, 5, 0, 1)[hh]][:, 0:384], C("decay", 4, 384)[:, hh, :],
                                    ALU.mult).then_inc(AT_ready, 1)
                mv = st[:, 48:64].rearrange("p (n c) -> p n c", c=2)
                for t in range(NT):
                    dve.wait_ge(ry_ps, 2 * l + t + 1)
                    for hh in range(HEADS):
                        lk.add(v.bn_stats(st[:, 112 + 6 * (4 * t + hh):118 + 6 * (4 * t + hh)],
                                          PB[4 + t][:, 128 * hh:128 * hh + 128]))
                lk.wait()
                for n in range(8):
                    lk.add(v.bn_aggr(mv[:, n, :], st[:, 112 + 6 * n:118 + 6 * n]))
                lk.wait()
                v.tensor_copy(st[:, 64:72], mv[:, :, 1]).then_inc(var_ready, 1)
                dve.wait_ge(proj_ready, PR + 12)
                for t in range(NT):
                    for hh in range(HEADS):
                        gcol = GR + 128 * hh
                        lk.add(v.scalar_tensor_tensor(xs[:, t, 256 + 128 * hh:384 + 128 * hh],
                                                      PB[4 + t][:, 128 * hh:128 * hh + 128],
                                                      mv[:, 4 * t + hh, 0:1], proj[:, t, gcol:gcol + 128],
                                                      ALU.subtract, ALU.mult))
                dve.wait_ge(att_ps, l + 1)
                rl = st[:, 104:112].rearrange("p (t h) -> p t h", t=NT)
                for t in range(NT):
                    v.tensor_tensor(xs[:, t, 0:256].rearrange("p (h d) -> p h d", d=HD),
                                    PB[7][:, 256 * t:256 * t + 256].rearrange("p (h d) -> p h d", d=HD),
                                    rl[:, t, :].unsqueeze(2).to_broadcast([P, HEADS, HD]),
                                    ALU.mult).then_inc(mixed_ready, 1)
                lk.wait()
                dve.wait_ge(rvar_ready, l + 1)
                rv = st[:, 72:80].rearrange("p (t h) -> p t h", t=NT)
                for t in range(NT):
                    z = xs[:, t, 256:768].rearrange("p (h d) -> p h d", d=RV)
                    v.tensor_tensor(z, z, rv[:, t, :].unsqueeze(2).to_broadcast([P, HEADS, RV]),
                                    ALU.mult).then_inc(mixed_ready, 1)
                dve.wait_ge(sgm_ready, 2 * (l + 1))
                dve.wait_ge(z_in, 16 * (l + 1))
                steps = lambda w, j: w[:, 6 + j, :].rearrange("p (k s) -> p s k", s=CH)
                for j in range(2):
                    lk.add(v.tensor_tensor(zT[:, j, :, :], zT[:, j, :, :], sgm[:, j, :, :], ALU.mult))
                lk.wait()
                for j in range(2):
                    lk.add(v.tensor_copy(steps(xnh, j), zT[:, j, :, :]))
                lk.wait()
                for j in range(2):
                    v.tensor_tensor(steps(xnl, j), zT[:, j, :, :], steps(xnh, j).bitcast(F32),
                                    ALU.subtract).then_inc(mixS_ready, 1)
                for c in range(6):
                    if c % 2 == 0:
                        dve.wait_ge(mixT_ready, 6 * l + c + 2)
                    src = PB[c // 2][:, 256 * (c % 2):256 * (c % 2) + 256]
                    hi = xnh[:, c, :].bitcast(F32)
                    if c < 2:
                        v.tensor_tensor(xnl[:, c, :], src, hi, ALU.subtract).then_inc(mixL_ready, 1)
                    else:
                        v.scalar_tensor_tensor(xnl[:, c, :], src, R(l, "gn")[:, c - 2:c - 1], hi,
                                               ALU.mult, ALU.subtract).then_inc(mixL_ready, 1)
                low_l(BASE[l] + 12)
                low_l(BASE[l] + 13)
                for n in range(2):
                    for t in range(NT):
                        if n and t == 0:
                            dve.wait_ge(rows0_ps, 2 * l + 1)
                        else:
                            dve.wait_ge(tile_used, BASE[l] + MIX - 1 + n)
                        hn = h[:, t, n * BLK:(n + 1) * BLK]
                        v.tensor_tensor(hn, hn, PB[4 + 2 * n + t], ALU.add).then_inc(h1_ready, 1)
                if l == 0:
                    low_l(MIX)
                    norm_low(1)
                    low_l(MIX + 1)

                    def product(val, p):
                        dve.wait_ge(sil_ready, val)
                        v.tensor_tensor(ff[p].rearrange("p a b -> p (a b)"), fsil[p], PB[2 + p],
                                        ALU.mult).then_inc(hT_ready, 1)

                    def hidden_low(val, p):
                        dve.wait_ge(fhh_ready, val)
                        v.tensor_tensor(fhl[p], ff[p], fhh[p].bitcast(F32), ALU.subtract).then_inc(fhl_ready, 1)

                    def unit(u, i=None):
                        add = (lambda n, w: w) if i is None else (lambda n, w: i * n + w)
                        c = 3 * u + MIX - 1
                        low_l(c + 1, i)
                        hidden_low(add(2, u), (u - 1) % 2)
                        low_l(c + 2, i)
                        if u == FU - 1:
                            product(FU, 0)
                            hidden_low(FU, 0)
                            low_l(c + 3)
                            return
                        low_l(c + 3, i)
                        product(add(2, u + 1), u % 2)

                    low_l(MIX + 2)
                    product(1, 0)
                    low_l(MIX + 3)
                    hidden_low(1, 0)
                    low_l(MIX + 4)
                    low_l(MIX + 5)
                    product(2, 1)
                    with dve.Fori(0, PAIRS - 1) as i:
                        for j in range(2):
                            unit(j + 2, i)
                    unit(FU - 1)
                    low_l(BASE[1])
                    dve.wait_ge(h1_ready, 4)
                    for t in range(NT):
                        if t == 0:
                            dve.wait_ge(rows0_ps, 2)
                        else:
                            dve.wait_ge(tile_used, d_at(FU - 1))
                        for n in range(2):
                            hn = h[:, t, n * BLK:(n + 1) * BLK]
                            v.tensor_tensor(hn, hn, PB[4 + 2 * n + t], ALU.add).then_inc(h2_ready, 1)
                    norm_low(2)
                    low_l(BASE[1] + 1)

            lg = rt[:, 0:16].rearrange("p (t e) -> p t e", t=NT)
            pr = lg
            S2 = lambda k: rt[:, 16 + 2 * k:18 + 2 * k]
            S16 = lambda k: rt[:, 48 + 16 * k:64 + 16 * k].rearrange("p (t e) -> p t e", t=NT)
            e8 = lambda w: w.unsqueeze(2).to_broadcast([P, NT, NE])
            rev = C("rev").unsqueeze(1).to_broadcast([P, NT, NE])
            def low(e, mt, ps):
                dve.wait_ge(whi_ready, e * ET + (ps * NE * ET + mt + 1))
                v.tensor_tensor(wlo[:, mt % RS, :], ringM[mt % RM], whi[:, mt % RS, :].bitcast(F32),
                                ALU.subtract).then_inc(wlo_ready, 1)

            def no_result_yet():
                v.memset(yb[:, 0:BLK], 0.0).then_inc(yA_ready, 1)
                v.memset(yb[:, BLK:D], 0.0).then_inc(yD_ready, 1)
                v.memset(PTcur, 0.0).then_inc(yD_ready, 1)

            dve.wait_ge(router_in, 16)
            wr = router.rearrange("p a b -> p (a b)")
            lk.link(v.tensor_copy(rth, wr))
            v.tensor_tensor(rtl, wr, rth.bitcast(F32), ALU.subtract).then_inc(rt_parts, 1)
            v.tensor_copy(tri_r, C("tri")).then_inc(rt_parts, 1)
            v.tensor_copy(ones_r, C("ones")).then_inc(rt_parts, 1)
            norm_low(3)
            v.memset(PH[:, :, NE, :], 0.0).then_inc(first_y, 1)
            no_result_yet()
            dve.wait_ge(lgT_ps, 1)
            v.tensor_copy(lgT[0:NE, :], PB[4][0:NE, 0:SEQ]).then_inc(lgT_ready, 1)
            dve.wait_ge(lg_ps, 1)
            logits = PB[5][:, 0:2 * NE].rearrange("p (t e) -> p t e", t=NT)
            lk.link(v.tensor_reduce(S2(0), logits, AX_X, ALU.max))
            v.tensor_tensor(lg, logits, e8(S2(0)), ALU.subtract).then_inc(lgm_ready, 1)
            dve.wait_ge(lge_ready, 1)
            lk.link(v.tensor_reduce(S2(1), lg, AX_X, ALU.add))
            lk.link(v.reciprocal(S2(2), S2(1)))
            lk.link(v.tensor_tensor(pr, lg, e8(S2(2)), ALU.mult))

            def best(src, top_, one, tmp, k):
                lk.link(v.tensor_reduce(top_, src, AX_X, ALU.max))
                lk.link(v.tensor_tensor(tmp, src, e8(top_), ALU.is_ge))
                lk.link(v.tensor_tensor(tmp, tmp, rev, ALU.mult))
                lk.link(v.tensor_reduce(S2(k), tmp, AX_X, ALU.max))
                lk.link(v.tensor_tensor(one, tmp, e8(S2(k)), ALU.is_ge))

            best(pr, S2(3), S16(0), S16(1), 4)
            lk.link(v.scalar_tensor_tensor(S16(2), S16(0), -2.0, pr, ALU.mult, ALU.add))
            best(S16(2), S2(5), S16(3), S16(1), 6)
            mask = chosen.bitcast(F32).rearrange("p (t e) -> p t e", t=NT)
            v.tensor_tensor(chosen.rearrange("p (t e) -> p t e", t=NT), S16(0), S16(3), ALU.add).then_inc(mask_ready, 1)
            lk.link(v.tensor_tensor(S2(7), S2(3), S2(5), ALU.add))
            lk.link(v.reciprocal(S2(8), S2(7)))
            lk.add(v.tensor_tensor(S2(9), S2(3), S2(8), ALU.mult))
            lk.add(v.tensor_tensor(S2(10), S2(5), S2(8), ALU.mult))
            lk.wait()
            gate = S16(5)
            lk.add(v.tensor_tensor(gate, S16(0), e8(S2(9)), ALU.mult))
            lk.add(v.tensor_tensor(S16(6), S16(3), e8(S2(10)), ALU.mult))
            lk.wait()
            lk.link(v.tensor_tensor(gate, gate, S16(6), ALU.add))
            slot = S16(7)
            dve.wait_ge(mask_ready, 1)
            low(0, 0, 0)
            dve.wait_ge(pos_ps, 1)
            lk.link(v.scalar_tensor_tensor(slot, PB[6][:, 0:16].rearrange("p (t e) -> p t e", t=NT), 1.0, mask,
                                           ALU.add, ALU.mult))
            lk.link(v.tensor_scalar(slot, slot, -1.0, None, ALU.add))
            lk.link(v.tensor_reduce(S2(11)[:, 0:1], PB[6][:, 16:24], AX_X, ALU.max))
            v.tensor_scalar(flag[:, 0:1], S2(11)[:, 0:1], float(P), None, ALU.is_gt).then_inc(flag_ready, 1)

            def expert_pass(ps):
                if ps:
                    lk.link(v.tensor_scalar(slot, slot, -float(P), None, ALU.add))
                for e in range(NE):
                    for t in range(NT):
                        v.tensor_scalar(PH[:, t, e, :], C("iota"), slot[:, t, e:e + 1], None,
                                        ALU.is_equal).then_inc(hot_ready, 1)
                        v.tensor_scalar(PG[:, t, e, :], C("iota"), slot[:, t, e:e + 1], gate[:, t, e:e + 1],
                                        ALU.is_equal, ALU.mult).then_inc(hot_ready, 1)
                if ps:
                    no_result_yet()
                n0, k0, G0 = ps * NE * MU, ps * NE * ET, ps * (NE + 1)
                s0 = 4 * G0

                def gathered(e):
                    for kc in range(KC):
                        if kc % 4 == 0:
                            dve.wait_ge(xgh_ready, e * KC + (KC * G0 + kc + 4))
                        v.scalar_tensor_tensor(xgl[:, kc, :], PB[1 + 2 * (kc // 4)][:, 128 * (kc % 4):128 * (kc % 4) + 128],
                                               R(1, "g2")[:, kc:kc + 1], xgh[:, kc, :].bitcast(F32),
                                               ALU.mult, ALU.subtract).then_inc(xgl_ready, 1)

                def product(e, u):
                    dve.wait_ge(msil_ready, e * MU + (n0 + u + 1))
                    if u >= 2:
                        dve.wait_ge(mhT_ps, e * MU + (n0 + u - 1))
                    v.tensor_tensor(mh[:, u % 2, :], msil[u % 2], PB[2 + u % 2], ALU.mult).then_inc(mh_ready, 1)

                def turned(e, u):
                    dve.wait_ge(mhh_ready, e * MU + (n0 + u + 1))
                    v.tensor_tensor(mhl[:, u % 2, :, :].rearrange("p a b -> p (a b)"), PB[6],
                                    mhh[:, u % 2, :, :].rearrange("p a b -> p (a b)").bitcast(F32),
                                    ALU.subtract).then_inc(mhl_ready, 1)

                def scattered(q, val, bank=7):
                    t, n = q // 2, q % 2
                    dve.wait_ge(sc_ps, val)
                    hn = h[:, t, n * BLK:(n + 1) * BLK]
                    v.tensor_tensor(hn, hn, PB[bank], ALU.add).then_inc(sc_done, 1)

                def expert(e, final):
                    for c in range(ET):
                        if c + RS - 1 < ET or not final:
                            low(e, c + RS - 1, ps)
                        for u in range(MU):
                            if mgu_at(u) == c + 1:
                                product(e, u)
                            if u and mgu_at(u) - 2 == c + 1:
                                if u <= 4:
                                    if u > 1:
                                        dve.wait_ge(sc_done, e * 4 + (s0 + u - 1))
                                    scattered(u - 1, e * 4 + (s0 + u))
                                turned(e, u - 1)
                        if c + 1 == ET - 2:
                            turned(e, MU - 1)
                            gathered(e + 1)
                    dve.wait_ge(mtile_used, e * ET + (k0 + ET))
                    v.tensor_copy(yb[:, BLK:D], PB[5]).then_inc(yD_ready, 1)
                    hot = PTg[:, e, :] if isinstance(e, int) else PTg[:, bass.ds(e, 1), :].rearrange("p a b -> p (a b)")
                    v.tensor_copy(PTcur, hot).then_inc(yD_ready, 1)

                dve.wait_ge(h1_ready, 8)
                for mt in range(RS - 1):
                    if ps or mt:
                        low(0, mt, ps)
                gathered(0)
                dve.wait_ge(PTg_ready, 4 * (ps + 1))
                with dve.Fori(0, NE - 1) as e:
                    expert(e, False)
                expert(NE - 1, True)
                dve.wait_ge(sc_done, s0 + 4 * NE)
                for q in range(4):
                    scattered(q, s0 + 4 * NE + q + 1, (7, 6, 0, 1)[q])
                dve.wait_ge(sc_done, s0 + 4 * (NE + 1))

            expert_pass(0)
            dve.wait_ge(flag_ready, 1)
            more = dve.value_load(flag[0:1, 0:1], min_val=0, max_val=1)
            with dve.If(more > 0):
                expert_pass(1)
            v.memset(rt[:, 0:16], 0.0).then_inc(out_ready, 1)

        @block.tensor
        def _(pe):
            m = nc.tensor.matmul
            tr = nc.tensor.transpose
            pe.wait_ge(cst_in, 16)

            def norm_turn(n):
                for q in range(4):
                    for c in range(2):
                        for t in range(NT):
                            if q == 0 and c == 0:
                                pe.wait_ge(xs_ready, NT * n + t + 1)
                            kc = 2 * q + c
                            last = tr(PB[q][:, 256 * c + 128 * t:256 * c + 128 * t + 128],
                                      xs[:, t, kc * P:(kc + 1) * P], ident)
                    last.then_inc(nT_ps, 1)

            def came(k, i=None):
                pe.wait_ge(llo_ready, 2 * (k + 1) if i is None else i * 12 + 2 * (k + 1))
                return lhi[k % RL], llo[k % RL]

            def three(o, ah, al, bh, bl, start, stop):
                m(o, ah, bh, start=start, stop=False, skip_group_check=True)
                m(o, ah, bl, start=False, stop=False, skip_group_check=True)
                return m(o, al, bh, start=False, stop=stop, skip_group_check=True)

            def block_of(l, b, idx):
                b0 = {4: 4, 0: 0, 1: 2, 2: 4, 3: 0}[b]
                for kh in range(2):
                    k = BASE[l] + 2 * idx + kh
                    wh, wl = (w.rearrange("p (c n) -> p c n", c=4) for w in came(k))
                    for c in range(4):
                        kc = 4 * kh + c
                        if idx == 0:
                            pe.wait_ge(xnl_ready, KC * 2 * l + kc + 1)
                        a_, z_ = kc == 0, kc == KC - 1
                        for t in range(NT):
                            n = 256 if b == 4 else BLK
                            tok = slice(t * P, (t + 1) * P)
                            last = three(PB[b0 + t][:, 0:n], xnh[:, kc, tok], xnl[:, kc, tok],
                                         wh[:, c, 0:n], wl[:, c, 0:n], a_, z_)
                        if b == 4:
                            for f in range(2):
                                col = slice(256 + f * P, 256 + (f + 1) * P)
                                last = three(PB[6 + f][:, 0:256], wh[:, c, col], wl[:, c, col],
                                             xnh[:, kc, :], xnl[:, kc, :], a_, z_)
                    if kh == 0:
                        last.then_inc(tile_used, 1)
                last.then_inc(tile_used, 1)

            for l in range(2):
                PR = 12 * l
                norm_turn(2 * l)
                block_of(l, 4, 0)
                block_of(l, 0, 1)
                block_of(l, 1, 2)
                if l == 0:
                    pe.wait_ge(proj_ready, PR + 2)
                    block_of(l, 2, 3)
                pe.wait_ge(cst2_in, 16)
                pe.wait_ge(prep_ready, l + 1)
                pe.wait_ge(u_ready, 2 * (l + 1))
                for q in range(4):
                    if q >= 2:
                        pe.wait_ge(prepT_ev, 4 * l + q - 1)
                    for k in range(4):
                        last = tr(PB[6 + q % 2][:, 128 * k:128 * k + 128],
                                  Wpre[:, 4 * q + k, :, :].rearrange("p a b -> p (a b)"), ident)
                    last.then_inc(prepT_ps, 1)
                for q in range(4):
                    if q < 2:
                        pe.wait_ge(prepT_ev, 4 * l + 3 + q)
                    else:
                        pe.wait_ge(K_raw, 4 * l + q - 1)
                    for k in range(4):
                        gq = 4 * q + k
                        last = m(PB[6 + q % 2][0:GC, 128 * k:128 * k + 128], Bb1[:, gq, :],
                                 V[:, gq, 0:CH, :].rearrange("p a b -> p (a b)"), start=True, stop=True)
                    last.then_inc(prepT_ps, 1)
                pe.wait_ge(u_in, 16 * CH * (l + 1))
                pe.wait_ge(K_raw, 4 * l + 3)
                for gq in range(GROUPS):
                    last = m(PB[6][:, NCH * gq:NCH * (gq + 1)], Wl[:, gq, :], U[:, gq, :],
                             start=True, stop=True)
                last.then_inc(x_ps, 1)
                if l:
                    pe.wait_ge(proj_ready, PR + 2)
                    block_of(l, 2, 3)
                pe.wait_ge(x_sb, l + 1)
                pe.wait_ge(K_raw, 4 * l + 4)
                m(PB[7], C("swap"), xsb.rearrange("p a b -> p (a b)"), start=True, stop=True).then_inc(perm_ps, 1)

                def turn_qk(c0, bank):
                    for c in range(2):
                        for t in range(NT):
                            col = c0 + 128 * c
                            last = tr(PB[bank][:, 256 * c + 128 * t:256 * c + 128 * t + 128],
                                      proj[:, t, col:col + 128], ident)
                    last.then_inc(qkT_ps, 1)

                pe.wait_ge(qk_ready, 4 * (l + 1))
                pe.wait_ge(proj_ready, PR + 6)
                turn_qk(QC, 2)
                turn_qk(QC + 256, 3)
                block_of(l, 3, 4)
                pe.wait_ge(scan_ready, l + 1)
                m(PB[6], C("swap"), G.rearrange("p a b -> p (a b)"), start=True, stop=True).then_inc(perm_ps, 1)
                pe.wait_ge(proj_ready, PR + 12)
                pe.wait_ge(qkT_ready, 4 * l + 2)
                for hh in range(HEADS):
                    lo = 64 * (hh % 2)
                    q_, k_ = qkT[lo:lo + 64, hh // 2, :], qkT[lo:lo + 64, 2 + hh // 2, :]
                    m(PB[hh][:, 0:128], q_[:, 0:128], k_[:, 0:128], start=True, stop=True)
                    m(PB[hh][:, 128:384], q_[:, 128:256], k_, start=True, stop=True).then_inc(s_ps, 1)
                pe.wait_ge(qr_ready, 4 * (l + 1))
                turn_qk(QR, 4)
                turn_qk(KR, 5)
                pe.wait_ge(toep_in, 16 * CH * (l + 1))
                pe.wait_ge(hs_ready, l + 1)
                for gq in range(GROUPS):
                    y_ = PB[7][:, NCH * gq:NCH * (gq + 1)]
                    m(y_, Mt[:, gq, :, :].rearrange("p a b -> p (a b)"), U[:, gq, :], start=True, stop=False)
                    last = m(y_, V[:, gq, 1:CH + 1, :].rearrange("p a b -> p (a b)"), Hs[:, gq, 0:NCH],
                             start=False, stop=True)
                last.then_inc(y_ps, 1)
                for hh in range(HEADS):
                    if hh == 0:
                        pe.wait_ge(qkT_ready, 4 * (l + 1))
                    if hh == 2:
                        pe.wait_ge(s_masked, 4 * l + 2)
                    bank = PB[(4, 5, 0, 1)[hh]]
                    lo = 64 * (hh % 2)
                    q_, k_ = qkT[lo:lo + 64, 4 + hh // 2, :], qkT[lo:lo + 64, 6 + hh // 2, :]
                    m(bank[:, 0:256], k_[:, 0:128], q_, start=True, stop=True)
                    m(bank[:, 256:384], k_[:, 128:256], q_[:, 128:256], start=True, stop=True).then_inc(rs_ps, 1)
                pe.wait_ge(p_ready, l + 1)
                for hh in range(HEADS):
                    if hh >= 2:
                        pe.wait_ge(PT_ready, 4 * l + hh - 1)
                    for k in range(3):
                        last = tr(PB[2 + hh % 2][:, 128 * k:128 * k + 128], E[:, hh, 128 * k:128 * k + 128], ident)
                    last.then_inc(pT_ps, 1)
                pe.wait_ge(AT_ready, 4 * (l + 1))
                for t in range(NT):
                    for hh in range(HEADS):
                        o = PB[4 + t][:, 128 * hh:128 * hh + 128]
                        c0 = VR + RV * hh
                        last = m(o, AT[:, hh, 128 * t:128 * t + 128], proj[:, 0, c0:c0 + RV],
                                 start=True, stop=t == 0)
                        if t:
                            last = m(o, AT[:, hh, 256:384], proj[:, 1, c0:c0 + RV], start=False, stop=True)
                    last.then_inc(ry_ps, 1)
                pe.wait_ge(gelu_ready, l + 1)
                pe.wait_ge(PT_ready, 4 * (l + 1))
                for t in range(NT):
                    for hh in range(HEADS):
                        o = PB[7][:, 256 * t + HD * hh:256 * t + HD * (hh + 1)]
                        c0 = VC + HD * hh
                        last = m(o, PT[:, hh, 128 * t:128 * t + 128], proj[:, 0, c0:c0 + HD],
                                 start=True, stop=t == 0)
                        if t:
                            last = m(o, PT[:, hh, 256:384], proj[:, 1, c0:c0 + HD], start=False, stop=True)
                last.then_inc(att_ps, 1)
                pe.wait_ge(z_in, 16 * (l + 1))
                gw = R(l, "gluw", 2, 256)
                for j in range(2):
                    for f in range(2):
                        last = m(PB[6][:, 256 * j:256 * j + 256], gw[:, f, 128 * j:128 * j + 128],
                                 zT[:, f, :, :].rearrange("p a b -> p (a b)"), start=f == 0, stop=f == 1)
                last.then_inc(glu_ps, 1)
                pe.wait_ge(mixed_ready, 4 * (l + 1))
                for q in range(3):
                    for c in range(2):
                        for t in range(NT):
                            cc = 2 * q + c
                            last = tr(PB[q][:, 256 * c + 128 * t:256 * c + 128 * t + 128],
                                      xs[:, t, cc * P:(cc + 1) * P], ident)
                    last.then_inc(mT_ps, 1)
                pe.wait_ge(sgm_ready, 2 * (l + 1))
                for j in range(4):
                    k, kh, n = BASE[l] + 10 + j, j // 2, j % 2
                    wh, wl = (w.rearrange("p (c n) -> p c n", c=4) for w in came(k))
                    order = [(c, t) for c in range(4) for t in range(NT)]
                    if j == 3:
                        order.sort(key=lambda ct: ct[1])
                    for c, t in order:
                        cc = 4 * kh + c
                        if n == 0 and t == 0:
                            if cc < 6:
                                pe.wait_ge(mixL_ready, 6 * l + cc + 1)
                            else:
                                pe.wait_ge(mixS_ready, 2 * l + cc - 5)
                        tok = slice(t * P, (t + 1) * P)
                        last = three(PB[4 + 2 * n + t], xnh[:, cc, tok], xnl[:, cc, tok],
                                     wh[:, c, :], wl[:, c, :], cc == 0, cc == KC - 1)
                        if j == 3 and (c, t) == (3, 0):
                            last.then_inc(rows0_ps, 1)
                    last.then_inc(tile_used, 1)
                norm_turn(2 * l + 1)
                if l == 0:
                    def gate_up(kk, i, p, first):
                        for which in range(2):
                            wh, wl = (w.rearrange("p (c n) -> p c n", c=KC) for w in came(kk + which, i))
                            for j in range(2):
                                for kc in range(KC):
                                    if first and which == 0 and j == 0:
                                        pe.wait_ge(xnl_ready, KC + max(kc + 1, 2))
                                    col = slice(P * j, P * (j + 1))
                                    last = three(PB[2 * which + p][:, 256 * j:256 * j + 256],
                                                 wh[:, kc, col], wl[:, kc, col], xnh[:, kc, :], xnl[:, kc, :],
                                                 kc == 0, kc == KC - 1)
                            last.then_inc(tile_used, 1)

                    def down(kk, i, p, first, final):
                        wh, wl = (w.rearrange("p (c n) -> p c n", c=2) for w in came(kk, i))
                        order = [(j, t) for j in range(2) for t in range(NT)]
                        if final:
                            order.sort(key=lambda jt: jt[1])
                        for j, t in order:
                            for n in range(2):
                                tok, col = slice(t * P, (t + 1) * P), slice(n * BLK, (n + 1) * BLK)
                                last = three(PB[4 + 2 * n + t], fhh[p][:, j, tok], fhl[p][:, j, tok],
                                             wh[:, j, col], wl[:, j, col], first and j == 0,
                                             final and j == 1)
                            if final and (j, t) == (1, 0):
                                last.then_inc(rows0_ps, 1)
                        last.then_inc(tile_used, 1)

                    gate_up(MIX, None, 0, True)
                    gate_up(MIX + 2, None, 1, False)
                    pe.wait_ge(fhl_ready, 1)
                    down(MIX + 4, None, 0, True, False)
                    with pe.Fori(0, PAIRS - 1) as i:
                        for j in range(2):
                            u = j + 2
                            gate_up(MIX + 3 * u - 1, i, u % 2, False)
                            pe.wait_ge(fhl_ready, i * 2 + u)
                            down(MIX + 3 * u + 1, i, (u - 1) % 2, False, False)
                    u = FU - 1
                    gate_up(MIX + 3 * u - 1, None, 0, False)
                    pe.wait_ge(fhl_ready, u)
                    down(MIX + 3 * u + 1, None, 1, False, False)
                    pe.wait_ge(fhl_ready, FU)
                    down(MIX + 3 * u + 2, None, 0, False, True)

            pe.wait_ge(rt_parts, 3)
            for kc in range(KC):
                pe.wait_ge(xnl_ready, 3 * KC + kc + 1)
                w = slice(NE * kc, NE * (kc + 1))
                last = three(PB[4][0:NE, 0:SEQ], rth[:, w], rtl[:, w], xnh[:, kc, :], xnl[:, kc, :],
                             kc == 0, kc == KC - 1)
            last.then_inc(lgT_ps, 1)
            pe.wait_ge(lgT_ready, 1)
            for t in range(NT):
                last = tr(PB[5][:, NE * t:NE * (t + 1)], lgT[0:NE, t * P:(t + 1) * P], ident[0:NE, 0:NE])
            last.then_inc(lg_ps, 1)
            pe.wait_ge(mask_ready, 1)
            m(PB[6][:, 0:8], tri_r, chosen[:, 0:NE], start=True, stop=True)
            m(PB[6][:, 8:16], ones_r, chosen[:, 0:NE], start=True, stop=False)
            m(PB[6][:, 8:16], tri_r, chosen[:, NE:2 * NE], start=False, stop=True)
            m(PB[6][:, 16:24], ones_r, chosen[:, 0:NE], start=True, stop=False)
            m(PB[6][:, 16:24], ones_r, chosen[:, NE:2 * NE], start=False, stop=True).then_inc(pos_ps, 1)

            def expert_pass(ps):
                G0 = (NE + 1) * ps

                def gather(e):
                    for half in range(2):
                        for c in range(4):
                            kc = 4 * half + c
                            for t in range(NT):
                                hot = (PH[:, t, e, :] if isinstance(e, int)
                                       else PH[:, t, bass.ds(e, 1), :].rearrange("p a b -> p (a b)"))
                                last = m(PB[1 + 2 * half][:, 128 * c:128 * c + 128], xs[:, t, kc * P:(kc + 1) * P],
                                         hot, start=t == 0, stop=t == NT - 1)
                        last.then_inc(xg_ps, 1)

                def scatter(q, bank=7):
                    t, n = q // 2, q % 2
                    m(PB[bank], PTcur[:, t * P:(t + 1) * P], yb[:, n * BLK:(n + 1) * BLK],
                      start=True, stop=True).then_inc(sc_ps, 1)

                pe.wait_ge(first_y, 1)
                pe.wait_ge(hot_ready, 32 * ps + 4)
                gather(0)
                pe.wait_ge(hot_ready, 32 * ps + 32)
                for e in range(NE):
                    for t in range(NT):
                        c0 = 256 * (e % 2) + 128 * t
                        last = tr(PB[4 + e // 2][:, c0:c0 + 128], PG[:, t, e, :], ident)
                    if e % 2:
                        last.then_inc(gT_ps, 1)
                with pe.Fori(0, NE) as e:
                    n0, s0 = ps * NE * MU, ps * 4 * (NE + 1)

                    def came(mt):
                        pe.wait_ge(wlo_ready, e * ET + (ps * NE * ET + mt + 1))
                        return whi[:, mt % RS, :], wlo[:, mt % RS, :]

                    def gate_or_up(u, which):
                        mt = (0 if u == 0 else 6 * u - 2) + 2 * which
                        for half in range(2):
                            wh, wl = (w.rearrange("p (c n) -> p c n", c=4) for w in came(mt + half))
                            for c in range(4):
                                kc = 4 * half + c
                                if u == 0 and which == 0:
                                    pe.wait_ge(xgl_ready, e * KC + (KC * G0 + kc + 1))
                                last = three(PB[2 * which + u % 2], xgh[:, kc, :], xgl[:, kc, :],
                                             wh[:, c, :], wl[:, c, :], kc == 0, kc == KC - 1)
                            last.then_inc(mtile_used, 1)

                    def turn(u):
                        pe.wait_ge(mh_ready, e * MU + (n0 + u + 1))
                        for k in range(4):
                            last = tr(PB[6][:, 128 * k:128 * k + 128], mh[:, u % 2, 128 * k:128 * k + 128], ident)
                        last.then_inc(mhT_ps, 1)

                    def down(u):
                        mt = 6 * u + 8 if u < MU - 1 else 6 * u + 4
                        pe.wait_ge(mhl_ready, e * MU + (n0 + u + 1))
                        for half in range(2):
                            wh, wl = (w.rearrange("p (c n) -> p c n", c=2) for w in came(mt + half))
                            for c in range(2):
                                j = 2 * half + c
                                for n in range(2):
                                    cols = slice(n * BLK, (n + 1) * BLK)
                                    last = three(PB[4 + n], mhh[:, u % 2, j, :], mhl[:, u % 2, j, :],
                                                 wh[:, c, cols], wl[:, c, cols],
                                                 u == 0 and j == 0, u == MU - 1 and j == 3)
                            last.then_inc(mtile_used, 1)

                    gate_or_up(0, 0)
                    gate_or_up(0, 1)
                    for u in range(1, MU):
                        if u >= 2:
                            pe.wait_ge(mh_ready, e * MU + (n0 + u - 1))
                        else:
                            pe.wait_ge(PTg_ready, 4 * (ps + 1))
                            pe.wait_ge(xgl_ready, e * KC + (KC * G0 + KC))
                            pe.wait_ge(yA_ready, e + (G0 + 1))
                            pe.wait_ge(yD_ready, e * 2 + (2 * G0 + 2))
                        gate_or_up(u, 0)
                        if u <= 4:
                            if u > 1:
                                pe.wait_ge(sc_done, e * 4 + (s0 + u - 1))
                            scatter(u - 1)
                        turn(u - 1)
                        gate_or_up(u, 1)
                        down(u - 1)
                    pe.wait_ge(sc_done, e * 4 + (s0 + 4))
                    gather(e + 1)
                    turn(MU - 1)
                    down(MU - 1)
                pe.wait_ge(yA_ready, NE + G0 + 1)
                pe.wait_ge(yD_ready, 2 * (NE + G0 + 1))
                pe.wait_ge(xgl_ready, KC * (NE + G0 + 1))
                for q in range(4):
                    scatter(q, (7, 6, 0, 1)[q])
                pe.wait_ge(sc_done, 4 * (NE + G0 + 1))

            expert_pass(0)
            pe.wait_ge(flag_ready, 1)
            more = pe.value_load(flag[0:1, 0:1], min_val=0, max_val=1)
            with pe.If(more > 0):
                expert_pass(1)


_WEIGHTS = ["x", "w_in", "w_out", "ffn_w_gate", "ffn_w_up", "ffn_w_down", "moe_w_gate", "moe_w_up", "moe_w_down"]


def small_params(i):
    def cols(v):
        return v.reshape(-1, P).T

    def both(a, b):
        return np.concatenate([a, b], 0).reshape(P, -1)

    def rows(v):
        return np.broadcast_to(v.reshape(1, -1), (P, v.size))

    layers = []
    for l in range(2):
        br, bi = (i[n][l].transpose(1, 0, 2).reshape(STATES, -1) for n in ("ssm_b_re", "ssm_b_im"))
        cr, ci = (i[n][l].transpose(2, 0, 1).reshape(STATES, -1) for n in ("ssm_c_re", "ssm_c_im"))
        skip = np.zeros((P, GROUPS, GC), np.float32)
        for c in range(GC):
            skip[c, :, c] = i["ssm_d"][l].reshape(GROUPS, GC)[:, c]
        layers.append(np.concatenate([
            cols(i["norm1_g"][l]), cols(i["norm2_g"][l]), cols(i["ret_gn_g"][l]), cols(i["ssm_glu_b"][l]),
            rows(i["q_norm_g"][l]), rows(i["k_norm_g"][l]),
            both(i["ssm_a_re"][l].T, i["ssm_a_re"][l].T), both(i["ssm_a_im"][l].T, i["ssm_a_im"][l].T),
            rows(i["ssm_log_dt"][l]), both(br, bi), both(bi, br), both(cr, ci), both(ci, cr),
            i["ssm_glu_w"][l].reshape(2, P, 256).transpose(1, 0, 2).reshape(P, -1), skip.reshape(P, -1),
        ], 1))
    return np.ascontiguousarray(np.stack(layers, 1), dtype=np.float32)


def kernel(**inputs):
    import concourse.bacc as _bacc
    from concourse.bass_utils import run_bass_kernel_spmd as _run

    i = {k: np.asarray(v) for k, v in inputs.items()}
    nc = _bacc.Bacc("TRN2", target_bir_lowering=False, num_devices=1)
    arrays = {n: np.ascontiguousarray(i[n]) for n in _WEIGHTS}
    arrays["consts"] = constants()
    arrays["params"] = small_params(i)
    arrays["router"] = np.ascontiguousarray(
        i["moe_router"][0].reshape(KC, P, NE).transpose(1, 0, 2))
    args = {n: nc.dram_tensor(f"in_{n}", v.shape, F32, kind="ExternalInput").ap() for n, v in arrays.items()}
    out = nc.dram_tensor("out_0", (1, SEQ, D), F32, kind="ExternalOutput").ap()
    trunk(nc, args, out)
    r = _run(nc, [{f"in_{n}": v for n, v in arrays.items()}], core_ids=[0])
    return r.results[0]["out_0"]
```
